# Optimizing a Trainium2 kernel written in Bass

```python
import jax, jax.numpy as jnp
from jax import lax
import numpy as np

D_MODEL = 1024
BATCH = 1
SEQ = 256
DEPTH = 2

HEAD_DIM = 64
N_HEADS_FOX = 8
N_HEADS_DIL = 8
FOX_WIDTH = N_HEADS_FOX * HEAD_DIM
DIL_WIDTH = N_HEADS_DIL * HEAD_DIM
DIL_PATTERNS = ((128, 1), (512, 4), (2048, 16))
ATTN_BLOCK = 128
ROPE_THETA = 10000.0
N_EXPERTS = 64
TOP_K = 8
N_GROUPS = 8
TOPK_GROUPS = 4
EXPERT_FF = 256
SHARED_FF = 256
ROUTED_SCALE = 2.5
MOE_BLOCK = 128
DN_ALPHA = (2 * DEPTH) ** 0.25
DN_BETA = (8 * DEPTH) ** -0.25
LN_EPS = 1e-5
FORGET_BIAS_INIT = 3.0
ADA_INIT = 0.2
NEG_INF = -1e30
IN_SIZES = (FOX_WIDTH, FOX_WIDTH, FOX_WIDTH, N_HEADS_FOX, DIL_WIDTH, DIL_WIDTH, DIL_WIDTH, D_MODEL, D_MODEL)
IN_COLS = FOX_WIDTH * 3 + N_HEADS_FOX + DIL_WIDTH * 3 + 2 * D_MODEL

kernel_name = "fox_dilated_gated_moe_deepnorm_adaln"

def _split_points(sizes):
    pts, acc = [], 0
    for s in sizes[:-1]:
        acc += s
        pts.append(acc)
    return pts

def layer_norm(x, g, b):
    xf = x.astype(jnp.float32)
    mu = jnp.mean(xf, axis=-1, keepdims=True)
    var = jnp.mean(jnp.square(xf - mu), axis=-1, keepdims=True)
    return ((xf - mu) * lax.rsqrt(var + LN_EPS) * g.astype(jnp.float32) + b.astype(jnp.float32)).astype(x.dtype)

def rotary(x, pos):
    half = HEAD_DIM // 2
    inv_freq = ROPE_THETA ** (-jnp.arange(half, dtype=jnp.float32) * 2.0 / HEAD_DIM)
    ang = pos[:, None] * inv_freq[None, :]
    cos = jnp.cos(ang)[None, :, None, :]
    sin = jnp.sin(ang)[None, :, None, :]
    xf = x.astype(jnp.float32)
    x1, x2 = xf[..., :half], xf[..., half:]
    return jnp.concatenate([x1 * cos - x2 * sin, x2 * cos + x1 * sin], axis=-1).astype(x.dtype)

def forgetting_attention(q, k, v, log_f):
    B, S, H, Dh = q.shape
    q, k, v = (t.transpose(0, 2, 1, 3) for t in (q, k, v))
    cum = jnp.cumsum(log_f, axis=1).transpose(0, 2, 1)
    scale = Dh ** -0.5
    outs = []
    for blk in range(S // ATTN_BLOCK):
        lo, hi = blk * ATTN_BLOCK, (blk + 1) * ATTN_BLOCK
        s = jnp.einsum('bhqd,bhkd->bhqk', q[:, :, lo:hi], k[:, :, :hi]).astype(jnp.float32) * scale
        s = s + cum[:, :, lo:hi, None] - cum[:, :, None, :hi]
        causal = jnp.arange(lo, hi)[:, None] >= jnp.arange(hi)[None, :]
        p = jax.nn.softmax(jnp.where(causal, s, NEG_INF), axis=-1).astype(v.dtype)
        outs.append(jnp.einsum('bhqk,bhkd->bhqd', p, v[:, :, :hi]))
    o = jnp.concatenate(outs, axis=2)
    return o.transpose(0, 2, 1, 3).reshape(B, S, H * Dh)

def dilated_window_attention(q, k, v, dilation, n_back):
    B, S, H, Dh = q.shape
    L = S // dilation
    nb = -(-L // ATTN_BLOCK)
    Lp = nb * ATTN_BLOCK

    def to_sub(t):
        t = t.reshape(B, L, dilation, H, Dh).transpose(0, 2, 3, 1, 4)
        return jnp.pad(t, ((0, 0), (0, 0), (0, 0), (0, Lp - L), (0, 0)))

    qs, ks, vs = to_sub(q), to_sub(k), to_sub(v)
    qb = qs.reshape(B, dilation, H, nb, ATTN_BLOCK, Dh)

    def key_band(t):
        tp = jnp.pad(t, ((0, 0), (0, 0), (0, 0), (ATTN_BLOCK, 0), (0, 0)))
        tp = tp.reshape(B, dilation, H, nb + 1, ATTN_BLOCK, Dh)
        return jnp.concatenate([tp[:, :, :, :-1], tp[:, :, :, 1:]], axis=4)

    kb, vb = key_band(ks), key_band(vs)
    s = jnp.einsum('brhnqd,brhnkd->brhnqk', qb, kb).astype(jnp.float32) * (Dh ** -0.5)
    i = jnp.arange(ATTN_BLOCK)[None, :, None]
    j = jnp.arange(2 * ATTN_BLOCK)[None, None, :]
    n = jnp.arange(nb)[:, None, None]
    dist = i + ATTN_BLOCK - j
    key_idx = n * ATTN_BLOCK + j - ATTN_BLOCK
    valid = (dist >= 0) & (dist <= n_back) & (key_idx >= 0)
    s = jnp.where(valid, s, NEG_INF)
    m = jnp.max(s, axis=-1, keepdims=True)
    e = jnp.exp(s - m)
    l = jnp.sum(e, axis=-1, keepdims=True)
    o = jnp.einsum('brhnqk,brhnkd->brhnqd', (e / l).astype(v.dtype), vb)
    lse = (m + jnp.log(l))[..., 0]
    o = o.reshape(B, dilation, H, Lp, Dh)[:, :, :, :L].transpose(0, 3, 1, 2, 4).reshape(B, S, H, Dh)
    lse = lse.reshape(B, dilation, H, Lp)[..., :L].transpose(0, 3, 1, 2).reshape(B, S, H)
    return o, lse

def dilated_mixture(q, k, v):
    B, S, H, Dh = q.shape
    outs, lses = [], []
    for window, dilation in DIL_PATTERNS:
        o, lse = dilated_window_attention(q, k, v, dilation, window // dilation)
        outs.append(o)
        lses.append(lse)
    w = jax.nn.softmax(jnp.stack(lses, axis=0), axis=0)
    o = jnp.sum(w[..., None] * jnp.stack(outs, axis=0).astype(jnp.float32), axis=0)
    return o.reshape(B, S, H * Dh).astype(v.dtype)

def token_mixer(u, w_in, b_forget, b_gate, w_br_fox, w_br_dil, w_o):
    B, S, D = u.shape
    proj = u @ w_in
    qf, kf, vf, ff, qd, kd, vd, ga, gb = jnp.split(proj, _split_points(IN_SIZES), axis=-1)
    fox_heads = lambda t: t.reshape(B, S, N_HEADS_FOX, HEAD_DIM)
    dil_heads = lambda t: t.reshape(B, S, N_HEADS_DIL, HEAD_DIM)
    log_f = jax.nn.log_sigmoid((ff + b_forget).astype(jnp.float32))
    y_fox = forgetting_attention(fox_heads(qf), fox_heads(kf), fox_heads(vf), log_f)
    pos = jnp.arange(S, dtype=jnp.float32)
    y_dil = dilated_mixture(rotary(dil_heads(qd), pos), rotary(dil_heads(kd), pos), dil_heads(vd))
    g_fox = jax.nn.sigmoid(ga + b_gate[:D])
    g_dil = jax.nn.sigmoid(gb + b_gate[D:])
    merged = g_fox * (y_fox @ w_br_fox) + g_dil * (y_dil @ w_br_dil)
    return merged @ w_o

def swiglu(h, w_gate, w_up, w_down):
    return (jax.nn.silu(h @ w_gate) * (h @ w_up)) @ w_down

def routed_experts(h, eidx, gw, w_eg, w_eu, w_ed):
    N, D = h.shape
    NK = N * TOP_K
    flat_e = eidx.reshape(NK)
    flat_w = gw.reshape(NK)
    flat_tok = jnp.arange(NK, dtype=jnp.int32) // TOP_K
    order = jnp.argsort(flat_e)
    e_s, tok_s, w_s = flat_e[order], flat_tok[order], flat_w[order]
    counts = jnp.bincount(flat_e, length=N_EXPERTS)
    starts = jnp.cumsum(counts) - counts
    padded = (counts + MOE_BLOCK - 1) // MOE_BLOCK * MOE_BLOCK
    pends = jnp.cumsum(padded)
    pstarts = pends - padded
    slot = pstarts[e_s] + (jnp.arange(NK, dtype=jnp.int32) - starts[e_s])
    n_blocks = -(-NK // MOE_BLOCK) + N_EXPERTS
    P = n_blocks * MOE_BLOCK
    slot_tok = jnp.full((P,), N, dtype=jnp.int32).at[slot].set(tok_s)
    slot_w = jnp.zeros((P,), h.dtype).at[slot].set(w_s)
    blk_e = jnp.minimum(jnp.searchsorted(pends, jnp.arange(n_blocks) * MOE_BLOCK, side='right'), N_EXPERTS - 1)
    h_pad = jnp.concatenate([h, jnp.zeros((1, D), h.dtype)], axis=0)

    def expert_block(args):
        toks, e = args
        xb = jnp.take(h_pad, toks, axis=0)
        return swiglu(xb, w_eg[e], w_eu[e], w_ed[e])

    out = lax.map(expert_block, (slot_tok.reshape(n_blocks, MOE_BLOCK), blk_e))
    out = out.reshape(P, D) * slot_w[:, None]
    return jax.ops.segment_sum(out, slot_tok, num_segments=N + 1)[:N]

def moe(h, w_router, router_bias, w_eg, w_eu, w_ed, w_sg, w_su, w_sd):
    N, D = h.shape
    scores = jax.nn.sigmoid(h.astype(jnp.float32) @ w_router.astype(jnp.float32))
    sel = scores + router_bias.astype(jnp.float32)
    grp = sel.reshape(N, N_GROUPS, N_EXPERTS // N_GROUPS)
    grp_score = jnp.sum(lax.top_k(grp, 2)[0], axis=-1)
    _, gidx = lax.top_k(grp_score, TOPK_GROUPS)
    gmask = jnp.sum(jax.nn.one_hot(gidx, N_GROUPS, dtype=jnp.float32), axis=1)
    emask = jnp.repeat(gmask, N_EXPERTS // N_GROUPS, axis=1)
    _, eidx = lax.top_k(jnp.where(emask > 0, sel, NEG_INF), TOP_K)
    gw = jnp.take_along_axis(scores, eidx, axis=-1)
    gw = gw / jnp.sum(gw, axis=-1, keepdims=True) * ROUTED_SCALE
    routed = routed_experts(h, eidx, gw.astype(h.dtype), w_eg, w_eu, w_ed)
    return routed + swiglu(h, w_sg, w_su, w_sd)

def setup_inputs(seed: int = 0) -> dict:
    key = jax.random.key(seed)
    ks = jax.random.split(key, 22)
    nrm = lambda k, shape, scale: jax.random.normal(k, shape, jnp.float32) * scale
    D = D_MODEL
    return {
        "x": nrm(ks[0], (BATCH, SEQ, D), 1.0),
        "c": nrm(ks[1], (BATCH, D), 1.0),
        "w_ada": nrm(ks[2], (DEPTH, D, 6 * D), ADA_INIT * D ** -0.5),
        "b_ada": nrm(ks[3], (DEPTH, 6 * D), 0.02),
        "w_in": nrm(ks[4], (DEPTH, D, IN_COLS), D ** -0.5),
        "b_forget": FORGET_BIAS_INIT + nrm(ks[5], (DEPTH, N_HEADS_FOX), 0.5),
        "b_gate": nrm(ks[6], (DEPTH, 2 * D), 0.02),
        "w_br_fox": nrm(ks[7], (DEPTH, FOX_WIDTH, D), FOX_WIDTH ** -0.5),
        "w_br_dil": nrm(ks[8], (DEPTH, DIL_WIDTH, D), DIL_WIDTH ** -0.5),
        "w_o": nrm(ks[9], (DEPTH, D, D), DN_BETA * D ** -0.5),
        "ln_g": 1.0 + nrm(ks[10], (DEPTH, 2, D), 0.02),
        "ln_b": nrm(ks[11], (DEPTH, 2, D), 0.02),
        "w_router": nrm(ks[12], (DEPTH, D, N_EXPERTS), D ** -0.5),
        "router_bias": nrm(ks[13], (DEPTH, N_EXPERTS), 0.01),
        "w_exp_gate": nrm(ks[14], (DEPTH, N_EXPERTS, D, EXPERT_FF), D ** -0.5),
        "w_exp_up": nrm(ks[15], (DEPTH, N_EXPERTS, D, EXPERT_FF), D ** -0.5),
        "w_exp_down": nrm(ks[16], (DEPTH, N_EXPERTS, EXPERT_FF, D), DN_BETA * EXPERT_FF ** -0.5),
        "w_sh_gate": nrm(ks[17], (DEPTH, D, SHARED_FF), D ** -0.5),
        "w_sh_up": nrm(ks[18], (DEPTH, D, SHARED_FF), D ** -0.5),
        "w_sh_down": nrm(ks[19], (DEPTH, SHARED_FF, D), DN_BETA * SHARED_FF ** -0.5),
    }

def reference(x, c, w_ada, b_ada, w_in, b_forget, b_gate, w_br_fox, w_br_dil, w_o, ln_g, ln_b,
              w_router, router_bias, w_exp_gate, w_exp_up, w_exp_down, w_sh_gate, w_sh_up, w_sh_down):
    B, S, D = x.shape
    cs = jax.nn.silu(c)
    for l in range(DEPTH):
        mod = cs @ w_ada[l] + b_ada[l]
        sh1, sc1, g1, sh2, sc2, g2 = [m[:, None, :] for m in jnp.split(mod, 6, axis=-1)]
        u = x * (1.0 + sc1) + sh1
        y = token_mixer(u, w_in[l], b_forget[l], b_gate[l], w_br_fox[l], w_br_dil[l], w_o[l])
        x = layer_norm(DN_ALPHA * x + (1.0 + g1) * y, ln_g[l, 0], ln_b[l, 0])
        u = (x * (1.0 + sc2) + sh2).reshape(B * S, D)
        y = moe(u, w_router[l], router_bias[l], w_exp_gate[l], w_exp_up[l], w_exp_down[l],
                w_sh_gate[l], w_sh_up[l], w_sh_down[l]).reshape(B, S, D)
        x = layer_norm(DN_ALPHA * x + (1.0 + g2) * y, ln_g[l, 1], ln_b[l, 1])
    return x


_drawn_inputs = setup_inputs


def setup_inputs(seed=0):
    import zlib

    import numpy as np

    out = dict(_drawn_inputs(seed))
    spreads = {}
    factors = {'b_gate': 6.049}
    for name, (base, spread) in spreads.items():
        noise = np.random.default_rng([zlib.crc32(name.encode()), seed]).standard_normal(out[name].shape)
        drawn = base * np.exp(spread * noise) if base else spread * noise
        out[name] = __import__('jax').numpy.asarray(drawn.astype(out[name].dtype))
    for name, factor in factors.items():
        out[name] = (out[name] * factor).astype(out[name].dtype)
    return out
```

```python
from contextlib import ExitStack

import numpy as np

import concourse.bass as bass
from concourse import mybir

P = 128
D = 1024
S = 256
DEPTH = 2
TT = S // P
KT = D // P
HD = 64
NH = 8
BW = NH * HD
BT = BW // P
NE = 64
TOPK = 8
NG = 8
FF = 256
CAP = 64
OCT = 8
ROUNDS = NE // OCT
SLOTS = 4
STATIC_LOADS = 24
GEN = STATIC_LOADS // SLOTS
SLOT = 2 * KT * FF + 2 * D
ADA_CHUNKS = 8
ADA_W = 6 * D // ADA_CHUNKS
ALPHA = float((2 * DEPTH) ** 0.25)
SCALE = HD ** -0.5
ROUTED_SCALE = 2.5
LN_EPS = 1e-5
NEG = -1e30
DVE_STEPS = 89
FF_COL = 3 * BW

F32 = mybir.dt.float32
I32 = mybir.dt.int32
ALU = mybir.AluOpType
ACT = mybir.ActivationFunctionType
AX = mybir.AxisListType.X

C_ROPE = 0
C_MASK = C_ROPE + TT * 64
C_TRI = C_MASK + 2 * 384
C_ONES = C_TRI + P
C_TRIS = C_ONES + P
C_ID = C_TRIS + P
C_IOTA = C_ID + P
C_LT8 = C_IOTA + CAP
C_QUAD = C_LT8 + NG * NG
C_ZERO = C_QUAD + P
C_THR = C_ZERO + NE
N_THR = -(-S // CAP) - 1
C_END = C_THR + N_THR


def constants():
    t = np.zeros((P, C_END), np.float32)
    half = HD // 2
    freq = (np.float32(10000.0) ** (-np.arange(half, dtype=np.float32) * np.float32(2.0) / np.float32(HD))).astype(np.float32)
    ang = (np.arange(S, dtype=np.float32)[:, None] * freq[None, :]).astype(np.float32)
    rope = np.stack([np.cos(ang), np.sin(ang)], axis=1).astype(np.float32)
    t[:, C_ROPE:C_MASK] = rope.reshape(TT, P, 64).transpose(1, 0, 2).reshape(P, -1)
    q = np.arange(S)[:, None]
    k = np.arange(S)[None, :]
    causal = q >= k
    fox = np.where(causal, 0.0, NEG)
    often = np.zeros((S, S))
    for window, dil in ((128, 1), (512, 4), (2048, 16)):
        often += causal & ((q - k) % dil == 0) & ((q - k) // dil <= window // dil)
    dilated = np.where(often > 0, np.log(np.maximum(often, 1.0)), NEG)
    for n, m in enumerate((fox, dilated)):
        t[:, C_MASK + 384 * n:C_MASK + 384 * n + P] = m[:P, :P]
        t[:, C_MASK + 384 * n + P:C_MASK + 384 * n + 384] = m[P:, :]
    r = np.arange(P)
    t[:, C_TRI:C_TRI + P] = r[:, None] <= r[None, :]
    t[:, C_ONES:C_ONES + P] = 1.0
    t[:, C_TRIS:C_TRIS + P] = r[:, None] < r[None, :]
    t[:, C_ID:C_ID + P] = np.eye(P)
    t[:, C_IOTA:C_IOTA + CAP] = np.arange(CAP)
    t[:, C_LT8:C_LT8 + NG * NG] = (np.arange(NG)[None, :] < np.arange(NG)[:, None]).reshape(-1)
    t[::32, C_QUAD:C_QUAD + P] = 1.0
    t[:, C_THR:C_END] = CAP * np.arange(1, N_THR + 1)
    return t


def decoder(nc, x, c, w_ada, b_ada, w_in, b_forget, b_gate, w_br_fox, w_br_dil, w_o, ln_g, ln_b, w_router,
            router_bias, w_exp_gate, w_exp_up, w_exp_down, w_sh_gate, w_sh_up, w_sh_down, consts, out):
    with ExitStack() as ctx:
        def sb(name, shape, dt=F32):
            return ctx.enter_context(nc.sbuf_tensor(name, shape, dt))

        def sem(name):
            return ctx.enter_context(nc.semaphore(name))

        ring = [sb(f"ring{i}", [P, SLOT]) for i in range(SLOTS)]
        cst = sb("cst", [P, C_END])
        xs = sb("xs", [P, TT, D])
        uz = sb("uz", [P, TT * D])
        uT = uz[:, :].rearrange("p (t n) -> p t n", t=KT)
        z = uz[:, :].rearrange("p (t n) -> p t n", t=TT)
        gate1p = sb("gate1p", [P, 2, D])
        lnp = sb("lnp", [P, 2, D])
        mod_parts = sb("mod_parts", [P, 6 * D])
        gatesT = mod_parts[:, 0:2 * KT * S].rearrange("p (g n) -> p g n", n=S)
        yT = mod_parts[:, 2 * KT * S:].rearrange("p (b t n) -> p b t n", b=2, t=BT)
        mid = sb("mid", [P, 6 * D])
        qkT = mid[:, 0:4 * D].rearrange("p (a t n) -> p a t n", a=4, t=BT)
        vv = mid[:, 4 * D:6 * D].rearrange("p (a t n) -> p a t n", a=2, t=TT)
        xg = mid[:, 0:4 * D].rearrange("p (t n) -> p t n", t=KT)
        sel = mid[:, 4 * D:5 * D].rearrange("p (t e s) -> p t e s", t=TT, e=OCT)
        selw = mid[:, 5 * D:6 * D].rearrange("p (t e s) -> p t e s", t=TT, e=OCT)
        shs = mid[:, 0:512]
        hsT = mid[:, 512:1024].rearrange("p (t n) -> p t n", t=2)
        small = sb("small", [P, 9 * 256])
        sS = [small[:, 384 * i:384 * i + 384] for i in range(2)]
        pS = [small[:, 768 + 384 * i:768 + 384 * i + 384] for i in range(2)]
        pT = [small[:, 1536 + 384 * i:1536 + 384 * i + 384] for i in range(2)]
        sg = small[:, 0:256]
        hb = small[:, 256:512]
        hT = small[:, 512:768]
        swT = [small[:, 768 + 256 * i:1024 + 256 * i] for i in range(2)]
        ys = small[:, 1280:2304]
        mr = sb("mr", [P, 2 * D])
        rot = mr[:, :].rearrange("p (a t n) -> p a t n", a=2, t=TT)
        mergedT = mr[:, :].rearrange("p (t n) -> p t n", t=KT)
        rope_tmp = mod_parts[:, 5 * D:].rearrange("p (i n) -> p i n", i=4)
        merge_tmp = small[:, 0:D].rearrange("p (i n) -> p i n", i=4)
        cT = sb("cT", [P, KT])
        csT = sb("csT", [P, KT])
        csrep = sb("csrep", [P, KT, 32])
        modc = sb("modc", [P, 4, KT])
        wff = sb("wff", [P, KT, NH])
        bgate = sb("bgate", [P, 2 * KT])
        bforget = sb("bforget", [P, NH])
        wrt = sb("wrt", [P, KT, NE])
        rbias = sb("rbias", [P, NE])
        zf = sb("zf", [P, TT, NH])
        zabs = sb("zabs", [P, TT, NH])
        zexp = sb("zexp", [P, TT, NH])
        softp = sb("softp", [P, TT, NH])
        zneg = sb("zneg", [P, TT, NH])
        nlogf = sb("nlogf", [P, TT, NH])
        ncum = sb("ncum", [P, TT, NH])
        ncumT = sb("ncumT", [NH, S])
        nmax = sb("nmax", [P, 2, TT])
        lsum = sb("lsum", [P, 2, TT])
        rsum = sb("rsum", [P, 2, TT])
        bst = sb("bst", [P, TT, 2, 6])
        mv = sb("mv", [P, TT, 2])
        ve = sb("ve", [P, TT])
        sd = sb("sd", [P, TT])
        rstd = sb("rstd", [P, TT])
        score = mr[:, 0:128].rearrange("p (t e) -> p t e", t=TT)
        choice = mr[:, 128:256].rearrange("p (t e) -> p t e", t=TT)
        gmax = mr[:, 1152:1280].rearrange("p (t g i) -> p t g i", t=TT, g=NG)
        gsc = sb("gsc", [P, TT, NG])
        gcmp = mr[:, 1280:1408].rearrange("p (t g i) -> p t g i", t=TT, g=NG)
        geq = mr[:, 1408:1536].rearrange("p (t g i) -> p t g i", t=TT, g=NG)
        grank = sb("grank", [P, TT, NG])
        gmask = sb("gmask", [P, TT, NG])
        gpen = sb("gpen", [P, TT, NG])
        top8 = sb("top8", [P, TT, 8])
        above = mr[:, 256:384].rearrange("p (t e) -> p t e", t=TT)
        nabove = sb("nabove", [P, TT])
        ties = mr[:, 384:512].rearrange("p (t e) -> p t e", t=TT)
        tiesum = mr[:, 512:640].rearrange("p (t e) -> p t e", t=TT)
        emask = mr[:, 640:768].rearrange("p (t e) -> p t e", t=TT)
        wraw = mr[:, 768:896].rearrange("p (t e) -> p t e", t=TT)
        wsum = sb("wsum", [P, TT])
        wrec = sb("wrec", [P, TT])
        wtok = mr[:, 896:1024].rearrange("p (t e) -> p t e", t=TT)
        erank = mr[:, 1024:1152].rearrange("p (t e) -> p t e", t=TT)
        mostf = sb("mostf", [P, 1])
        overf = sb("overf", [P, N_THR])
        morep = sb("morep", [P, 1])
        passf = sb("passf", [P, 1])
        passi = sb("passi", [P, 1], I32)
        slotno = sb("slotno", [P, CAP])

        ps = [ctx.enter_context(nc.psum_tensor(f"ps{i}", [P, 512], F32)) for i in range(8)]
        ACC = ps[0:4]
        HB, GB, YB = ps[4], ps[5], ps[6:8]

        ident = cst[:, C_ID:C_ID + P]
        tri = cst[:, C_TRI:C_TRI + P]
        tri_ones = cst[:, C_TRI:C_TRI + 2 * P]
        tri_strict = cst[:, C_TRIS:C_TRIS + P]
        ones = cst[:, C_ONES:C_ONES + P]
        quad = cst[:, C_QUAD:C_QUAD + P]

        def mask(kind, tt):
            a = C_MASK + 384 * kind
            return cst[:, a:a + P] if tt == 0 else cst[:, a + P:a + 384]

        def part(tt):
            return slice(0, P) if tt == 0 else slice(P, 384)

        def gu_view(s):
            return ring[s][:, 0:2 * KT * FF].rearrange("p (g t f) -> p g t f", g=2, t=KT)

        def down_view(s, at=2 * KT * FF):
            return ring[s][:, at:at + 2 * D].rearrange("p (t n) -> p t n", t=2)

        const_in, x_in, c_in = sem("const_in"), sem("x_in"), sem("c_in")
        params_in, bias_in, ln_in = sem("params_in"), sem("bias_in"), sem("ln_in")
        ring_full = [sem(f"ring_full{i}") for i in range(SLOTS)]
        ring_free = [sem(f"ring_free{i}") for i in range(SLOTS)]
        out_done = sem("out_done")
        cs_ready, csrep_ready = sem("cs_ready"), sem("csrep_ready")
        zero_parts, ada_ready, parts_ready = sem("zero_parts"), sem("ada_ready"), sem("parts_ready")
        modcol_ready, modc_ready, grow_ready = sem("modcol_ready"), sem("modc_ready"), sem("grow_ready")
        gate_ready1p = sem("gate_ready1p")
        xt_ready, u_dve, u_act = sem("xt_ready"), sem("u_dve"), sem("u_act")
        proj_ready, qkv_act, rot_ready = sem("proj_ready"), sem("qkv_act"), sem("rot_ready")
        rt_ready = sem("rt_ready")
        ff_ready, ffz_ready, softp_ready = sem("ff_ready"), sem("ffz_ready"), sem("softp_ready")
        nlogf_ready, cum_ready, cumc_ready = sem("nlogf_ready"), sem("cum_ready"), sem("cumc_ready")
        s_ready, nm_ready, exp_ready = sem("s_ready"), sem("nm_ready"), sem("exp_ready")
        p_ready, pt_ready, pts_ready = sem("p_ready"), sem("pt_ready"), sem("pts_ready")
        pv_ready, y_ready = sem("pv_ready"), sem("y_ready")
        gate_ready, gates_raw, gates_ready = sem("gate_ready"), sem("gates_raw"), sem("gates_ready")
        br_ready, merged_ready, wo_ready = sem("br_ready"), sem("merged_ready"), sem("wo_ready")
        ve_ready, sd_ready, xn_ready = sem("ve_ready"), sem("sd_ready"), sem("xn_ready")
        x_ready = sem("x_ready")
        logits_ready, score_ready, shgu_ready = sem("logits_ready"), sem("score_ready"), sem("shgu_ready")
        shs_ready, hs_ready, emask_ready = sem("shs_ready"), sem("hs_ready"), sem("emask_ready")
        rank_ready, wtok_ready, pass_ready = sem("rank_ready"), sem("wtok_ready"), sem("pass_ready")
        sel_ready, selw_ready, iota_ready = sem("sel_ready"), sem("selw_ready"), sem("iota_ready")
        gth_ready, xg_dve, xg_act = sem("gth_ready"), sem("xg_dve"), sem("xg_act")
        gu_ready, sg_ready, h_ready = sem("gu_ready"), sem("sg_ready"), sem("h_ready")
        ht_ready, hts_ready = sem("ht_ready"), sem("hts_ready")
        swt_ready, swts_ready, yp_ready = sem("swt_ready"), sem("swts_ready"), sem("yp_ready")
        ya_ready, yd_ready, acc_ready = sem("ya_ready"), sem("yd_ready"), sem("acc_ready")
        dve_step, act_step, pool_step = sem("dve_step"), sem("act_step"), sem("pool_step")
        gone_by = sem("gone_by")


        def apart(eng):
            eng.sem_inc(gone_by, 1)

        block = ctx.enter_context(nc.Block())

        @block.sync
        def _(sp):
            sp.dma_start(cst[:, :], consts).then_inc(const_in, 16)
            sp.dma_start(cT[:, :], c.rearrange("o (p t) -> p (o t)", t=KT)).then_inc(c_in, 16)
            sp.dma_start(xs[:, :, :], x[0].rearrange("(t p) d -> p t d", p=P)).then_inc(x_in, 16)

            ada = w_ada.rearrange("l (p t) n -> l p t n", t=KT)
            win = w_in.rearrange("l (p t) n -> l p t n", t=KT)
            wbr = [w.rearrange("l (t p) n -> l p t n", p=P) for w in (w_br_fox, w_br_dil)]
            wo = w_o.rearrange("l (t p) n -> l p t n", p=P)
            sh_g, sh_u = (w.rearrange("l (p t) f -> l p t f", t=KT) for w in (w_sh_gate, w_sh_up))
            sh_d = w_sh_down.rearrange("l (p t) n -> l p t n", t=2)
            ex_g, ex_u = (w.rearrange("l (o e) (p t) f -> l o e p t f", e=OCT, t=KT) for w in (w_exp_gate, w_exp_up))
            ex_d = w_exp_down.rearrange("l (o e) (p t) n -> l o e p t n", e=OCT, t=2)

            def load(n, gen, pieces):
                sp.wait_ge(ring_free[n % SLOTS], gen + 1)
                assert len(pieces) == 3
                for dst, src in pieces:
                    sp.dma_start(dst, src).then_inc(ring_full[n % SLOTS], 16)

            def rows(n, width, src, count=KT):
                dst = ring[n % SLOTS][:, 0:count * width].rearrange("p (t n) -> p t n", t=count)
                a, b = count // 2, count - count // 4
                return [(dst[:, i:j, :], src[:, i:j, :]) for i, j in ((0, a), (a, b), (b, count))]

            def expert(n, gen, l, o, j):
                gu = gu_view(n % SLOTS)
                load(n, gen, [(gu[:, 0, :, :], ex_g[l, o, j]), (gu[:, 1, :, :], ex_u[l, o, j]),
                              (down_view(n % SLOTS), ex_d[l, o, j])])

            with sp.Fori(0, DEPTH) as l:
                sp.wait_ge(pass_ready, l + 1)
                apart(sp)
                base = sp.value_load(passi[0:1, 0:1], min_val=0, max_val=4 * DEPTH)
                gen0 = l * GEN + base * (NE // SLOTS)
                n = 0
                for i in range(ADA_CHUNKS):
                    load(n, gen0 + n // SLOTS, rows(n, ADA_W, ada[l][:, :, i * ADA_W:(i + 1) * ADA_W]))
                    n += 1
                for col in (0, BW, FF_COL + NH, FF_COL + NH + BW, 2 * BW, FF_COL + NH + 2 * BW,
                            *(FF_COL + NH + 3 * BW + BW * i for i in range(4))):
                    load(n, gen0 + n // SLOTS, rows(n, BW, win[l][:, :, col:col + BW]))
                    n += 1
                for w in wbr:
                    load(n, gen0 + n // SLOTS, rows(n, D, w[l], BT))
                    n += 1
                for half in range(2):
                    load(n, gen0 + n // SLOTS, rows(n, 512, wo[l][:, :, half * 512:half * 512 + 512]))
                    n += 1
                gu = gu_view(n % SLOTS)
                load(n, gen0 + n // SLOTS, [(gu[:, 0, :, :], sh_g[l]), (gu[:, 1, 0:4, :], sh_u[l][:, 0:4, :]),
                                            (gu[:, 1, 4:8, :], sh_u[l][:, 4:8, :])])
                n += 1
                dn = down_view(n % SLOTS, 0)
                load(n, gen0 + n // SLOTS, [(dn[:, 0, :], sh_d[l][:, 0, :]), (dn[:, 1, 0:512], sh_d[l][:, 1, 0:512]),
                                            (dn[:, 1, 512:D], sh_d[l][:, 1, 512:D])])
                n += 1
                assert n == STATIC_LOADS
                for j in range(OCT):
                    expert(j, gen0 + GEN + j // SLOTS, l, 0, j)
                sp.wait_ge(pass_ready, l + 2)
                apart(sp)
                end = sp.value_load(passi[0:1, 0:1], min_val=1, max_val=4 * DEPTH)
                with sp.Fori(base * ROUNDS + 1, end * ROUNDS) as rnd:
                    for j in range(OCT):
                        expert(j, (l + 1) * GEN + rnd * (OCT // SLOTS) + j // SLOTS, l, rnd % ROUNDS, j)
            sp.wait_ge(x_ready, 4 * DEPTH + 1)
            sp.dma_start(out[0].rearrange("(t p) d -> p t d", p=P), xs[:, :, :]).then_inc(out_done, 16)
            sp.wait_ge(out_done, 16)

        @block.gpsimd
        def _(pool):
            pool.memset(morep[:, :], 0.0).then_inc(x_ready, 1)
            with pool.Fori(0, DEPTH) as l:
                pool.wait_ge(pass_ready, l + 1)
                apart(pool)
                base = pool.value_load(passi[0:1, 0:1], min_val=0, max_val=4 * (DEPTH - 1))
                pool.wait_ge(x_ready, l * 4 + 1)
                apart(pool)
                pool.memset(mod_parts[:, :], 0.0).then_inc(zero_parts, 1)
                pool.wait_ge(zero_parts, l + 1)
                pool.dma_start(mod_parts[0:1, :], b_ada.unsqueeze(1)[l]).then_inc(bias_in, 16)
                for dst, src in ((wff[:, :, :], w_in.rearrange("l (p t) n -> l p t n", t=KT)[l][:, :, FF_COL:FF_COL + NH]),
                                 (bgate[:, :], b_gate.rearrange("l (g p) -> l p g", p=P)[l]),
                                 (bforget[:, :], b_forget[l].partition_broadcast(P)),
                                 (wrt[:, :, :], w_router.rearrange("l (p t) n -> l p t n", t=KT)[l]),
                                 (rbias[:, :], router_bias[l].partition_broadcast(P))):
                    pool.dma_start(dst, src, allow_slow_non_contiguous=True).then_inc(params_in, 16)

                def norm_params(which):
                    for i, w in enumerate((ln_g, ln_b)):
                        pool.dma_start(lnp[:, i, :], w[l][which, :].partition_broadcast(P)).then_inc(ln_in, 16)

                def norm_tail(which):
                    pool.wait_ge(ln_in, l * 64 + 32 * (which + 1))
                    for tt in range(TT):
                        n = which * TT + tt
                        pool.wait_ge(xn_ready, l * 4 + n + 1)
                        pool.tensor_tensor(xs[:, tt, :], xs[:, tt, :], lnp[:, 0, :], ALU.mult).then_inc(pool_step, 1)
                        pool.wait_ge(pool_step, l * 4 + n + 1)
                        pool.tensor_tensor(xs[:, tt, :], xs[:, tt, :], lnp[:, 1, :], ALU.add).then_inc(x_ready, 1)

                norm_params(0)
                norm_tail(0)
                pool.wait_ge(x_ready, l * 4 + 3)
                norm_params(1)
                pool.wait_ge(wtok_ready, l + 1)
                pool.wait_ge(pass_ready, l + 2)
                apart(pool)
                end = pool.value_load(passi[0:1, 0:1], min_val=1, max_val=4 * DEPTH)
                with pool.Fori(base * ROUNDS, end * ROUNDS) as rnd:
                    for tt in range(TT):
                        pool.wait_ge(sel_ready, rnd * TT + tt + 1)
                        w8 = wtok[:, tt, bass.ds((rnd % ROUNDS) * OCT, OCT)]
                        pool.tensor_tensor(selw[:, tt, :, :], sel[:, tt, :, :],
                                           w8.unsqueeze(2).to_broadcast([P, OCT, CAP]), ALU.mult).then_inc(selw_ready, 1)
                norm_tail(1)

        @block.tensor
        def _(pe):
            def mm(dst, lhsT, rhs, start=True, stop=True, **kw):
                return nc.tensor.matmul(dst, lhsT, rhs, start=start, stop=stop, **kw)

            for i in range(SLOTS):
                pe.sem_inc(ring_free[i], 1)
            pe.wait_ge(const_in, 16)
            pe.wait_ge(x_in, 16)
            pe.wait_ge(csrep_ready, 1)
            with pe.Fori(0, DEPTH) as l:
                pe.wait_ge(pass_ready, l + 1)
                apart(pe)
                base = pe.value_load(passi[0:1, 0:1], min_val=0, max_val=4 * (DEPTH - 1))
                gen0 = l * GEN + base * (NE // SLOTS)
                freed = []

                def landed(n, gen):
                    pe.wait_ge(ring_full[n % SLOTS], (gen + 1) * 48)

                def free(ins):
                    ins.then_inc(ring_free[freed.pop()], 1)

                for n in range(ADA_CHUNKS):
                    landed(n, gen0 + n // SLOTS)
                    w = ring[n % SLOTS][:, 0:KT * ADA_W].rearrange("p (t n) -> p t n", t=KT)
                    for half in range(2):
                        k = 2 * n + half
                        if k >= 4:
                            pe.wait_ge(parts_ready, l * 16 + k - 3)
                        elif k == 0:
                            pe.wait_ge(x_ready, l * 4 + 1)
                        for t in range(KT):
                            q = t % 4
                            m = mm(ps[k % 4][32 * q:32 * q + 32, 0:ADA_W // 2], csrep[:, t, :],
                                   w[:, t, half * ADA_W // 2:(half + 1) * ADA_W // 2],
                                   start=t < 4, stop=t >= 4, tile_position=(0, 32 * q))
                            if t == 0 and freed:
                                free(m)
                        m.then_inc(ada_ready, 1)
                    freed.append(n % SLOTS)
                pe.wait_ge(parts_ready, l * 16 + 16)
                for i, j in enumerate((0, 3, 1, 4)):
                    for t in range(KT):
                        m = mm(ps[3][:, i * KT + t:i * KT + t + 1], mod_parts[:, j * D + t:(j + 1) * D:KT], quad[:, 0:1])
                        if freed:
                            free(m)
                m.then_inc(modcol_ready, 1)
                for i in range(4):
                    if i == 3:
                        pe.wait_ge(modc_ready, l * 2 + 2)
                    a = (2, 5)[i // 2] * D + i % 2 * 512
                    mm(ps[i][:, :], quad, mod_parts[:, a:a + 512]).then_inc(grow_ready, 1)

                def transpose_x(which):
                    for b in range(4):
                        for t in (2 * b, 2 * b + 1):
                            for tt in range(TT):
                                a = t % 2 * S + tt * P
                                m = nc.tensor.transpose(ps[4 + b][:, a:a + P], xs[:, tt, t:D:KT], ident)
                        m.then_inc(xt_ready, 1)

                transpose_x(0)
                pe.wait_ge(u_dve, l * 8 + 4)
                pe.wait_ge(u_act, l * 8 + 4)
                pe.wait_ge(gate_ready1p, l * 4 + 4)

                for i in range(6):
                    n = ADA_CHUNKS + i
                    landed(n, gen0 + n // SLOTS)
                    w = ring[n % SLOTS][:, 0:KT * BW].rearrange("p (t n) -> p t n", t=KT)
                    if i >= 4:
                        pe.wait_ge(qkv_act, l * 12 + 2 * (i - 3))
                    for half in range(2):
                        bank = ps[2 * (i % 4) + half]
                        for b in range(2 if i < 2 else 1):
                            for t in range(KT):
                                if i < 2:
                                    f = (2 * half + b) * P
                                    m = mm(bank[:, b * S:b * S + S], w[:, t, f:f + P], uT[:, t, :], t == 0, t == KT - 1)
                                else:
                                    m = mm(bank[:, :], uT[:, t, half * P:half * P + P], w[:, t, :], t == 0, t == KT - 1)
                                if freed:
                                    free(m)
                        m.then_inc(proj_ready, 1)
                    freed.append(n % SLOTS)
                pe.wait_ge(qkv_act, l * 12 + 6)
                pe.wait_ge(params_in, l * 80 + 80)
                for tt in range(TT):
                    for t in range(KT):
                        m = mm(ps[0][:, tt * NH:tt * NH + NH], uT[:, t, tt * P:tt * P + P], wff[:, t, :], t == 0, t == KT - 1)
                        if freed:
                            free(m)
                m.then_inc(ff_ready, 1)
                pe.wait_ge(rot_ready, l * 4 + 4)
                for b in range(4):
                    for kt in (2 * b, 2 * b + 1):
                        for tt in range(TT):
                            a = kt % 2 * S + tt * P
                            m = nc.tensor.transpose(ps[4 + b][:, a:a + P], rot[:, kt // BT, tt, kt % BT * P:kt % BT * P + P], ident)
                    m.then_inc(rt_ready, 1)
                pe.wait_ge(nlogf_ready, l + 1)
                mm(ps[1][:, 0:NH], tri, nlogf[:, 0, :])
                mm(ps[1][:, NH:2 * NH], ones, nlogf[:, 0, :], True, False)
                mm(ps[1][:, NH:2 * NH], tri, nlogf[:, 1, :], False, True)
                mm(ps[1][0:NH, P:3 * P], nlogf[:, 0, :], tri_ones, True, False)
                mm(ps[1][0:NH, 2 * P:3 * P], nlogf[:, 1, :], tri, False, True).then_inc(cum_ready, 1)

                def scores(h):
                    kind, hh = divmod(h, NH)
                    a, kt = 64 * (hh % 2), hh // 2
                    if h >= 2:
                        pe.wait_ge(nm_ready, l * 16 + h - 1)
                    q, k = qkT[a:a + HD, 2 * kind, kt, :], qkT[a:a + HD, 2 * kind + 1, kt, :]
                    for tt in range(TT):
                        dst = ps[4 + h % 2][:, part(tt)]
                        keys = (tt + 1) * P
                        m = mm(dst, q[:, tt * P:tt * P + P], k[:, 0:keys], True, kind == 1)
                        if kind == 0:
                            m = mm(dst, ident[0:NH, hh:hh + 1].to_broadcast([NH, P]), ncumT[:, 0:keys], False, True)
                    m.then_inc(s_ready, 1)

                def gate_columns(g):
                    n = ADA_CHUNKS + 6 + g // 4
                    if g % 4 == 0:
                        landed(n, gen0 + n // SLOTS)
                    if g >= 2:
                        pe.wait_ge(gates_raw, l * 16 + g - 1)
                    w = ring[n % SLOTS][:, 0:KT * BW].rearrange("p (t n) -> p t n", t=KT)
                    for t in range(KT):
                        m = mm(ps[g % 2][:, 0:S], w[:, t, g % 4 * P:g % 4 * P + P], uT[:, t, :], t == 0, t == KT - 1)
                        if freed:
                            free(m)
                    m.then_inc(gate_ready, 1)
                    if g % 4 == 3:
                        freed.append(n % SLOTS)

                def probs_transposed(h):
                    pe.wait_ge(p_ready, l * 16 + h + 1)
                    if h >= 2:
                        pe.wait_ge(pts_ready, l * 16 + h - 1)
                    for i in range(3):
                        m = nc.tensor.transpose(ps[6 + h % 2][:, (0, 1, 2)[i] * P:(i + 1) * P], pS[h % 2][:, i * P:i * P + P], ident)
                    m.then_inc(pt_ready, 1)

                def values(h):
                    kind, hh = divmod(h, NH)
                    a, kt = 64 * (hh % 2), hh // 2
                    bank = ps[2 + h // 2 % 2]
                    if h >= 4 and h % 2 == 0:
                        pe.wait_ge(y_ready, l * 8 + h // 2 - 1)
                    pe.wait_ge(pts_ready, l * 16 + h + 1)
                    col = slice(hh * HD, hh * HD + HD)
                    mm(bank[a:a + HD, 0:S], vv[:, kind, 0, col], pT[h % 2][:, 0:S], True, False, tile_position=(0, a))
                    m = mm(bank[a:a + HD, P:S], vv[:, kind, 1, col], pT[h % 2][:, S:S + P], False, True, tile_position=(0, a))
                    if h % 2:
                        m.then_inc(pv_ready, 1)

                pe.wait_ge(cumc_ready, l * 2 + 2)
                pe.wait_ge(qkv_act, l * 12 + 12)
                for h in range(2 * NH + 2):
                    if h < 2 * NH:
                        scores(h)
                        gate_columns(h)
                    if 1 <= h <= 2 * NH:
                        probs_transposed(h - 1)
                    if h >= 2:
                        values(h - 2)

                nb = ADA_CHUNKS + 10
                landed(nb, gen0 + nb // SLOTS)
                landed(nb + 1, gen0 + (nb + 1) // SLOTS)
                pe.wait_ge(y_ready, l * 8 + 8)
                pe.wait_ge(gates_ready, l + 1)
                for j in range(KT):
                    if j >= 4:
                        pe.wait_ge(merged_ready, l * 8 + j - 3)
                    for b in range(2):
                        w = ring[(nb + b) % SLOTS][:, 0:BT * D].rearrange("p (t n) -> p t n", t=BT)
                        for kt in range(BT):
                            m = mm(ps[j % 4][:, b * S:b * S + S], w[:, kt, j * P:j * P + P], yT[:, b, kt, :], kt == 0, kt == BT - 1)
                            if freed:
                                free(m)
                    m.then_inc(br_ready, 1)
                freed += [nb % SLOTS, (nb + 1) % SLOTS]
                pe.wait_ge(merged_ready, l * 8 + 8)
                for half in range(2):
                    n = nb + 2 + half
                    landed(n, gen0 + n // SLOTS)
                    w = ring[n % SLOTS][:, 0:KT * 512].rearrange("p (t n) -> p t n", t=KT)
                    for tt in range(TT):
                        for t in range(KT):
                            m = mm(ps[4 + 2 * half + tt][:, :], mergedT[:, t, tt * P:tt * P + P], w[:, t, :], t == 0, t == KT - 1)
                            if freed:
                                free(m)
                        m.then_inc(wo_ready, 1)
                    freed.append(n % SLOTS)

                pe.wait_ge(x_ready, l * 4 + 3)
                transpose_x(1)
                pe.wait_ge(u_dve, l * 8 + 8)
                pe.wait_ge(u_act, l * 8 + 8)
                for tt in range(TT):
                    for t in range(KT):
                        m = mm(ps[0][:, tt * NE:tt * NE + NE], uT[:, t, tt * P:tt * P + P], wrt[:, t, :], t == 0, t == KT - 1)
                        if freed:
                            free(m)
                m.then_inc(logits_ready, 1)
                n = nb + 4
                landed(n, gen0 + n // SLOTS)
                for g in range(2):
                    for ft in range(2):
                        for t in range(KT):
                            m = mm(ps[1 + g][:, ft * S:ft * S + S], gu_view(n % SLOTS)[:, g, t, ft:FF:2], uT[:, t, :], t == 0, t == KT - 1)
                m.then_inc(shgu_ready, 1)
                freed.append(n % SLOTS)
                pe.wait_ge(emask_ready, l * 2 + 2)
                free(mm(ps[3][:, 0:NE], tri_strict, emask[:, 0, :]))
                mm(ps[3][:, NE:2 * NE], ones, emask[:, 0, :], True, False)
                mm(ps[3][:, NE:2 * NE], tri_strict, emask[:, 1, :], False, True)
                mm(ps[3][:, 2 * NE:3 * NE], ones, emask[:, 0, :], True, False)
                mm(ps[3][:, 2 * NE:3 * NE], ones, emask[:, 1, :], False, True).then_inc(rank_ready, 1)
                n += 1
                landed(n, gen0 + n // SLOTS)
                pe.wait_ge(pass_ready, l + 2)
                pe.wait_ge(hs_ready, l + 1)
                for tt in range(TT):
                    for half in range(2):
                        for ft in range(2):
                            m = mm(ACC[tt * 2 + half][:, :], hsT[:, ft, tt * P:tt * P + P],
                                   down_view(n % SLOTS, 0)[:, ft, half * 512:half * 512 + 512], ft == 0, False, skip_group_check=True)
                m.then_inc(ring_free[n % SLOTS], 1)
                apart(pe)
                end = pe.value_load(passi[0:1, 0:1], min_val=1, max_val=4 * DEPTH)

                with pe.Fori(base * ROUNDS, end * ROUNDS) as rnd:
                    genr = (l + 1) * GEN + rnd * (OCT // SLOTS)

                    def scatter(q, half):
                        if half == 0:
                            pe.wait_ge(swts_ready, rnd * 4 + q + 1)
                            pe.wait_ge(ya_ready, rnd * 4 + q + 1)
                        else:
                            pe.wait_ge(yd_ready, rnd * 4 + q + 1)
                        out_ = []
                        for tt in range(TT):
                            out_.append(mm(ACC[tt * 2 + half][:, :], swT[q % 2][:, tt * P:tt * P + P],
                                           ys[:, half * 512:half * 512 + 512], False, False, skip_group_check=True))
                        return out_

                    pe.wait_ge(sel_ready, rnd * TT + 2)
                    for t in range(KT):
                        if t >= 2:
                            pe.wait_ge((xg_act, xg_dve)[t % 2], rnd * 4 + t // 2)
                        for tt in range(TT):
                            m = mm((GB, HB)[t % 2][:, :], xs[:, tt, t:D:KT], sel[:, tt, :, :], tt == 0, tt == TT - 1)
                        m.then_inc(gth_ready, 1)
                    pe.wait_ge(xg_act, rnd * 4 + 4)
                    pe.wait_ge(xg_dve, rnd * 4 + 4)
                    for q in range(OCT // 2):
                        js = (2 * q, 2 * q + 1)
                        for j in js:
                            landed(j, genr + j // SLOTS)
                        for t in range(KT):
                            for e, j in enumerate(js):
                                m = mm(HB[64 * e:64 * e + 64, :], xg[:, t, j * CAP:j * CAP + CAP], gu_view(j % SLOTS)[:, :, t, :],
                                       t == 0, t == KT - 1, tile_position=(0, 64 * e))
                                if freed:
                                    free(m)
                        m.then_inc(gu_ready, 1)
                        if q:
                            scatter(q - 1, 0)
                        pe.wait_ge(h_ready, rnd * 4 + q + 1)
                        for ft in range(2):
                            m = nc.tensor.transpose(HB[:, ft * P:ft * P + P], hb[:, ft:FF:2], ident)
                        m.then_inc(ht_ready, 1)
                        if q == 0:
                            pe.wait_ge(selw_ready, rnd * TT + 2)
                        else:
                            pe.wait_ge(swts_ready, rnd * 4 + q)
                        for tt in range(TT):
                            m = nc.tensor.transpose(GB[:, tt * P:tt * P + P], selw[:, tt, 2 * q:2 * q + 2, :], ident)
                        m.then_inc(swt_ready, 1)
                        if q:
                            scatter(q - 1, 1)
                        pe.wait_ge(hts_ready, rnd * 4 + q + 1)
                        for half in range(2):
                            for ft in range(2):
                                for e, j in enumerate(js):
                                    m = mm(YB[half][64 * e:64 * e + 64, :], hT[:, ft * P + e * CAP:ft * P + e * CAP + CAP],
                                           down_view(j % SLOTS)[:, ft, half * 512:half * 512 + 512], ft == 0, ft == 1,
                                           tile_position=(0, 64 * e))
                                    if half and ft and e == 0:
                                        m.then_inc(ring_free[j % SLOTS], 1)
                            m.then_inc(yp_ready, 1)
                        freed.append(js[1] % SLOTS)
                    free(scatter(3, 0)[0])
                    scatter(3, 1)[1].then_inc(acc_ready, 1)

        @block.scalar
        def _(act):
            def apply(dst, src, func=ACT.Copy, **kw):
                return nc.scalar.activation(dst, src, func, **kw)

            act.wait_ge(c_in, 16)
            apply(csT[:, :], cT[:, :], ACT.Silu).then_inc(cs_ready, 1)
            with act.Fori(0, DEPTH) as l:
                act.wait_ge(pass_ready, l + 1)
                apart(act)
                base = act.value_load(passi[0:1, 0:1], min_val=0, max_val=4 * (DEPTH - 1))

                def modulate(which):
                    act.wait_ge(modc_ready, l * 2 + 2)
                    for b in (1, 3):
                        act.wait_ge(xt_ready, l * 8 + which * 4 + b + 1)
                        for t in (2 * b, 2 * b + 1):
                            apply(uT[:, t, :], ps[4 + b][:, t % 2 * S:t % 2 * S + S], ACT.Identity,
                                  scale=modc[:, 2 + which, t:t + 1], bias=modc[:, which, t:t + 1]).then_inc(u_act, 1)

                modulate(0)
                for half in range(2):
                    act.wait_ge(proj_ready, l * 12 + half + 1)
                    apply(qkT[:, 0, 2 * half:2 * half + 2, :], ps[half][:, :].rearrange("p (t n) -> p t n", t=2), scale=SCALE)\
                        .then_inc(qkv_act, 1)
                for half in range(2):
                    act.wait_ge(proj_ready, l * 12 + half + 3)
                    apply(qkT[:, 1, 2 * half:2 * half + 2, :], ps[2 + half][:, :].rearrange("p (t n) -> p t n", t=2))\
                        .then_inc(qkv_act, 1)
                for i in range(4):
                    act.wait_ge(proj_ready, l * 12 + 9 + i)
                    apply(vv[:, i // 2, i % 2, :], ps[i][:, :]).then_inc(qkv_act, 1)
                act.wait_ge(ffz_ready, l + 1)
                apply(zabs[:, :, :], zf[:, :, :], ACT.Abs).then_inc(act_step, 1)
                act.wait_ge(act_step, l * 2 + 1)
                apply(zexp[:, :, :], zabs[:, :, :], ACT.Exp, scale=-1.0).then_inc(act_step, 1)
                act.wait_ge(act_step, l * 2 + 2)
                apply(softp[:, :, :], zexp[:, :, :], ACT.Ln, bias=1.0).then_inc(softp_ready, 1)
                for b in range(4):
                    act.wait_ge(rt_ready, l * 4 + b + 1)
                    apply(qkT[:, 2 + b // 2, 2 * (b % 2):2 * (b % 2) + 2, :], ps[4 + b][:, :].rearrange("p (t n) -> p t n", t=2),
                          scale=SCALE if b < 2 else 1.0).then_inc(qkv_act, 1)
                act.wait_ge(pass_ready, l + 1)
                for h in range(2 * NH + 1):
                    if h < 2 * NH:
                        act.wait_ge(nm_ready, l * 16 + h + 1)
                        for tt in range(TT):
                            m = apply(pS[h % 2][:, part(tt)], sS[h % 2][:, part(tt)], ACT.Exp, bias=nmax[:, h % 2, tt:tt + 1],
                                      accum_out=lsum[:, h % 2, tt:tt + 1])
                        m.then_inc(exp_ready, 1)
                        act.wait_ge(gate_ready, l * 16 + h + 1)
                        apply(gatesT[:, h, :], ps[h % 2][:, 0:S], ACT.Identity, bias=bgate[:, h:h + 1]).then_inc(gates_raw, 1)
                    if h:
                        act.wait_ge(pt_ready, l * 16 + h)
                        apply(pT[(h - 1) % 2], ps[6 + (h - 1) % 2][:, 0:384]).then_inc(pts_ready, 1)
                act.wait_ge(gates_raw, l * 16 + 16)
                apply(gatesT, gatesT, ACT.Sigmoid).then_inc(gates_ready, 1)

                def norm_sqrt(which):
                    for tt in range(TT):
                        act.wait_ge(ve_ready, l * 4 + 2 * which + tt + 1)
                        apply(sd[:, tt:tt + 1], ve[:, tt:tt + 1], ACT.Sqrt).then_inc(sd_ready, 1)

                norm_sqrt(0)
                modulate(1)
                act.wait_ge(logits_ready, l + 1)
                apply(score[:, :, :], ps[0][:, 0:2 * NE].rearrange("p (t n) -> p t n", t=TT), ACT.Sigmoid)\
                    .then_inc(score_ready, 1)
                act.wait_ge(shgu_ready, l + 1)
                apply(shs, ps[1][:, :], ACT.Silu).then_inc(shs_ready, 1)

                act.wait_ge(pass_ready, l + 2)
                apart(act)
                end = act.value_load(passi[0:1, 0:1], min_val=1, max_val=4 * DEPTH)
                with act.Fori(base * ROUNDS, end * ROUNDS) as rnd:
                    for t in range(0, KT, 2):
                        act.wait_ge(gth_ready, rnd * KT + t + 1)
                        apply(xg[:, t, :], GB[:, :], ACT.Identity, scale=modc[:, 3, t:t + 1], bias=modc[:, 1, t:t + 1])\
                            .then_inc(xg_act, 1)
                    for q in range(OCT // 2):
                        act.wait_ge(gu_ready, rnd * 4 + q + 1)
                        apply(sg, HB[:, 0:FF], ACT.Silu).then_inc(sg_ready, 1)
                        act.wait_ge(swt_ready, rnd * 4 + q + 1)
                        apply(swT[q % 2], GB[:, 0:S]).then_inc(swts_ready, 1)
                        act.wait_ge(yp_ready, rnd * 8 + 2 * q + 1)
                        apply(ys[:, 0:512], YB[0][:, :]).then_inc(ya_ready, 1)
                norm_sqrt(1)

        @block.vector
        def _(dve):
            V = nc.vector

            V.memset(passf[:, :], 0.0).then_inc(dve_step, 1)
            dve.wait_ge(dve_step, 1)
            V.tensor_copy(passi[:, :], passf[:, :]).then_inc(pass_ready, 1)
            dve.wait_ge(cs_ready, 1)
            V.tensor_copy(csrep[:, :, :], csT[:, :].unsqueeze(2).to_broadcast([P, KT, 32])).then_inc(csrep_ready, 1)
            dve.wait_ge(const_in, 16)
            dve.wait_ge(x_in, 16)
            with dve.Fori(0, DEPTH) as l:
                dve.wait_ge(pass_ready, l + 1)
                apart(dve)
                base = dve.value_load(passi[0:1, 0:1], min_val=0, max_val=4 * (DEPTH - 1))
                steps = [0]

                def step(ins):
                    steps[0] += 1
                    ins.then_inc(dve_step, 1)
                    dve.wait_ge(dve_step, l * DVE_STEPS + steps[0] + 1)

                dve.wait_ge(bias_in, l * 16 + 16)
                for k in range(2 * ADA_CHUNKS):
                    dve.wait_ge(ada_ready, l * 16 + k + 1)
                    to = mod_parts[:, k * ADA_W // 2:(k + 1) * ADA_W // 2]
                    V.tensor_tensor(to, ps[k % 4][:, 0:ADA_W // 2], to, ALU.add).then_inc(parts_ready, 1)
                dve.wait_ge(modcol_ready, l + 1)
                V.tensor_copy(modc[:, 0:2, :], ps[3][:, 0:2 * KT].rearrange("p (a t) -> p a t", a=2)).then_inc(modc_ready, 1)
                V.tensor_scalar(modc[:, 2:4, :], ps[3][:, 2 * KT:4 * KT].rearrange("p (a t) -> p a t", a=2), 1.0, None, ALU.add)\
                    .then_inc(modc_ready, 1)
                for i in range(4):
                    dve.wait_ge(grow_ready, l * 4 + i + 1)
                    V.tensor_scalar(gate1p[:, i // 2, i % 2 * 512:i % 2 * 512 + 512], ps[i][:, :], 1.0, None, ALU.add)\
                        .then_inc(gate_ready1p, 1)

                def modulate(which):
                    dve.wait_ge(modc_ready, l * 2 + 2)
                    for b in (0, 2):
                        dve.wait_ge(xt_ready, l * 8 + which * 4 + b + 1)
                        for t in (2 * b, 2 * b + 1):
                            V.tensor_scalar(uT[:, t, :], ps[4 + b][:, t % 2 * S:t % 2 * S + S], modc[:, 2 + which, t:t + 1],
                                            modc[:, which, t:t + 1], ALU.mult, ALU.add).then_inc(u_dve, 1)

                modulate(0)
                for a in range(2):
                    for tt in range(TT):
                        dve.wait_ge(proj_ready, l * 12 + (2 + a) * 2 + tt + 1)
                        w = ps[2 * (2 + a) + tt][:, :].rearrange("p (h c j) -> p h c j", c=2, j=HD // 2)
                        o = rot[:, a, tt, :].rearrange("p (h c j) -> p h c j", c=2, j=HD // 2)
                        cos, sin = (cst[:, C_ROPE + tt * HD + i * 32:C_ROPE + tt * HD + i * 32 + 32].unsqueeze(1)
                                    .to_broadcast([P, NH, HD // 2]) for i in range(2))
                        tmp = [rope_tmp[:, i, :].rearrange("p (h j) -> p h j", h=NH) for i in range(4)]
                        if a or tt:
                            dve.wait_ge(rot_ready, l * 4 + 2 * a + tt)
                        V.tensor_tensor(tmp[0], w[:, :, 0, :], cos, ALU.mult)
                        V.tensor_tensor(tmp[1], w[:, :, 1, :], sin, ALU.mult)
                        V.tensor_tensor(tmp[2], w[:, :, 1, :], cos, ALU.mult)
                        step(V.tensor_tensor(tmp[3], w[:, :, 0, :], sin, ALU.mult))
                        V.tensor_tensor(o[:, :, 0, :], tmp[0], tmp[1], ALU.subtract)
                        V.tensor_tensor(o[:, :, 1, :], tmp[2], tmp[3], ALU.add).then_inc(rot_ready, 1)
                dve.wait_ge(ff_ready, l + 1)
                dve.wait_ge(params_in, l * 80 + 80)
                V.tensor_tensor(zf[:, :, :], ps[0][:, 0:TT * NH].rearrange("p (t h) -> p t h", t=TT),
                                bforget[:, :].unsqueeze(1).to_broadcast([P, TT, NH]), ALU.add).then_inc(ffz_ready, 1)
                dve.wait_ge(ffz_ready, l + 1)
                step(V.tensor_scalar(zneg[:, :, :], zf[:, :, :], -1.0, 0.0, ALU.mult, ALU.max))
                dve.wait_ge(softp_ready, l + 1)
                V.tensor_tensor(nlogf[:, :, :], zneg[:, :, :], softp[:, :, :], ALU.add).then_inc(nlogf_ready, 1)
                dve.wait_ge(cum_ready, l + 1)
                V.tensor_copy(ncum[:, :, :], ps[1][:, 0:TT * NH].rearrange("p (t h) -> p t h", t=TT)).then_inc(cumc_ready, 1)
                V.tensor_copy(ncumT[:, :], ps[1][0:NH, P:3 * P]).then_inc(cumc_ready, 1)
                dve.wait_ge(cumc_ready, l * 2 + 2)

                def biased_max(h):
                    kind, hh = divmod(h, NH)
                    dve.wait_ge(s_ready, l * 16 + h + 1)
                    for tt in range(TT):
                        dst, src = sS[h % 2][:, part(tt)], ps[4 + h % 2][:, part(tt)]
                        if kind == 0:
                            m = V.scalar_tensor_tensor(dst, src, ncum[:, tt, hh:hh + 1], mask(0, tt), ALU.subtract, ALU.add)
                        else:
                            m = V.tensor_tensor(dst, src, mask(1, tt), ALU.add)
                    step(m)
                    for tt in range(TT):
                        m = V.tensor_reduce(nmax[:, h % 2, tt:tt + 1], sS[h % 2][:, part(tt)], AX, ALU.max, negate=True)
                    m.then_inc(nm_ready, 1)

                def normalise(h):
                    dve.wait_ge(exp_ready, l * 16 + h + 1)
                    step(V.reciprocal(rsum[:, h % 2, :], lsum[:, h % 2, :]))
                    for tt in range(TT):
                        m = V.tensor_scalar(pS[h % 2][:, part(tt)], pS[h % 2][:, part(tt)], rsum[:, h % 2, tt:tt + 1], None, ALU.mult)
                    m.then_inc(p_ready, 1)

                for h in range(2 * NH + 2):
                    if h < 2 * NH:
                        biased_max(h)
                    if 1 <= h <= 2 * NH:
                        normalise(h - 1)
                    if h >= 3 and h % 2:
                        n = (h - 3) // 2
                        dve.wait_ge(pv_ready, l * 8 + n + 1)
                        V.tensor_copy(yT[:, n // BT, n % BT, :], ps[2 + n % 2][:, 0:S]).then_inc(y_ready, 1)
                dve.wait_ge(gates_ready, l + 1)
                for j in range(KT):
                    dve.wait_ge(br_ready, l * 8 + j + 1)
                    a, b = merge_tmp[:, 2 * (j % 2), :], merge_tmp[:, 2 * (j % 2) + 1, :]
                    if j >= 2:
                        dve.wait_ge(merged_ready, l * 8 + j - 1)
                    V.tensor_tensor(a, ps[j % 4][:, 0:S], gatesT[:, j, :], ALU.mult)
                    step(V.tensor_tensor(b, ps[j % 4][:, S:2 * S], gatesT[:, KT + j, :], ALU.mult))
                    V.tensor_tensor(mergedT[:, j, :], a, b, ALU.add).then_inc(merged_ready, 1)

                def norm(which, banks, ready):
                    for tt in range(TT):
                        ready(tt)
                        for half in range(2):
                            a = slice(half * 512, half * 512 + 512)
                            m = V.tensor_tensor(z[:, tt, a], banks(tt, half)[:, :], gate1p[:, which, a], ALU.mult)
                        step(m)
                        step(V.scalar_tensor_tensor(z[:, tt, :], xs[:, tt, :], ALPHA, z[:, tt, :], ALU.mult, ALU.add))
                        for half in range(2):
                            m = V.bn_stats(bst[:, tt, half, :], z[:, tt, half * 512:half * 512 + 512])
                        step(m)
                        apart(dve)
                        step(V.bn_aggr(mv[:, tt, :], bst[:, tt, :, :].rearrange("p a b -> p (a b)")))
                        V.tensor_scalar(ve[:, tt:tt + 1], mv[:, tt, 1:2], LN_EPS, None, ALU.add).then_inc(ve_ready, 1)
                    for tt in range(TT):
                        dve.wait_ge(sd_ready, l * 4 + 2 * which + tt + 1)
                        step(V.reciprocal(rstd[:, tt:tt + 1], sd[:, tt:tt + 1]))
                        V.tensor_scalar(xs[:, tt, :], z[:, tt, :], mv[:, tt, 0:1], rstd[:, tt:tt + 1], ALU.subtract, ALU.mult)\
                            .then_inc(xn_ready, 1)

                norm(0, lambda tt, half: ps[4 + 2 * half + tt], lambda tt: dve.wait_ge(wo_ready, l * 4 + 3 + tt))
                modulate(1)

                dve.wait_ge(score_ready, l + 1)
                step(V.tensor_tensor(choice[:, :, :], score[:, :, :], rbias[:, :].unsqueeze(1).to_broadcast([P, TT, NE]), ALU.add))
                apart(dve)
                for tt in range(TT):
                    for g in range(NG):
                        m = V.max(gmax[:, tt, g, :], choice[:, tt, g * 8:g * 8 + 8])
                step(m)
                step(V.tensor_tensor(gsc[:, :, :], gmax[:, :, :, 0], gmax[:, :, :, 1], ALU.add))
                other = gsc[:, :, :].unsqueeze(2).to_broadcast([P, TT, NG, NG])
                own = gsc[:, :, :].unsqueeze(3).to_broadcast([P, TT, NG, NG])
                V.tensor_tensor(gcmp[:, :, :, :], other, own, ALU.is_gt)
                step(V.tensor_tensor(geq[:, :, :, :], other, own, ALU.is_equal))
                lower = cst[:, C_LT8:C_LT8 + NG * NG].rearrange("p (a b) -> p a b", a=NG).unsqueeze(1).to_broadcast([P, TT, NG, NG])
                step(V.tensor_tensor(geq[:, :, :, :], geq[:, :, :, :], lower, ALU.mult))
                step(V.tensor_tensor(gcmp[:, :, :, :], gcmp[:, :, :, :], geq[:, :, :, :], ALU.add))
                step(V.tensor_reduce(grank[:, :, :], gcmp[:, :, :, :], AX, ALU.add))
                step(V.tensor_scalar(gmask[:, :, :], grank[:, :, :], 4.0, None, ALU.is_lt))
                V.tensor_scalar(gpen[:, :, :], gmask[:, :, :], 1.0, -NEG, ALU.subtract, ALU.mult)
                grouped = choice[:, :, :].rearrange("p t (g e) -> p (t g) e", g=NG)
                flat = gmask[:, :, :].rearrange("p t g -> p (t g)").unsqueeze(2).to_broadcast([P, TT * NG, 8])
                step(V.tensor_tensor(grouped, grouped, flat, ALU.mult))
                pen = gpen[:, :, :].rearrange("p t g -> p (t g)").unsqueeze(2).to_broadcast([P, TT * NG, 8])
                step(V.tensor_tensor(grouped, grouped, pen, ALU.add))
                apart(dve)
                for tt in range(TT):
                    m = V.max(top8[:, tt, :], choice[:, tt, :])
                step(m)
                for tt in range(TT):
                    eighth = top8[:, tt, 7:8]
                    V.tensor_scalar(above[:, tt, :], choice[:, tt, :], eighth, None, ALU.is_gt)
                    m = V.tensor_scalar(ties[:, tt, :], choice[:, tt, :], eighth, None, ALU.is_equal)
                step(m)
                step(V.tensor_reduce(nabove[:, :], above[:, :, :], AX, ALU.add))
                step(V.tensor_scalar(nabove[:, :], nabove[:, :], -1.0, float(TOPK), ALU.mult, ALU.add))
                for tt in range(TT):
                    m = V.tensor_tensor_scan(tiesum[:, tt, :], ties[:, tt, :], cst[:, C_ZERO:C_ZERO + NE], 0.0, ALU.add, ALU.add)
                step(m)
                for tt in range(TT):
                    m = V.scalar_tensor_tensor(ties[:, tt, :], tiesum[:, tt, :], nabove[:, tt:tt + 1], ties[:, tt, :],
                                               ALU.is_le, ALU.mult)
                step(m)
                for tt in range(TT):
                    V.tensor_tensor(emask[:, tt, :], above[:, tt, :], ties[:, tt, :], ALU.add).then_inc(emask_ready, 1)
                dve.wait_ge(shs_ready, l + 1)
                V.tensor_tensor(hsT, shs.rearrange("p (t n) -> p t n", t=2), ps[2][:, :].rearrange("p (t n) -> p t n", t=2),
                                ALU.mult).then_inc(hs_ready, 1)
                dve.wait_ge(emask_ready, l * 2 + 2)
                for tt in range(TT):
                    m = V.scalar_tensor_tensor(wraw[:, tt, :], score[:, tt, :], 1.0, emask[:, tt, :], ALU.mult, ALU.mult,
                                               accum_out=wsum[:, tt:tt + 1])
                step(m)
                step(V.reciprocal(wrec[:, :], wsum[:, :]))
                for tt in range(TT):
                    m = V.tensor_scalar(wtok[:, tt, :], wraw[:, tt, :], wrec[:, tt:tt + 1], ROUTED_SCALE, ALU.mult, ALU.mult)
                m.then_inc(wtok_ready, 1)
                dve.wait_ge(rank_ready, l + 1)
                step(V.scalar_tensor_tensor(erank[:, :, :], ps[3][:, 0:2 * NE].rearrange("p (t e) -> p t e", t=TT), 1.0,
                                            emask[:, :, :], ALU.add, ALU.mult))
                step(V.tensor_scalar(erank[:, :, :], erank[:, :, :], 1.0, None, ALU.subtract))
                step(V.tensor_reduce(mostf[:, :], ps[3][:, 2 * NE:3 * NE], AX, ALU.max))
                step(V.tensor_tensor(overf[:, :], mostf[:, :].to_broadcast([P, N_THR]), cst[:, C_THR:C_END], ALU.is_gt))
                step(V.tensor_reduce(morep[:, :], overf[:, :], AX, ALU.add))
                step(V.scalar_tensor_tensor(passf[:, :], morep[:, :], 1.0, passf[:, :], ALU.add, ALU.add))
                V.tensor_copy(slotno[:, :], cst[:, C_IOTA:C_IOTA + CAP]).then_inc(iota_ready, 1)
                V.tensor_copy(passi[:, :], passf[:, :]).then_inc(pass_ready, 1)

                dve.wait_ge(pass_ready, l + 2)
                apart(dve)
                end = dve.value_load(passi[0:1, 0:1], min_val=1, max_val=4 * DEPTH)
                with dve.Fori(base, end) as pss:
                    dve.wait_ge(iota_ready, l + 1 + pss)
                    apart(dve)
                    with dve.Fori(0, ROUNDS) as o:
                        rnd = pss * ROUNDS + o
                        for tt in range(TT):
                            V.tensor_tensor(sel[:, tt, :, :],
                                            erank[:, tt, bass.ds(o * OCT, OCT)].unsqueeze(2).to_broadcast([P, OCT, CAP]),
                                            slotno[:, :].unsqueeze(1).to_broadcast([P, OCT, CAP]), ALU.is_equal)\
                                .then_inc(sel_ready, 1)
                        for t in range(1, KT, 2):
                            dve.wait_ge(gth_ready, rnd * KT + t + 1)
                            V.tensor_scalar(xg[:, t, :], HB[:, :], modc[:, 3, t:t + 1], modc[:, 1, t:t + 1], ALU.mult, ALU.add)\
                                .then_inc(xg_dve, 1)
                        for q in range(OCT // 2):
                            dve.wait_ge(sg_ready, rnd * 4 + q + 1)
                            V.tensor_tensor(hb, sg, HB[:, FF:2 * FF], ALU.mult).then_inc(h_ready, 1)
                            dve.wait_ge(ht_ready, rnd * 4 + q + 1)
                            V.tensor_copy(hT, HB[:, 0:FF]).then_inc(hts_ready, 1)
                            dve.wait_ge(yp_ready, rnd * 8 + 2 * q + 2)
                            V.tensor_copy(ys[:, 512:D], YB[1][:, :]).then_inc(yd_ready, 1)
                    V.tensor_scalar(slotno[:, :], slotno[:, :], float(CAP), None, ALU.add).then_inc(iota_ready, 1)

                norm(1, lambda tt, half: ACC[tt * 2 + half], lambda tt: dve.wait_ge(acc_ready, end * ROUNDS))
                assert steps[0] == DVE_STEPS, steps


INPUTS = ("x", "c", "w_ada", "b_ada", "w_in", "b_forget", "b_gate", "w_br_fox", "w_br_dil", "w_o", "ln_g", "ln_b", "w_router",
          "router_bias", "w_exp_gate", "w_exp_up", "w_exp_down", "w_sh_gate", "w_sh_up", "w_sh_down")


def kernel(**inputs):
    import concourse.bacc as bacc
    from concourse.bass_utils import run_bass_kernel_spmd

    nc = bacc.Bacc("TRN2", target_bir_lowering=False, num_devices=1)
    arrays = {f"in_{name}": np.ascontiguousarray(inputs[name]) for name in INPUTS}
    arrays["in_constants"] = constants()
    args = [nc.dram_tensor(n, a.shape, mybir.dt.from_np(a.dtype), kind="ExternalInput").ap() for n, a in arrays.items()]
    args.append(nc.dram_tensor("out_x", (1, S, D), F32, kind="ExternalOutput").ap())
    decoder(nc, *args)
    return run_bass_kernel_spmd(nc, [arrays], core_ids=[0]).results[0]["out_x"]
```

```python
from contextlib import ExitStack

import numpy as np

import concourse.bass as bass
from concourse import mybir

P = 128
D = 1024
S = 256
DEPTH = 2
TT = S // P
KT = D // P
HD = 64
NH = 8
BW = NH * HD
BT = BW // P
NE = 64
TOPK = 8
NG = 8
FF = 256
CAP = 64
OCT = 8
ROUNDS = NE // OCT
SLOTS = 12
PIECE = KT * FF
PAIR_PIECES = 6
PER_ROUND = OCT // 2 * PAIR_PIECES // SLOTS
STATIC_LOADS = 28
STATIC_AT = -2 * STATIC_LOADS % SLOTS
INPUT_AT = (0, 3, 6, 9, 12, 13)
GATES_AT = 14
ADA_AT = (1, 4, 7, 10, 18, 20)
BRANCH_AT, WO_AT, SHARED_AT = 22, 24, 26
ADA_VECTORS = (2, 3, 4, 5, 0, 1)
AHEAD = 2
ALPHA = float((2 * DEPTH) ** 0.25)
SCALE = HD ** -0.5
ROUTED_SCALE = 2.5
LN_EPS = 1e-5
NEG = -1e30


def slot_of(n):
    return (STATIC_AT + 2 * n) % SLOTS


LOADS_AHEAD = [int((s - STATIC_AT) % SLOTS >= SLOTS - 4 * AHEAD) for s in range(SLOTS)]
LOADS_STATIC = [len(range((s - STATIC_AT) % SLOTS, 2 * STATIC_LOADS - 1, SLOTS)) for s in range(SLOTS)]


def static_gen(slot, n, l, rounds):
    return LOADS_AHEAD[slot] + l * LOADS_STATIC[slot] + rounds * PER_ROUND + 2 * n // SLOTS


def expert_gen(slot, q, l, rnd):
    return LOADS_AHEAD[slot] + (l + 1) * LOADS_STATIC[slot] + rnd * PER_ROUND + q // 2


DVE_STEPS = 98
FF_COL = 3 * BW

F32 = mybir.dt.float32
BF16 = mybir.dt.bfloat16
I32 = mybir.dt.int32
ALU = mybir.AluOpType
ACT = mybir.ActivationFunctionType
AX = mybir.AxisListType.X

C_ROPE = 0
C_MASK = C_ROPE + TT * 64
C_TRI = C_MASK + 2 * 384
C_ONES = C_TRI + P
C_TRIS = C_ONES + P
C_ID = C_TRIS + P
C_IOTA = C_ID + P
C_LT8 = C_IOTA + 5 * CAP
C_QUAD = C_LT8 + NG * NG
C_ZERO = C_QUAD + P
C_THR = C_ZERO + NE
N_THR = -(-S // CAP) - 1
C_END = C_THR + N_THR


def constants():
    t = np.zeros((P, C_END), np.float32)
    half = HD // 2
    freq = (np.float32(10000.0) ** (-np.arange(half, dtype=np.float32) * np.float32(2.0) / np.float32(HD))).astype(np.float32)
    ang = (np.arange(S, dtype=np.float32)[:, None] * freq[None, :]).astype(np.float32)
    rope = np.stack([np.cos(ang), np.sin(ang)], axis=1).astype(np.float32)
    t[:, C_ROPE:C_MASK] = rope.reshape(TT, P, 64).transpose(1, 0, 2).reshape(P, -1)
    q = np.arange(S)[:, None]
    k = np.arange(S)[None, :]
    causal = q >= k
    fox = np.where(causal, 0.0, NEG)
    often = np.zeros((S, S))
    for window, dil in ((128, 1), (512, 4), (2048, 16)):
        often += causal & ((q - k) % dil == 0) & ((q - k) // dil <= window // dil)
    dilated = np.where(often > 0, np.log(np.maximum(often, 1.0)), NEG)
    for n, m in enumerate((fox, dilated)):
        t[:, C_MASK + 384 * n:C_MASK + 384 * n + P] = m[:P, :P]
        t[:, C_MASK + 384 * n + P:C_MASK + 384 * n + 384] = m[P:, :]
    r = np.arange(P)
    t[:, C_TRI:C_TRI + P] = r[:, None] <= r[None, :]
    t[:, C_ONES:C_ONES + P] = 1.0
    t[:, C_TRIS:C_TRIS + P] = r[:, None] < r[None, :]
    t[:, C_ID:C_ID + P] = np.eye(P)
    t[:, C_IOTA:C_IOTA + 5 * CAP] = np.arange(5 * CAP)
    t[:, C_LT8:C_LT8 + NG * NG] = (np.arange(NG)[None, :] < np.arange(NG)[:, None]).reshape(-1)
    t[::32, C_QUAD:C_QUAD + P] = 1.0
    t[:, C_THR:C_END] = CAP * np.arange(1, N_THR + 1)
    return t


def decoder(nc, x, c, w_ada, b_ada, w_in, b_forget, b_gate, w_br_fox, w_br_dil, w_o, ln_g, ln_b, w_router,
            router_bias, w_exp_gate, w_exp_up, w_exp_down, w_sh_gate, w_sh_up, w_sh_down, consts, out):
    with ExitStack() as ctx:
        def sb(name, shape, dt=F32):
            return ctx.enter_context(nc.sbuf_tensor(name, shape, dt))

        def sem(name):
            return ctx.enter_context(nc.semaphore(name))

        ring = sb("ring", [P, SLOTS * PIECE])
        cst = sb("cst", [P, C_END])
        xs = sb("xs", [P, TT, D])
        uz = sb("uz", [P, TT * D])
        uT = uz[:, :].rearrange("p (t n) -> p t n", t=KT)
        z = uz[:, :].rearrange("p (t n) -> p t n", t=TT)
        gate1p = sb("gate1p", [P, 2, D])
        lnp = sb("lnp", [P, 2, D])
        parts = [sb(f"parts{i}", [P, D]) for i in range(2)]
        wide = sb("wide", [P, 6 * D])
        gatesT = wide[:, 0:2 * KT * S].rearrange("p (g n) -> p g n", n=S)
        yT = wide[:, 2 * KT * S:].rearrange("p (b t n) -> p b t n", b=2, t=BT)
        xp = wide[:, 0:3 * D].bitcast(BF16).rearrange("p (i t n) -> p i t n", i=3, t=TT)
        xrest = wide[:, 3 * D:5 * D].rearrange("p (t n) -> p t n", t=TT)
        yp = wide[:, 3 * D:3 * D + 3 * D // 2].bitcast(BF16).rearrange("p (i n) -> p i n", i=3)
        yrest = wide[:, 5 * D:6 * D]
        mid = sb("mid", [P, 6 * D])
        qkT = mid[:, 0:4 * D].rearrange("p (a t n) -> p a t n", a=4, t=BT)
        vv = mid[:, 4 * D:6 * D].rearrange("p (a t n) -> p a t n", a=2, t=TT)
        xg = [mid[:, D * i:D * i + D].rearrange("p (t n) -> p t n", t=KT) for i in range(2)]
        sel = mid[:, 4 * D:4 * D + D // 2].bitcast(BF16).rearrange("p (t e s) -> p t e s", t=TT, e=OCT)
        shs = mid[:, 0:512]
        hsT = mid[:, 512:1024].rearrange("p (t n) -> p t n", t=2)
        small = sb("small", [P, 9 * 256])
        sS = [small[:, 384 * i:384 * i + 384] for i in range(2)]
        pS = [small[:, 768 + 384 * i:768 + 384 * i + 384] for i in range(2)]
        pT = [small[:, 1536 + 384 * i:1536 + 384 * i + 384] for i in range(2)]
        sg = small[:, 0:256]
        hb = small[:, 256:512]
        hT = small[:, 512:768]
        selT = [small[:, 768 + 128 * i:896 + 128 * i].bitcast(BF16) for i in range(2)]
        rot = wide[:, 0:2 * D].rearrange("p (a t n) -> p a t n", a=2, t=TT)
        mergedT = mid[:, 0:2 * D].rearrange("p (t n) -> p t n", t=KT)
        rope_tmp = wide[:, 5 * D:].rearrange("p (i n) -> p i n", i=4)
        merge_tmp = small[:, 0:D].rearrange("p (i n) -> p i n", i=4)
        cT = sb("cT", [P, KT])
        csT = sb("csT", [P, KT])
        csrep = sb("csrep", [P, KT, 32])
        modc = sb("modc", [P, 4, KT])
        wff = sb("wff", [P, KT, NH])
        bgate = sb("bgate", [P, 2 * KT])
        bforget = sb("bforget", [P, NH])
        wrt = sb("wrt", [P, KT, NE])
        rbias = sb("rbias", [P, NE])
        zf = sb("zf", [P, TT, NH])
        zabs = sb("zabs", [P, TT, NH])
        zexp = sb("zexp", [P, TT, NH])
        softp = sb("softp", [P, TT, NH])
        zneg = sb("zneg", [P, TT, NH])
        nlogf = sb("nlogf", [P, TT, NH])
        ncum = sb("ncum", [P, TT, NH])
        ncumT = sb("ncumT", [NH, S])
        nmax = sb("nmax", [P, 2, TT])
        lsum = sb("lsum", [P, 2, TT])
        rsum = sb("rsum", [P, 2, TT])
        bst = sb("bst", [P, TT, 2, 6])
        mv = sb("mv", [P, TT, 2])
        ve = sb("ve", [P, TT])
        sd = sb("sd", [P, TT])
        rstd = sb("rstd", [P, TT])
        score = mid[:, 1024:1152].rearrange("p (t e) -> p t e", t=TT)
        choice = mid[:, 1152:1280].rearrange("p (t e) -> p t e", t=TT)
        gmax = mid[:, 2176:2304].rearrange("p (t g i) -> p t g i", t=TT, g=NG)
        gsc = sb("gsc", [P, TT, NG])
        gcmp = mid[:, 2304:2432].rearrange("p (t g i) -> p t g i", t=TT, g=NG)
        geq = mid[:, 2432:2560].rearrange("p (t g i) -> p t g i", t=TT, g=NG)
        grank = sb("grank", [P, TT, NG])
        gmask = sb("gmask", [P, TT, NG])
        gpen = sb("gpen", [P, TT, NG])
        top8 = sb("top8", [P, TT, 8])
        above = mid[:, 1280:1408].rearrange("p (t e) -> p t e", t=TT)
        nabove = sb("nabove", [P, TT])
        ties = mid[:, 1408:1536].rearrange("p (t e) -> p t e", t=TT)
        tiesum = mid[:, 1536:1664].rearrange("p (t e) -> p t e", t=TT)
        emask = mid[:, 1664:1792].rearrange("p (t e) -> p t e", t=TT)
        wraw = mid[:, 1792:1920].rearrange("p (t e) -> p t e", t=TT)
        wsum = sb("wsum", [P, TT])
        wrec = sb("wrec", [P, TT])
        wtok = mid[:, 1920:2048].rearrange("p (t e) -> p t e", t=TT)
        erank = mid[:, 4 * D + 704:4 * D + 832].rearrange("p (t e) -> p t e", t=TT)
        mostf = sb("mostf", [P, 1])
        overf = sb("overf", [P, N_THR])
        morep = sb("morep", [P, 1])
        passf = sb("passf", [P, 1])
        passi = sb("passi", [P, 1], I32)
        wp = mid[:, 4 * D + 512:4 * D + 704].bitcast(BF16).rearrange("p (i t e) -> p i t e", i=3, t=TT)
        wslot = sb("wslot", [P, OCT // 2])
        identb = sb("identb", [P, P], BF16)

        ps = [ctx.enter_context(nc.psum_tensor(f"ps{i}", [P, 512], F32)) for i in range(8)]
        ACC = ps[0:4]
        HB, GB, YB = ps[4], ps[5], ps[6:8]
        HB16 = HB[:, FF:FF + P].bitcast(BF16)

        ident = cst[:, C_ID:C_ID + P]
        tri = cst[:, C_TRI:C_TRI + P]
        tri_ones = cst[:, C_TRI:C_TRI + 2 * P]
        tri_strict = cst[:, C_TRIS:C_TRIS + P]
        ones = cst[:, C_ONES:C_ONES + P]
        quad = cst[:, C_QUAD:C_QUAD + P]

        def mask(kind, tt):
            a = C_MASK + 384 * kind
            return cst[:, a:a + P] if tt == 0 else cst[:, a + P:a + 384]

        def part(tt):
            return slice(0, P) if tt == 0 else slice(P, 384)

        def static_view(n, tiles):
            at = slot_of(n) * PIECE
            return ring[:, at:at + 2 * PIECE].rearrange("p (t n) -> p t n", t=tiles)

        def gu_view(slot):
            return ring[:, slot * PIECE:(slot + 2) * PIECE].rearrange("p (g t f) -> p g t f", g=2, t=KT)

        def down_view(slot):
            return ring[:, slot * PIECE:(slot + 1) * PIECE].rearrange("p (t n) -> p t n", t=2)

        def gu_slots(q):
            return [PAIR_PIECES * (q % 2) + i for i in range(4)]

        def down_slots(q):
            return [PAIR_PIECES * (q % 2) + 4 + e for e in range(2)]

        const_in, x_in, c_in = sem("const_in"), sem("x_in"), sem("c_in")
        params_in, ln_in = sem("params_in"), sem("ln_in")
        bias_in = [sem(f"bias_in{i}") for i in range(2)]
        ring_full = [sem(f"ring_full{i}") for i in range(SLOTS)]
        ring_free = [sem(f"ring_free{i}") for i in range(SLOTS)]
        out_done = sem("out_done")
        cs_ready, csrep_ready = sem("cs_ready"), sem("csrep_ready")
        zero_parts, ada_ready, parts_ready = sem("zero_parts"), sem("ada_ready"), sem("parts_ready")
        red_ready, red_used = sem("red_ready"), sem("red_used")
        xt_ready, u_dve, u_act = sem("xt_ready"), sem("u_dve"), sem("u_act")
        proj_ready, qkv_act, rot_ready = sem("proj_ready"), sem("qkv_act"), sem("rot_ready")
        rt_ready = sem("rt_ready")
        ff_ready, ffz_ready, softp_ready = sem("ff_ready"), sem("ffz_ready"), sem("softp_ready")
        nlogf_ready, cum_ready, cumc_ready = sem("nlogf_ready"), sem("cum_ready"), sem("cumc_ready")
        s_ready, nm_ready, exp_ready = sem("s_ready"), sem("nm_ready"), sem("exp_ready")
        p_ready, pt_ready, pts_ready = sem("p_ready"), sem("pt_ready"), sem("pts_ready")
        pv_ready, y_ready = sem("pv_ready"), sem("y_ready")
        gate_ready, gates_raw, gates_ready = sem("gate_ready"), sem("gates_raw"), sem("gates_ready")
        br_ready, merged_ready, wo_ready = sem("br_ready"), sem("merged_ready"), sem("wo_ready")
        ve_ready, sd_ready, x_ready = sem("ve_ready"), sem("sd_ready"), sem("x_ready")
        xp0_ready, xr_ready, xp1_ready, xp2_ready = sem("xp0_ready"), sem("xr_ready"), sem("xp1_ready"), sem("xp2_ready")
        logits_ready, score_ready, shgu_ready = sem("logits_ready"), sem("score_ready"), sem("shgu_ready")
        shs_ready, hs_ready, emask_ready = sem("shs_ready"), sem("hs_ready"), sem("emask_ready")
        rank_ready, pass_ready = sem("rank_ready"), sem("pass_ready")
        sel_ready, zeroed = sem("sel_ready"), sem("zeroed")
        gth0_ready, gth1_ready, xg_act, xg_dve = sem("gth0_ready"), sem("gth1_ready"), sem("xg_act"), sem("xg_dve")
        gu_ready, sg_ready, h_ready = sem("gu_ready"), sem("sg_ready"), sem("h_ready")
        ht_ready, hts_ready = sem("ht_ready"), sem("hts_ready")
        sts_ready, yb_ready, y0_ready = sem("sts_ready"), sem("yb_ready"), sem("y0_ready")
        yr_ready, y1_ready, y2_ready, acc_ready = sem("yr_ready"), sem("y1_ready"), sem("y2_ready"), sem("acc_ready")
        dve_step, act_step = sem("dve_step"), sem("act_step")
        gone_by = sem("gone_by")


        def apart(eng):
            eng.sem_inc(gone_by, 1)

        block = ctx.enter_context(nc.Block())

        @block.sync
        def _(sp):
            sp.dma_start(cst[:, :], consts).then_inc(const_in, 16)
            sp.dma_start(cT[:, :], c.rearrange("o (p t) -> p (o t)", t=KT)).then_inc(c_in, 16)
            sp.dma_start(xs[:, :, :], x[0].rearrange("(t p) d -> p t d", p=P)).then_inc(x_in, 16)

            ada = w_ada.rearrange("l (p t) n -> l p t n", t=KT)
            win = w_in.rearrange("l (p t) n -> l p t n", t=KT)
            wbr = [w.rearrange("l (t p) n -> l p t n", p=P) for w in (w_br_fox, w_br_dil)]
            wo = w_o.rearrange("l (t p) n -> l p t n", p=P)
            sh_g, sh_u = (w.rearrange("l (p t) f -> l p t f", t=KT) for w in (w_sh_gate, w_sh_up))
            sh_d = w_sh_down.rearrange("l (p t) n -> l p t n", t=2)
            ex_g, ex_u = (w.rearrange("l (o e) (p t) f -> l o e p t f", e=OCT, t=KT) for w in (w_exp_gate, w_exp_up))
            ex_d = w_exp_down.rearrange("l (o e) (p t) n -> l o e p t n", e=OCT, t=2)

            def load(slot, gen, src, rows):
                sp.wait_ge(ring_free[slot], gen + 1)
                dst = ring[:, slot * PIECE:(slot + 1) * PIECE].rearrange("p (t n) -> p t n", t=rows)
                sp.dma_start(dst, src).then_inc(ring_full[slot], 16)

            for v in (0, 1):
                for half in range(2):
                    slot = slot_of(2 * v + half - 2 * AHEAD)
                    for i in range(2):
                        load(slot + i, 0, ada[0][:, 4 * i:4 * i + 4, v * D + half * 512:v * D + half * 512 + 512], 4)

            with sp.Fori(0, DEPTH) as l:
                sp.wait_ge(pass_ready, l + 1)
                apart(sp)
                base = sp.value_load(passi[0:1, 0:1], min_val=0, max_val=4 * (DEPTH - 1))

                def columns(n, w, col, width=512, count=KT):
                    for i in range(2):
                        tiles = slice(i * count // 2, (i + 1) * count // 2)
                        slot = slot_of(n) + i
                        load(slot, static_gen(slot, n, l, base * ROUNDS), w[:, tiles, col:col + width], count // 2)

                def pair(q, rnd, o):
                    for slot, e, w in zip(gu_slots(q), (0, 0, 1, 1), (ex_g, ex_u, ex_g, ex_u)):
                        load(slot, expert_gen(slot, q, l, rnd), w[l, o, 2 * q + e], KT)
                    for e, slot in enumerate(down_slots(q)):
                        load(slot, expert_gen(slot, q, l, rnd), ex_d[l, o, 2 * q + e], 2)

                def vector(u):
                    of = l if u < 4 else (l + 1) % DEPTH
                    for half in range(2):
                        columns(ADA_AT[u] + half, ada[of], ADA_VECTORS[u] * D + half * 512)

                for i, col in enumerate((0, BW, FF_COL + NH, FF_COL + NH + BW, 2 * BW, FF_COL + NH + 2 * BW)):
                    columns(INPUT_AT[i], win[l], col)
                    if i < 4:
                        vector(i)
                for i in range(4):
                    columns(GATES_AT + i, win[l], FF_COL + NH + 3 * BW + BW * i)
                vector(4)
                vector(5)
                for i, w in enumerate(wbr):
                    columns(BRANCH_AT + i, w[l], 0, D, BT)
                for half in range(2):
                    columns(WO_AT + half, wo[l], half * 512)
                slot = slot_of(SHARED_AT)
                for i, w in enumerate((sh_g, sh_u)):
                    load(slot + i, static_gen(slot + i, SHARED_AT, l, base * ROUNDS), w[l], KT)
                slot = slot_of(SHARED_AT + 1)
                load(slot, static_gen(slot, SHARED_AT + 1, l, base * ROUNDS), sh_d[l], 2)
                assert SHARED_AT + 2 == STATIC_LOADS
                for q in range(OCT // 2):
                    pair(q, base * ROUNDS, 0)
                sp.wait_ge(pass_ready, l + 2)
                apart(sp)
                end = sp.value_load(passi[0:1, 0:1], min_val=1, max_val=4 * DEPTH)
                with sp.Fori(base * ROUNDS + 1, end * ROUNDS) as rnd:
                    for q in range(OCT // 2):
                        pair(q, rnd, rnd % ROUNDS)
            sp.wait_ge(x_ready, 4 * DEPTH + 1)
            sp.dma_start(out[0].rearrange("(t p) d -> p t d", p=P), xs[:, :, :]).then_inc(out_done, 16)
            sp.wait_ge(out_done, 16)

        @block.gpsimd
        def _(pool):
            def bias_row(u, of, v, uses):
                pool.memset(parts[u % 2][:, :], 0.0).then_inc(zero_parts, 1)
                pool.wait_ge(zero_parts, 2 * uses + u % 2 + 1)
                pool.dma_start(parts[u % 2][0:1, :], b_ada.unsqueeze(1)[of][:, v * D:v * D + D]).then_inc(bias_in[u % 2], 16)

            bias_row(0, 0, 0, 0)
            bias_row(1, 0, 1, 0)
            with pool.Fori(0, DEPTH) as l:
                pool.wait_ge(x_ready, l * 4 + 1)
                for dst, src in ((wff[:, :, :], w_in.rearrange("l (p t) n -> l p t n", t=KT)[l][:, :, FF_COL:FF_COL + NH]),
                                 (bgate[:, :], b_gate.rearrange("l (g p) -> l p g", p=P)[l]),
                                 (bforget[:, :], b_forget[l].partition_broadcast(P)),
                                 (wrt[:, :, :], w_router.rearrange("l (p t) n -> l p t n", t=KT)[l]),
                                 (rbias[:, :], router_bias[l].partition_broadcast(P))):
                    pool.dma_start(dst, src, allow_slow_non_contiguous=True).then_inc(params_in, 16)

                def norm_params(which):
                    for i, w in enumerate((ln_g, ln_b)):
                        pool.dma_start(lnp[:, i, :], w[l][which, :].partition_broadcast(P)).then_inc(ln_in, 16)

                norm_params(0)
                for u in range(6):
                    pool.wait_ge(red_ready, l * 6 + u + 1)
                    apart(pool)
                    bias_row(u, l if u < 4 else (l + 1) % DEPTH, ADA_VECTORS[u], l * 3 + u // 2 + 1)
                pool.wait_ge(x_ready, l * 4 + 3)
                norm_params(1)
                pool.wait_ge(xp0_ready, l + 1)
                pool.tensor_tensor(xrest, xs[:, :, :], xp[:, 0, :, :], ALU.subtract).then_inc(xr_ready, 1)
                pool.wait_ge(xp1_ready, l + 1)
                pool.tensor_tensor(xp[:, 2, :, :], xrest, xp[:, 1, :, :], ALU.subtract).then_inc(xp2_ready, 1)
                pool.wait_ge(xp2_ready, l + 1)
                apart(pool)
                pool.memset(wide[:, 3 * D:3 * D + 3 * D // 2], 0.0).then_inc(zeroed, 1)
                pool.memset(small[:, 896:1024], 0.0).then_inc(zeroed, 1)

        @block.tensor
        def _(pe):
            def mm(dst, lhsT, rhs, start=True, stop=True, **kw):
                return nc.tensor.matmul(dst, lhsT, rhs, start=start, stop=stop, **kw)

            for i in range(SLOTS):
                pe.sem_inc(ring_free[i], 1)
            pe.wait_ge(const_in, 16)
            pe.wait_ge(x_in, 16)
            pe.wait_ge(csrep_ready, 1)
            freed = []

            def free(ins):
                ins.then_inc(ring_free[freed.pop(0)], 1)

            def both_landed(slot, gens):
                pe.wait_ge(ring_full[slot], (gens[0] + 1) * 16)
                pe.wait_ge(ring_full[slot + 1], (gens[1] + 1) * 16)

            def vector_sums(n, gens, banks):
                for half in range(2):
                    both_landed(slot_of(n + half), gens[half])
                    w = static_view(n + half, KT)
                    for t in range(KT):
                        q = t % 4
                        m = mm(ps[banks + half][32 * q:32 * q + 32, :], csrep[:, t, :], w[:, t, :], t < 4, t >= 4,
                               tile_position=(0, 32 * q))
                        if freed and t < 7:
                            free(m)
                    m.then_inc(ada_ready, 1)
                    freed.extend((slot_of(n + half), slot_of(n + half) + 1))

            def vector_reduced(v, buf, bank):
                if v in (2, 5):
                    for half in range(2):
                        m = mm(ps[bank + half][:, :], quad, parts[buf][:, half * 512:half * 512 + 512])
                        if freed and half == 0:
                            free(m)
                else:
                    for t in range(KT):
                        m = mm(ps[bank][:, t:t + 1], parts[buf][:, t:D:KT], quad[:, 0:1])
                        if freed and t < 7:
                            free(m)
                m.then_inc(red_ready, 1)

            for v in (0, 1):
                vector_sums(2 * v - 2 * AHEAD, ((0, 0), (0, 0)), 2 * v)
            for v in (0, 1):
                pe.wait_ge(parts_ready, 2 * v + 2)
                vector_reduced(v, v, 4 + v)
            with pe.Fori(0, DEPTH) as l:
                pe.wait_ge(pass_ready, l + 1)
                apart(pe)
                base = pe.value_load(passi[0:1, 0:1], min_val=0, max_val=4 * (DEPTH - 1))

                def gens(n):
                    return [static_gen(slot_of(n) + i, n, l, base * ROUNDS) for i in range(2)]

                def landed(n):
                    both_landed(slot_of(n), gens(n))

                def sums(u, banks):
                    n = ADA_AT[u]
                    vector_sums(n, (gens(n), gens(n + 1)), banks)

                def reduced(u, bank):
                    pe.wait_ge(parts_ready, 2 * (AHEAD + 6 * l + u) + 2)
                    vector_reduced(ADA_VECTORS[u], u % 2, bank)

                def transpose_x(which):
                    first = 4 * (1 - which)
                    for tt in range(TT):
                        pe.wait_ge(x_ready, l * 4 + (3 if which else 1) - (1 - tt) * which)
                        for b in range(4):
                            for t in (2 * b, 2 * b + 1):
                                a = t % 2 * S + tt * P
                                m = nc.tensor.transpose(ps[first + b][:, a:a + P], xs[:, tt, t:D:KT], ident)
                                if freed:
                                    free(m)
                            if tt:
                                m.then_inc(xt_ready, 1)

                pe.wait_ge(red_used, AHEAD + 6 * l)
                transpose_x(0)
                pe.wait_ge(u_dve, l * 8 + 4)
                pe.wait_ge(u_act, l * 8 + 4)

                for i in range(6):
                    n = INPUT_AT[i]
                    landed(n)
                    w = static_view(n, KT)
                    if i in (2, 3):
                        pe.wait_ge(qkv_act, l * 12 + 2 * (i - 1))
                    if i in (4, 5):
                        pe.wait_ge(rot_ready, l * 4 + 2 * (i - 3))
                    for half in range(2):
                        bank = ps[2 * (i % 2) + half]
                        for b in range(2 if i < 2 else 1):
                            for t in range(KT):
                                if i < 2:
                                    f = (2 * half + b) * P
                                    m = mm(bank[:, b * S:b * S + S], w[:, t, f:f + P], uT[:, t, :], t == 0, t == KT - 1)
                                else:
                                    m = mm(bank[:, :], uT[:, t, half * P:half * P + P], w[:, t, :], t == 0, t == KT - 1)
                                if freed and t < KT - 1:
                                    free(m)
                        m.then_inc(proj_ready, 1)
                    freed.extend((slot_of(n), slot_of(n) + 1))
                    if 1 <= i <= 4:
                        if i >= 2:
                            pe.wait_ge(red_used, AHEAD + 6 * l + i - 1)
                        reduced(i - 1, 6)
                    if i < 4:
                        sums(i, 4)
                pe.wait_ge(red_used, AHEAD + 6 * l + 4)
                pe.wait_ge(params_in, l * 80 + 80)
                for tt in range(TT):
                    for t in range(KT):
                        m = mm(ps[4][:, tt * NH:tt * NH + NH], uT[:, t, tt * P:tt * P + P], wff[:, t, :], t == 0, t == KT - 1)
                        if freed:
                            free(m)
                m.then_inc(ff_ready, 1)
                pe.wait_ge(rot_ready, l * 4 + 4)
                for b in range(4):
                    if b % 2 == 0:
                        pe.wait_ge(qkv_act, l * 12 + 6 + b)
                    for kt in (2 * b, 2 * b + 1):
                        for tt in range(TT):
                            a = kt % 2 * S + tt * P
                            m = nc.tensor.transpose(ps[b][:, a:a + P], rot[:, kt // BT, tt, kt % BT * P:kt % BT * P + P], ident)
                    m.then_inc(rt_ready, 1)
                pe.wait_ge(nlogf_ready, l + 1)
                mm(ps[5][:, 0:NH], tri, nlogf[:, 0, :])
                mm(ps[5][:, NH:2 * NH], ones, nlogf[:, 0, :], True, False)
                mm(ps[5][:, NH:2 * NH], tri, nlogf[:, 1, :], False, True)
                mm(ps[5][0:NH, P:3 * P], nlogf[:, 0, :], tri_ones, True, False)
                mm(ps[5][0:NH, 2 * P:3 * P], nlogf[:, 1, :], tri, False, True).then_inc(cum_ready, 1)

                def scores(h):
                    kind, hh = divmod(h, NH)
                    a, kt = 64 * (hh % 2), hh // 2
                    if h >= 2:
                        pe.wait_ge(nm_ready, l * 16 + h - 1)
                    q, k = qkT[a:a + HD, 2 * kind, kt, :], qkT[a:a + HD, 2 * kind + 1, kt, :]
                    for tt in range(TT):
                        dst = ps[4 + h % 2][:, part(tt)]
                        keys = (tt + 1) * P
                        m = mm(dst, q[:, tt * P:tt * P + P], k[:, 0:keys], True, kind == 1)
                        if kind == 0:
                            m = mm(dst, ident[0:NH, hh:hh + 1].to_broadcast([NH, P]), ncumT[:, 0:keys], False, True)
                    m.then_inc(s_ready, 1)

                def gate_columns(g):
                    n = GATES_AT + g // 4
                    if g % 4 == 0:
                        landed(n)
                    if g >= 2:
                        pe.wait_ge(gates_raw, l * 16 + g - 1)
                    w = static_view(n, KT)
                    for t in range(KT):
                        m = mm(ps[g % 2][:, 0:S], w[:, t, g % 4 * P:g % 4 * P + P], uT[:, t, :], t == 0, t == KT - 1)
                        if freed:
                            free(m)
                    m.then_inc(gate_ready, 1)
                    if g % 4 == 3:
                        freed.extend((slot_of(n), slot_of(n) + 1))

                def probs_transposed(h):
                    pe.wait_ge(p_ready, l * 16 + h + 1)
                    if h >= 2:
                        pe.wait_ge(pts_ready, l * 16 + h - 1)
                    for i in range(3):
                        m = nc.tensor.transpose(ps[6 + h % 2][:, (0, 1, 2)[i] * P:(i + 1) * P], pS[h % 2][:, i * P:i * P + P], ident)
                    m.then_inc(pt_ready, 1)

                def values(h):
                    kind, hh = divmod(h, NH)
                    a, kt = 64 * (hh % 2), hh // 2
                    bank = ps[2 + h // 2 % 2]
                    if h >= 4 and h % 2 == 0:
                        pe.wait_ge(y_ready, l * 8 + h // 2 - 1)
                    pe.wait_ge(pts_ready, l * 16 + h + 1)
                    col = slice(hh * HD, hh * HD + HD)
                    mm(bank[a:a + HD, 0:S], vv[:, kind, 0, col], pT[h % 2][:, 0:S], True, False, tile_position=(0, a))
                    m = mm(bank[a:a + HD, P:S], vv[:, kind, 1, col], pT[h % 2][:, S:S + P], False, True, tile_position=(0, a))
                    if h % 2:
                        m.then_inc(pv_ready, 1)

                pe.wait_ge(cumc_ready, l * 2 + 2)
                pe.wait_ge(qkv_act, l * 12 + 12)
                for h in range(2 * NH + 2):
                    if h < 2 * NH:
                        scores(h)
                        gate_columns(h)
                    if 1 <= h <= 2 * NH:
                        probs_transposed(h - 1)
                    if h >= 2:
                        values(h - 2)

                sums(4, 4)
                pe.wait_ge(y_ready, l * 8 + 8)
                sums(5, 2)
                nb = BRANCH_AT
                landed(nb)
                landed(nb + 1)
                pe.wait_ge(gates_ready, l + 1)
                for j in range(KT):
                    if j >= 2:
                        pe.wait_ge(merged_ready, l * 8 + j - 1)
                    for b in range(2):
                        w = static_view(nb + b, BT)
                        for kt in range(BT):
                            m = mm(ps[j % 2][:, b * S:b * S + S], w[:, kt, j * P:j * P + P], yT[:, b, kt, :], kt == 0, kt == BT - 1)
                            if freed and kt < BT - 1:
                                free(m)
                    m.then_inc(br_ready, 1)
                    if j in (1, 2):
                        reduced(3 + j, 5 + j)
                freed += [slot_of(nb) + i for i in range(2)] + [slot_of(nb + 1) + i for i in range(2)]
                pe.wait_ge(merged_ready, l * 8 + 8)
                pe.wait_ge(red_used, AHEAD + 6 * l + 6)
                for tt in range(TT):
                    for half in range(2):
                        n = WO_AT + half
                        if tt == 0:
                            landed(n)
                        w = static_view(n, KT)
                        for t in range(KT):
                            m = mm(ps[4 + 2 * tt + half][:, :], mergedT[:, t, tt * P:tt * P + P], w[:, t, :], t == 0, t == KT - 1)
                            if freed and t < KT - 1:
                                free(m)
                    m.then_inc(wo_ready, 1)
                freed += [slot_of(WO_AT) + i for i in range(2)] + [slot_of(WO_AT + 1) + i for i in range(2)]

                transpose_x(1)
                pe.wait_ge(u_dve, l * 8 + 8)
                pe.wait_ge(u_act, l * 8 + 8)
                for tt in range(TT):
                    for t in range(KT):
                        m = mm(ps[4][:, tt * NE:tt * NE + NE], uT[:, t, tt * P:tt * P + P], wrt[:, t, :], t == 0, t == KT - 1)
                        if freed:
                            free(m)
                m.then_inc(logits_ready, 1)
                n = SHARED_AT
                landed(n)
                for g in range(2):
                    for ft in range(2):
                        for t in range(KT):
                            m = mm(ps[5 + g][:, ft * S:ft * S + S], gu_view(slot_of(n))[:, g, t, ft:FF:2], uT[:, t, :], t == 0, t == KT - 1)
                m.then_inc(shgu_ready, 1)
                freed.extend((slot_of(n), slot_of(n) + 1))
                pe.wait_ge(emask_ready, l * 2 + 2)
                free(mm(ps[7][:, 0:NE], tri_strict, emask[:, 0, :]))
                free(mm(ps[7][:, NE:2 * NE], ones, emask[:, 0, :], True, False))
                assert not freed
                mm(ps[7][:, NE:2 * NE], tri_strict, emask[:, 1, :], False, True)
                mm(ps[7][:, 2 * NE:3 * NE], ones, emask[:, 0, :], True, False)
                mm(ps[7][:, 2 * NE:3 * NE], ones, emask[:, 1, :], False, True).then_inc(rank_ready, 1)
                n += 1
                pe.wait_ge(ring_full[slot_of(n)], (gens(n)[0] + 1) * 16)
                pe.wait_ge(pass_ready, l + 2)
                pe.wait_ge(hs_ready, l + 1)
                for tt in range(TT):
                    for half in range(2):
                        for ft in range(2):
                            m = mm(ACC[tt * 2 + half][:, :], hsT[:, ft, tt * P:tt * P + P],
                                   down_view(slot_of(n))[:, ft, half * 512:half * 512 + 512], ft == 0, False, skip_group_check=True)
                m.then_inc(ring_free[slot_of(n)], 1)
                apart(pe)
                end = pe.value_load(passi[0:1, 0:1], min_val=1, max_val=4 * DEPTH)

                pe.wait_ge(zeroed, l * 2 + 2)
                pe.wait_ge(xp2_ready, l + 1)

                def scatter(pairs, q, half):
                    if half == 0:
                        pe.wait_ge(sts_ready, pairs + 1)
                        pe.wait_ge(y2_ready, pairs + 1)
                    for tt in range(TT):
                        for i in range(3):
                            m = mm(ACC[tt * 2 + half][:, :], selT[q % 2][:, tt * P:tt * P + P],
                                   yp[:, i, half * 512:half * 512 + 512], False, False, skip_group_check=True)
                    return m

                def gather(gathers, q, half):
                    if half == 0:
                        pe.wait_ge(sel_ready, gathers + l + 1)
                    else:
                        pe.wait_ge(xg_act, gathers + 1)
                    for t in range(4 * half, 4 * half + 4):
                        for i in range(3):
                            for tt in range(TT):
                                m = mm(GB[:, t % 4 * P:t % 4 * P + P], xp[:, i, tt, t:D:KT], sel[:, tt, 2 * q:2 * q + 2, :],
                                       i == 0 and tt == 0, i == 2 and tt == TT - 1)
                                if freed:
                                    free(m)
                    m.then_inc((gth0_ready, gth1_ready)[half], 1)

                for half in range(2):
                    gather(base * ROUNDS * 4 + l, 0, half)
                with pe.Fori(base * ROUNDS, end * ROUNDS) as rnd:
                    for q in range(OCT // 2):
                        n = rnd * 4 + q
                        gu, down = gu_slots(q), down_slots(q)
                        for slot in gu:
                            pe.wait_ge(ring_full[slot], (expert_gen(slot, q, l, rnd) + 1) * 16)
                        pe.wait_ge(sts_ready, n + 1)
                        pe.wait_ge(xg_act, n + l + 1)
                        for t in range(KT):
                            if t == 4:
                                pe.wait_ge(xg_dve, n + l + 1)
                            for e in range(2):
                                m = mm(HB[64 * e:64 * e + 64, :], xg[q % 2][:, t, e * CAP:e * CAP + CAP],
                                       gu_view(gu[2 * e])[:, :, t, :], t == 0, t == KT - 1, tile_position=(0, 64 * e))
                                if freed:
                                    free(m)
                        m.then_inc(gu_ready, 1)
                        freed.extend(gu)
                        gather(n + l + 1, (q + 1) % 4, 0)
                        scatter(n, q + 3, 0)
                        pe.wait_ge(h_ready, n + 1)
                        for ft in range(2):
                            nc.tensor.transpose(HB[:, ft * P:ft * P + P], hb[:, ft:FF:2], ident)
                        for tt in range(TT):
                            nc.tensor.transpose(HB16[:, tt * P:tt * P + P], sel[:, tt, 2 * q:2 * q + 2, :], identb[:, :])
                        own = (rnd % ROUNDS) * OCT + 2 * q
                        for i in range(3):
                            for tt in range(TT):
                                m = mm(HB[:, FF + P:FF + P + 2], sel[:, tt, 2 * q:2 * q + 2, :], wp[:, i, tt, bass.ds(own, 2)],
                                       i == 0 and tt == 0, i == 2 and tt == TT - 1)
                        m.then_inc(ht_ready, 1)
                        scatter(n, q + 3, 1)
                        gather(n + l + 1, (q + 1) % 4, 1)
                        for slot in down:
                            pe.wait_ge(ring_full[slot], (expert_gen(slot, q, l, rnd) + 1) * 16)
                        pe.wait_ge(hts_ready, n + 1)
                        for half in range(2):
                            for ft in range(2):
                                for e in range(2):
                                    m = mm(YB[half][64 * e:64 * e + 64, :], hT[:, ft * P + e * CAP:ft * P + e * CAP + CAP],
                                           down_view(down[e])[:, ft, half * 512:half * 512 + 512], ft == 0, ft == 1,
                                           tile_position=(0, 64 * e))
                                    if half and ft and e == 0:
                                        m.then_inc(ring_free[down[0]], 1)
                            m.then_inc(yb_ready, 1)
                        freed.append(down[1])
                    pe.wait_ge(sts_ready, rnd * 4 + 5)
                    free(nc.tensor.transpose(HB[:, 0:P], hb[:, 0:FF:2], ident))
                scatter(end * 4 * ROUNDS, 3, 0)
                scatter(end * 4 * ROUNDS, 3, 1).then_inc(acc_ready, 1)

        @block.scalar
        def _(act):
            def apply(dst, src, func=ACT.Copy, **kw):
                return nc.scalar.activation(dst, src, func, **kw)

            act.wait_ge(c_in, 16)
            apply(csT[:, :], cT[:, :], ACT.Silu).then_inc(cs_ready, 1)
            apply(sd[:, :], cT[:, 0:TT]).then_inc(sts_ready, 1)
            with act.Fori(0, DEPTH) as l:
                act.wait_ge(pass_ready, l + 1)
                apart(act)
                base = act.value_load(passi[0:1, 0:1], min_val=0, max_val=4 * (DEPTH - 1))

                def modulate(which):
                    act.wait_ge(red_used, AHEAD + 6 * l + 4 * which)
                    first = 4 * (1 - which)
                    for b in (1, 3):
                        act.wait_ge(xt_ready, l * 8 + which * 4 + b + 1)
                        for t in (2 * b, 2 * b + 1):
                            apply(uT[:, t, :], ps[first + b][:, t % 2 * S:t % 2 * S + S], ACT.Identity,
                                  scale=modc[:, 2 + which, t:t + 1], bias=modc[:, which, t:t + 1]).then_inc(u_act, 1)

                modulate(0)
                for half in range(2):
                    act.wait_ge(proj_ready, l * 12 + half + 1)
                    apply(qkT[:, 0, 2 * half:2 * half + 2, :], ps[half][:, :].rearrange("p (t n) -> p t n", t=2), scale=SCALE)\
                        .then_inc(qkv_act, 1)
                for half in range(2):
                    act.wait_ge(proj_ready, l * 12 + half + 3)
                    apply(qkT[:, 1, 2 * half:2 * half + 2, :], ps[2 + half][:, :].rearrange("p (t n) -> p t n", t=2))\
                        .then_inc(qkv_act, 1)
                for i in range(4):
                    act.wait_ge(proj_ready, l * 12 + 9 + i)
                    apply(vv[:, i // 2, i % 2, :], ps[i][:, :]).then_inc(qkv_act, 1)
                act.wait_ge(ffz_ready, l + 1)
                apply(zabs[:, :, :], zf[:, :, :], ACT.Abs).then_inc(act_step, 1)
                act.wait_ge(act_step, l * 2 + 1)
                apply(zexp[:, :, :], zabs[:, :, :], ACT.Exp, scale=-1.0).then_inc(act_step, 1)
                act.wait_ge(act_step, l * 2 + 2)
                apply(softp[:, :, :], zexp[:, :, :], ACT.Ln, bias=1.0).then_inc(softp_ready, 1)
                for b in range(4):
                    act.wait_ge(rt_ready, l * 4 + b + 1)
                    apply(qkT[:, 2 + b // 2, 2 * (b % 2):2 * (b % 2) + 2, :], ps[b][:, :].rearrange("p (t n) -> p t n", t=2),
                          scale=SCALE if b < 2 else 1.0).then_inc(qkv_act, 1)
                act.wait_ge(pass_ready, l + 1)
                for h in range(2 * NH + 1):
                    if h < 2 * NH:
                        act.wait_ge(nm_ready, l * 16 + h + 1)
                        for tt in range(TT):
                            m = apply(pS[h % 2][:, part(tt)], sS[h % 2][:, part(tt)], ACT.Exp, bias=nmax[:, h % 2, tt:tt + 1],
                                      accum_out=lsum[:, h % 2, tt:tt + 1])
                        m.then_inc(exp_ready, 1)
                        act.wait_ge(gate_ready, l * 16 + h + 1)
                        apply(gatesT[:, h, :], ps[h % 2][:, 0:S], ACT.Identity, bias=bgate[:, h:h + 1]).then_inc(gates_raw, 1)
                    if h:
                        act.wait_ge(pt_ready, l * 16 + h)
                        apply(pT[(h - 1) % 2], ps[6 + (h - 1) % 2][:, 0:384]).then_inc(pts_ready, 1)
                act.wait_ge(gates_raw, l * 16 + 16)
                apply(gatesT, gatesT, ACT.Sigmoid).then_inc(gates_ready, 1)

                def norm_sqrt(which):
                    for tt in range(TT):
                        act.wait_ge(ve_ready, l * 4 + 2 * which + tt + 1)
                        apply(sd[:, tt:tt + 1], ve[:, tt:tt + 1], ACT.Sqrt).then_inc(sd_ready, 1)

                norm_sqrt(0)
                modulate(1)
                act.wait_ge(x_ready, l * 4 + 3)
                apply(xp[:, 0, :, :], xs[:, :, :]).then_inc(xp0_ready, 1)
                act.wait_ge(logits_ready, l + 1)
                apply(score[:, :, :], ps[4][:, 0:2 * NE].rearrange("p (t n) -> p t n", t=TT), ACT.Sigmoid)\
                    .then_inc(score_ready, 1)
                act.wait_ge(shgu_ready, l + 1)
                apply(shs, ps[5][:, :], ACT.Silu).then_inc(shs_ready, 1)
                act.wait_ge(xr_ready, l + 1)
                apply(xp[:, 1, :, :], xrest).then_inc(xp1_ready, 1)

                act.wait_ge(pass_ready, l + 2)
                apart(act)
                end = act.value_load(passi[0:1, 0:1], min_val=1, max_val=4 * DEPTH)
                def gathered(gathers, b):
                    act.wait_ge(gth0_ready, gathers + 1)
                    for t in range(4):
                        m = apply(xg[b][:, t, :], GB[:, t * P:t * P + P], ACT.Identity, scale=modc[:, 3, t:t + 1], bias=modc[:, 1, t:t + 1])
                    m.then_inc(xg_act, 1)

                gathered(base * ROUNDS * 4 + l, 0)
                with act.Fori(base * ROUNDS, end * ROUNDS) as rnd:
                    for q in range(OCT // 2):
                        n = rnd * 4 + q
                        act.wait_ge(gu_ready, n + 1)
                        apply(sg, HB[:, 0:FF], ACT.Silu).then_inc(sg_ready, 1)
                        gathered(n + l + 1, (q + 1) % 2)
                        act.wait_ge(hts_ready, n + 1)
                        for e in range(2):
                            rows = slice(64 * e, 64 * e + 64)
                            apply(wslot[rows, q:q + 1], HB[rows, FF + P + e:FF + P + e + 1])
                        apply(selT[q % 2], HB16[:, :]).then_inc(sts_ready, 1)
                        act.wait_ge(sts_ready, n + 2)
                        for half in range(2):
                            act.wait_ge(yb_ready, rnd * 8 + 2 * q + half + 1)
                            apply(yp[:, 0, half * 512:half * 512 + 512], YB[half][:, :], scale=wslot[:, q:q + 1])\
                                .then_inc(y0_ready, 1)
                        act.wait_ge(yr_ready, rnd * 8 + 2 * q + 2)
                        apply(yp[:, 1, :], yrest).then_inc(y1_ready, 1)
                norm_sqrt(1)

        @block.vector
        def _(dve):
            V = nc.vector

            V.memset(passf[:, :], 0.0).then_inc(dve_step, 1)
            dve.wait_ge(dve_step, 1)
            V.tensor_copy(passi[:, :], passf[:, :]).then_inc(pass_ready, 1)
            V.memset(morep[:, :], 0.0).then_inc(y2_ready, 1)
            dve.wait_ge(cs_ready, 1)
            V.tensor_copy(csrep[:, :, :], csT[:, :].unsqueeze(2).to_broadcast([P, KT, 32])).then_inc(csrep_ready, 1)
            dve.wait_ge(const_in, 16)
            V.tensor_copy(identb[:, :], ident)
            dve.wait_ge(x_in, 16)
            V.memset(rstd[:, :], 0.0).then_inc(x_ready, 1)

            def vector_parts(unit, buf, uses, banks):
                dve.wait_ge(bias_in[buf], uses * 16)
                for half in range(2):
                    dve.wait_ge(ada_ready, 2 * unit + half + 1)
                    to = parts[buf][:, half * 512:half * 512 + 512]
                    V.tensor_tensor(to, ps[banks + half][:, :], to, ALU.add).then_inc(parts_ready, 1)

            def vector_used(unit, v, bank):
                dve.wait_ge(red_ready, unit + 1)
                if v in (2, 5):
                    for half in range(2):
                        m = V.tensor_scalar(gate1p[:, v // 5, half * 512:half * 512 + 512], ps[bank + half][:, :], 1.0, None, ALU.add)
                else:
                    scale = v in (1, 4)
                    m = V.tensor_scalar(modc[:, 2 * scale + v // 3, :], ps[bank][:, 0:KT], float(scale), None, ALU.add)
                m.then_inc(red_used, 1)

            for v in (0, 1):
                vector_parts(v, v, 1, 2 * v)
            for v in (0, 1):
                vector_used(v, v, 4 + v)
            with dve.Fori(0, DEPTH) as l:
                dve.wait_ge(pass_ready, l + 1)
                apart(dve)
                base = dve.value_load(passi[0:1, 0:1], min_val=0, max_val=4 * (DEPTH - 1))
                steps = [0]

                def step(ins):
                    steps[0] += 1
                    ins.then_inc(dve_step, 1)
                    dve.wait_ge(dve_step, l * DVE_STEPS + steps[0] + 1)

                def take(u, banks):
                    vector_parts(AHEAD + 6 * l + u, u % 2, 3 * l + u // 2 + 2, banks)

                def use(u, bank):
                    vector_used(AHEAD + 6 * l + u, ADA_VECTORS[u], bank)

                def modulate(which):
                    dve.wait_ge(red_used, AHEAD + 6 * l + 4 * which)
                    first = 4 * (1 - which)
                    for b in (0, 2):
                        dve.wait_ge(xt_ready, l * 8 + which * 4 + b + 1)
                        for t in (2 * b, 2 * b + 1):
                            V.tensor_scalar(uT[:, t, :], ps[first + b][:, t % 2 * S:t % 2 * S + S], modc[:, 2 + which, t:t + 1],
                                            modc[:, which, t:t + 1], ALU.mult, ALU.add).then_inc(u_dve, 1)

                modulate(0)
                take(0, 4)
                use(0, 6)
                take(1, 4)
                for a in range(2):
                    for tt in range(TT):
                        dve.wait_ge(proj_ready, l * 12 + (2 + a) * 2 + tt + 1)
                        w = ps[2 * a + tt][:, :].rearrange("p (h c j) -> p h c j", c=2, j=HD // 2)
                        o = rot[:, a, tt, :].rearrange("p (h c j) -> p h c j", c=2, j=HD // 2)
                        cos, sin = (cst[:, C_ROPE + tt * HD + i * 32:C_ROPE + tt * HD + i * 32 + 32].unsqueeze(1)
                                    .to_broadcast([P, NH, HD // 2]) for i in range(2))
                        tmp = [rope_tmp[:, i, :].rearrange("p (h j) -> p h j", h=NH) for i in range(4)]
                        if a or tt:
                            dve.wait_ge(rot_ready, l * 4 + 2 * a + tt)
                        V.tensor_tensor(tmp[0], w[:, :, 0, :], cos, ALU.mult)
                        V.tensor_tensor(tmp[1], w[:, :, 1, :], sin, ALU.mult)
                        V.tensor_tensor(tmp[2], w[:, :, 1, :], cos, ALU.mult)
                        step(V.tensor_tensor(tmp[3], w[:, :, 0, :], sin, ALU.mult))
                        V.tensor_tensor(o[:, :, 0, :], tmp[0], tmp[1], ALU.subtract)
                        V.tensor_tensor(o[:, :, 1, :], tmp[2], tmp[3], ALU.add).then_inc(rot_ready, 1)
                    use(1 + a, 6)
                    take(2 + a, 4)
                use(3, 6)
                dve.wait_ge(ff_ready, l + 1)
                dve.wait_ge(params_in, l * 80 + 80)
                V.tensor_tensor(zf[:, :, :], ps[4][:, 0:TT * NH].rearrange("p (t h) -> p t h", t=TT),
                                bforget[:, :].unsqueeze(1).to_broadcast([P, TT, NH]), ALU.add).then_inc(ffz_ready, 1)
                dve.wait_ge(ffz_ready, l + 1)
                step(V.tensor_scalar(zneg[:, :, :], zf[:, :, :], -1.0, 0.0, ALU.mult, ALU.max))
                dve.wait_ge(softp_ready, l + 1)
                V.tensor_tensor(nlogf[:, :, :], zneg[:, :, :], softp[:, :, :], ALU.add).then_inc(nlogf_ready, 1)
                dve.wait_ge(cum_ready, l + 1)
                V.tensor_copy(ncum[:, :, :], ps[5][:, 0:TT * NH].rearrange("p (t h) -> p t h", t=TT)).then_inc(cumc_ready, 1)
                V.tensor_copy(ncumT[:, :], ps[5][0:NH, P:3 * P]).then_inc(cumc_ready, 1)
                dve.wait_ge(cumc_ready, l * 2 + 2)

                def biased_max(h):
                    kind, hh = divmod(h, NH)
                    dve.wait_ge(s_ready, l * 16 + h + 1)
                    for tt in range(TT):
                        dst, src = sS[h % 2][:, part(tt)], ps[4 + h % 2][:, part(tt)]
                        if kind == 0:
                            m = V.scalar_tensor_tensor(dst, src, ncum[:, tt, hh:hh + 1], mask(0, tt), ALU.subtract, ALU.add)
                        else:
                            m = V.tensor_tensor(dst, src, mask(1, tt), ALU.add)
                    step(m)
                    for tt in range(TT):
                        m = V.tensor_reduce(nmax[:, h % 2, tt:tt + 1], sS[h % 2][:, part(tt)], AX, ALU.max, negate=True)
                    m.then_inc(nm_ready, 1)

                def normalise(h):
                    dve.wait_ge(exp_ready, l * 16 + h + 1)
                    step(V.reciprocal(rsum[:, h % 2, :], lsum[:, h % 2, :]))
                    for tt in range(TT):
                        m = V.tensor_scalar(pS[h % 2][:, part(tt)], pS[h % 2][:, part(tt)], rsum[:, h % 2, tt:tt + 1], None, ALU.mult)
                    m.then_inc(p_ready, 1)

                for h in range(2 * NH + 2):
                    if h < 2 * NH:
                        biased_max(h)
                    if 1 <= h <= 2 * NH:
                        normalise(h - 1)
                    if h >= 3 and h % 2:
                        n = (h - 3) // 2
                        dve.wait_ge(pv_ready, l * 8 + n + 1)
                        V.tensor_copy(yT[:, n // BT, n % BT, :], ps[2 + n % 2][:, 0:S]).then_inc(y_ready, 1)
                take(4, 4)
                take(5, 2)
                dve.wait_ge(gates_ready, l + 1)
                for j in range(KT):
                    dve.wait_ge(br_ready, l * 8 + j + 1)
                    a, b = merge_tmp[:, 2 * (j % 2), :], merge_tmp[:, 2 * (j % 2) + 1, :]
                    if j >= 2:
                        dve.wait_ge(merged_ready, l * 8 + j - 1)
                    V.tensor_tensor(a, ps[j % 2][:, 0:S], gatesT[:, j, :], ALU.mult)
                    step(V.tensor_tensor(b, ps[j % 2][:, S:2 * S], gatesT[:, KT + j, :], ALU.mult))
                    V.tensor_tensor(mergedT[:, j, :], a, b, ALU.add).then_inc(merged_ready, 1)
                    if j in (2, 3):
                        use(2 + j, 4 + j)

                def norm(which, banks, ready):
                    for tt in range(TT):
                        ready(tt)
                        for half in range(2):
                            a = slice(half * 512, half * 512 + 512)
                            m = V.tensor_tensor(z[:, tt, a], banks(tt, half)[:, :], gate1p[:, which, a], ALU.mult)
                        step(m)
                        step(V.scalar_tensor_tensor(z[:, tt, :], xs[:, tt, :], ALPHA, z[:, tt, :], ALU.mult, ALU.add))
                        for half in range(2):
                            m = V.bn_stats(bst[:, tt, half, :], z[:, tt, half * 512:half * 512 + 512])
                        step(m)
                        apart(dve)
                        step(V.bn_aggr(mv[:, tt, :], bst[:, tt, :, :].rearrange("p a b -> p (a b)")))
                        V.tensor_scalar(ve[:, tt:tt + 1], mv[:, tt, 1:2], LN_EPS, None, ALU.add).then_inc(ve_ready, 1)
                    for tt in range(TT):
                        dve.wait_ge(sd_ready, l * 4 + 2 * which + tt + 1)
                        step(V.reciprocal(rstd[:, tt:tt + 1], sd[:, tt:tt + 1]))
                        dve.wait_ge(ln_in, l * 64 + 32 * (which + 1))
                        step(V.scalar_tensor_tensor(z[:, tt, :], z[:, tt, :], mv[:, tt, 0:1], lnp[:, 0, :], ALU.subtract, ALU.mult))
                        V.scalar_tensor_tensor(xs[:, tt, :], z[:, tt, :], rstd[:, tt:tt + 1], lnp[:, 1, :], ALU.mult, ALU.add)\
                            .then_inc(x_ready, 1)

                norm(0, lambda tt, half: ps[4 + 2 * tt + half], lambda tt: dve.wait_ge(wo_ready, l * 2 + 1 + tt))
                modulate(1)

                dve.wait_ge(score_ready, l + 1)
                step(V.tensor_tensor(choice[:, :, :], score[:, :, :], rbias[:, :].unsqueeze(1).to_broadcast([P, TT, NE]), ALU.add))
                apart(dve)
                for tt in range(TT):
                    for g in range(NG):
                        m = V.max(gmax[:, tt, g, :], choice[:, tt, g * 8:g * 8 + 8])
                step(m)
                step(V.tensor_tensor(gsc[:, :, :], gmax[:, :, :, 0], gmax[:, :, :, 1], ALU.add))
                other = gsc[:, :, :].unsqueeze(2).to_broadcast([P, TT, NG, NG])
                own = gsc[:, :, :].unsqueeze(3).to_broadcast([P, TT, NG, NG])
                V.tensor_tensor(gcmp[:, :, :, :], other, own, ALU.is_gt)
                step(V.tensor_tensor(geq[:, :, :, :], other, own, ALU.is_equal))
                lower = cst[:, C_LT8:C_LT8 + NG * NG].rearrange("p (a b) -> p a b", a=NG).unsqueeze(1).to_broadcast([P, TT, NG, NG])
                step(V.tensor_tensor(geq[:, :, :, :], geq[:, :, :, :], lower, ALU.mult))
                step(V.tensor_tensor(gcmp[:, :, :, :], gcmp[:, :, :, :], geq[:, :, :, :], ALU.add))
                step(V.tensor_reduce(grank[:, :, :], gcmp[:, :, :, :], AX, ALU.add))
                step(V.tensor_scalar(gmask[:, :, :], grank[:, :, :], 4.0, None, ALU.is_lt))
                V.tensor_scalar(gpen[:, :, :], gmask[:, :, :], 1.0, -NEG, ALU.subtract, ALU.mult)
                grouped = choice[:, :, :].rearrange("p t (g e) -> p (t g) e", g=NG)
                flat = gmask[:, :, :].rearrange("p t g -> p (t g)").unsqueeze(2).to_broadcast([P, TT * NG, 8])
                step(V.tensor_tensor(grouped, grouped, flat, ALU.mult))
                pen = gpen[:, :, :].rearrange("p t g -> p (t g)").unsqueeze(2).to_broadcast([P, TT * NG, 8])
                step(V.tensor_tensor(grouped, grouped, pen, ALU.add))
                apart(dve)
                for tt in range(TT):
                    m = V.max(top8[:, tt, :], choice[:, tt, :])
                step(m)
                for tt in range(TT):
                    eighth = top8[:, tt, 7:8]
                    V.tensor_scalar(above[:, tt, :], choice[:, tt, :], eighth, None, ALU.is_gt)
                    m = V.tensor_scalar(ties[:, tt, :], choice[:, tt, :], eighth, None, ALU.is_equal)
                step(m)
                step(V.tensor_reduce(nabove[:, :], above[:, :, :], AX, ALU.add))
                step(V.tensor_scalar(nabove[:, :], nabove[:, :], -1.0, float(TOPK), ALU.mult, ALU.add))
                for tt in range(TT):
                    m = V.tensor_tensor_scan(tiesum[:, tt, :], ties[:, tt, :], cst[:, C_ZERO:C_ZERO + NE], 0.0, ALU.add, ALU.add)
                step(m)
                for tt in range(TT):
                    m = V.scalar_tensor_tensor(ties[:, tt, :], tiesum[:, tt, :], nabove[:, tt:tt + 1], ties[:, tt, :],
                                               ALU.is_le, ALU.mult)
                step(m)
                for tt in range(TT):
                    V.tensor_tensor(emask[:, tt, :], above[:, tt, :], ties[:, tt, :], ALU.add).then_inc(emask_ready, 1)
                dve.wait_ge(shs_ready, l + 1)
                V.tensor_tensor(hsT, shs.rearrange("p (t n) -> p t n", t=2), ps[6][:, :].rearrange("p (t n) -> p t n", t=2),
                                ALU.mult).then_inc(hs_ready, 1)
                dve.wait_ge(emask_ready, l * 2 + 2)
                for tt in range(TT):
                    m = V.scalar_tensor_tensor(wraw[:, tt, :], score[:, tt, :], 1.0, emask[:, tt, :], ALU.mult, ALU.mult,
                                               accum_out=wsum[:, tt:tt + 1])
                step(m)
                step(V.reciprocal(wrec[:, :], wsum[:, :]))
                for tt in range(TT):
                    m = V.tensor_scalar(wtok[:, tt, :], wraw[:, tt, :], wrec[:, tt:tt + 1], ROUTED_SCALE, ALU.mult, ALU.mult)
                step(m)
                step(V.tensor_copy(wp[:, 0, :, :], wtok[:, :, :]))
                step(V.tensor_tensor(wraw[:, :, :], wtok[:, :, :], wp[:, 0, :, :], ALU.subtract))
                step(V.tensor_copy(wp[:, 1, :, :], wraw[:, :, :]))
                step(V.tensor_tensor(wp[:, 2, :, :], wraw[:, :, :], wp[:, 1, :, :], ALU.subtract))
                dve.wait_ge(rank_ready, l + 1)
                step(V.scalar_tensor_tensor(erank[:, :, :], ps[7][:, 0:2 * NE].rearrange("p (t e) -> p t e", t=TT), 1.0,
                                            emask[:, :, :], ALU.add, ALU.mult))
                step(V.tensor_scalar(erank[:, :, :], erank[:, :, :], 1.0, None, ALU.subtract))
                step(V.tensor_reduce(mostf[:, :], ps[7][:, 2 * NE:3 * NE], AX, ALU.max))
                step(V.tensor_tensor(overf[:, :], mostf[:, :].to_broadcast([P, N_THR]), cst[:, C_THR:C_END], ALU.is_gt))
                step(V.tensor_reduce(morep[:, :], overf[:, :], AX, ALU.add))
                step(V.scalar_tensor_tensor(passf[:, :], morep[:, :], 1.0, passf[:, :], ALU.add, ALU.add))
                V.tensor_copy(passi[:, :], passf[:, :]).then_inc(pass_ready, 1)

                def select(n_pass, o, q):
                    V.tensor_tensor(sel[:, :, 2 * q:2 * q + 2, :],
                                    erank[:, :, bass.ds(o * OCT + 2 * q, 2)].unsqueeze(3).to_broadcast([P, TT, 2, CAP]),
                                    cst[:, bass.ds(n_pass * CAP + C_IOTA, CAP)].unsqueeze(1).unsqueeze(1).to_broadcast([P, TT, 2, CAP]),
                                    ALU.is_equal).then_inc(sel_ready, 1)

                def gathered(gathers, b):
                    dve.wait_ge(gth1_ready, gathers + 1)
                    for t in range(4, KT):
                        m = V.tensor_scalar(xg[b][:, t, :], GB[:, t % 4 * P:t % 4 * P + P], modc[:, 3, t:t + 1], modc[:, 1, t:t + 1],
                                            ALU.mult, ALU.add)
                    m.then_inc(xg_dve, 1)

                select(0, 0, 0)
                select(0, 0, 1)
                dve.wait_ge(pass_ready, l + 2)
                apart(dve)
                end = dve.value_load(passi[0:1, 0:1], min_val=1, max_val=4 * DEPTH)
                gathered(base * ROUNDS * 4 + l, 0)
                with dve.Fori(0, end - base) as n_pass:
                    with dve.Fori(0, ROUNDS) as o:
                        rnd = (base + n_pass) * ROUNDS + o
                        for q in range(OCT // 2):
                            n = rnd * 4 + q
                            dve.wait_ge(sg_ready, n + 1)
                            V.tensor_tensor(hb, sg, HB[:, FF:2 * FF], ALU.mult).then_inc(h_ready, 1)
                            dve.wait_ge(ht_ready, n + 1)
                            V.tensor_copy(hT, HB[:, 0:FF]).then_inc(hts_ready, 1)
                            if q < 2:
                                select(n_pass, o, q + 2)
                            else:
                                select(n_pass + (o + 1) // ROUNDS, (o + 1) % ROUNDS, q - 2)
                            gathered(n + l + 1, (q + 1) % 2)
                            for half in range(2):
                                a = slice(half * 512, half * 512 + 512)
                                dve.wait_ge(y0_ready, rnd * 8 + 2 * q + half + 1)
                                V.scalar_tensor_tensor(yrest[:, a], YB[half][:, :], wslot[:, q:q + 1], yp[:, 0, a],
                                                       ALU.mult, ALU.subtract).then_inc(yr_ready, 1)
                            dve.wait_ge(y1_ready, n + 1)
                            V.tensor_tensor(yp[:, 2, :], yrest, yp[:, 1, :], ALU.subtract).then_inc(y2_ready, 1)

                norm(1, lambda tt, half: ACC[tt * 2 + half], lambda tt: dve.wait_ge(acc_ready, l + 1))
                assert steps[0] == DVE_STEPS, steps


INPUTS = ("x", "c", "w_ada", "b_ada", "w_in", "b_forget", "b_gate", "w_br_fox", "w_br_dil", "w_o", "ln_g", "ln_b", "w_router",
          "router_bias", "w_exp_gate", "w_exp_up", "w_exp_down", "w_sh_gate", "w_sh_up", "w_sh_down")


def kernel(**inputs):
    import concourse.bacc as bacc
    from concourse.bass_utils import run_bass_kernel_spmd

    nc = bacc.Bacc("TRN2", target_bir_lowering=False, num_devices=1)
    arrays = {f"in_{name}": np.ascontiguousarray(inputs[name]) for name in INPUTS}
    arrays["in_constants"] = constants()
    args = [nc.dram_tensor(n, a.shape, mybir.dt.from_np(a.dtype), kind="ExternalInput").ap() for n, a in arrays.items()]
    args.append(nc.dram_tensor("out_x", (1, S, D), F32, kind="ExternalOutput").ap())
    decoder(nc, *args)
    return run_bass_kernel_spmd(nc, [arrays], core_ids=[0]).results[0]["out_x"]
```

```python
from contextlib import ExitStack

import numpy as np

import concourse.bass as bass
from concourse import mybir

P = 128
D = 1024
S = 256
DEPTH = 2
TT = S // P
KT = D // P
HD = 64
NH = 8
BW = NH * HD
BT = BW // P
NE = 64
TOPK = 8
NG = 8
FF = 256
CAP = 64
OCT = 8
ROUNDS = NE // OCT
SLOTS = 12
PIECE = KT * FF
PAIR_PIECES = 6
PER_ROUND = OCT // 2 * PAIR_PIECES // SLOTS
STATIC_LOADS = 28
STATIC_AT = -2 * STATIC_LOADS % SLOTS
INPUT_AT = (0, 1, 2, 3, 4, 5)
GATES_AT = (6, 9, 13, 17)
BRANCH_AT, WO_AT, SHARED_AT = 18, 20, 26
ADA_AT = (None, None, (7, 8), (10, 11), (12, 14), (15, 16))
NEXT_AT = 22
GATES = (2, 5)
ADA_STEPS = [(v, what, i) for v in range(2, 6) for what in ("sum", "reduce")
             for i in range(1 if what == "reduce" and v not in GATES else 2)]
SUMS = 2 * 6
REDUCED = (None, None, 0, 2, 3, 4)
REDUCTIONS = 7


def reductions(l, v=2, more=0):
    return 1 + l * REDUCTIONS + REDUCED[v] + more


def half_sums(l, v=2, more=0):
    return 4 + l * SUMS + 2 * (v - 2) + more


ALPHA = float((2 * DEPTH) ** 0.25)
SCALE = HD ** -0.5
ROUTED_SCALE = 2.5
LN_EPS = 1e-5
NEG = -1e30


def slot_of(n):
    return (STATIC_AT + 2 * n) % SLOTS


AHEAD = 4
LOADS_AHEAD = [int((s - STATIC_AT) % SLOTS >= SLOTS - 2 * AHEAD) for s in range(SLOTS)]
LOADS_STATIC = [len(range((s - STATIC_AT) % SLOTS, 2 * STATIC_LOADS - 1, SLOTS)) for s in range(SLOTS)]


def static_gen(slot, n, l, rounds):
    return LOADS_AHEAD[slot] + l * LOADS_STATIC[slot] + rounds * PER_ROUND + 2 * n // SLOTS


def expert_gen(slot, q, l, rnd):
    return LOADS_AHEAD[slot] + (l + 1) * LOADS_STATIC[slot] + rnd * PER_ROUND + q // 2


DVE_STEPS = 98
FF_COL = 3 * BW

F32 = mybir.dt.float32
BF16 = mybir.dt.bfloat16
I32 = mybir.dt.int32
ALU = mybir.AluOpType
ACT = mybir.ActivationFunctionType
AX = mybir.AxisListType.X

C_ROPE = 0
C_MASK = C_ROPE + TT * 64
C_TRI = C_MASK + 2 * 384
C_ONES = C_TRI + P
C_TRIS = C_ONES + P
C_ID = C_TRIS + P
C_IOTA = C_ID + P
C_LT8 = C_IOTA + 5 * CAP
C_QUAD = C_LT8 + NG * NG
C_ZERO = C_QUAD + P
C_THR = C_ZERO + NE
N_THR = -(-S // CAP) - 1
C_END = C_THR + N_THR


def constants():
    t = np.zeros((P, C_END), np.float32)
    half = HD // 2
    freq = (np.float32(10000.0) ** (-np.arange(half, dtype=np.float32) * np.float32(2.0) / np.float32(HD))).astype(np.float32)
    ang = (np.arange(S, dtype=np.float32)[:, None] * freq[None, :]).astype(np.float32)
    rope = np.stack([np.cos(ang), np.sin(ang)], axis=1).astype(np.float32)
    t[:, C_ROPE:C_MASK] = rope.reshape(TT, P, 64).transpose(1, 0, 2).reshape(P, -1)
    q = np.arange(S)[:, None]
    k = np.arange(S)[None, :]
    causal = q >= k
    fox = np.where(causal, 0.0, NEG)
    often = np.zeros((S, S))
    for window, dil in ((128, 1), (512, 4), (2048, 16)):
        often += causal & ((q - k) % dil == 0) & ((q - k) // dil <= window // dil)
    dilated = np.where(often > 0, np.log(np.maximum(often, 1.0)), NEG)
    for n, m in enumerate((fox, dilated)):
        t[:, C_MASK + 384 * n:C_MASK + 384 * n + P] = m[:P, :P]
        t[:, C_MASK + 384 * n + P:C_MASK + 384 * n + 384] = m[P:, :]
    r = np.arange(P)
    t[:, C_TRI:C_TRI + P] = r[:, None] <= r[None, :]
    t[:, C_ONES:C_ONES + P] = 1.0
    t[:, C_TRIS:C_TRIS + P] = r[:, None] < r[None, :]
    t[:, C_ID:C_ID + P] = np.eye(P)
    t[:, C_IOTA:C_IOTA + 5 * CAP] = np.arange(5 * CAP)
    t[:, C_LT8:C_LT8 + NG * NG] = (np.arange(NG)[None, :] < np.arange(NG)[:, None]).reshape(-1)
    t[::32, C_QUAD:C_QUAD + P] = 1.0
    t[:, C_THR:C_END] = CAP * np.arange(1, N_THR + 1)
    return t


def decoder(nc, x, c, w_ada, b_ada, w_in, b_forget, b_gate, w_br_fox, w_br_dil, w_o, ln_g, ln_b, w_router,
            router_bias, w_exp_gate, w_exp_up, w_exp_down, w_sh_gate, w_sh_up, w_sh_down, consts, out):
    with ExitStack() as ctx:
        def sb(name, shape, dt=F32):
            return ctx.enter_context(nc.sbuf_tensor(name, shape, dt))

        def sem(name):
            return ctx.enter_context(nc.semaphore(name))

        ring = sb("ring", [P, SLOTS * PIECE])
        cst = sb("cst", [P, C_END])
        xs = sb("xs", [P, TT, D])
        uT = sb("uT", [P, KT, S])
        gate1p = sb("gate1p", [P, 2, D])
        lnp = sb("lnp", [P, 2, D])
        parts = [sb(f"parts{i}", [P, D]) for i in range(2)]
        wide = sb("wide", [P, 6 * D])
        gatesT = wide[:, 0:2 * KT * S].rearrange("p (g n) -> p g n", n=S)
        yT = wide[:, 2 * KT * S:].rearrange("p (b t n) -> p b t n", b=2, t=BT)
        z = wide[:, 0:2 * D].rearrange("p (t n) -> p t n", t=TT)
        xp = wide[:, 0:3 * D].bitcast(BF16).rearrange("p (i t n) -> p i t n", i=3, t=TT)
        xrest = wide[:, 3 * D:5 * D].rearrange("p (t n) -> p t n", t=TT)
        yp = wide[:, 3 * D:3 * D + 3 * D // 2].bitcast(BF16).rearrange("p (i n) -> p i n", i=3)
        yrest = wide[:, 5 * D:6 * D]
        mid = sb("mid", [P, 6 * D])
        qkT = mid[:, 0:4 * D].rearrange("p (a t n) -> p a t n", a=4, t=BT)
        vv = mid[:, 4 * D:6 * D].rearrange("p (a t n) -> p a t n", a=2, t=TT)
        xg = [mid[:, D * i:D * i + D].rearrange("p (t n) -> p t n", t=KT) for i in range(2)]
        sel = mid[:, 4 * D:4 * D + D // 2].bitcast(BF16).rearrange("p (t e s) -> p t e s", t=TT, e=OCT)
        shs = mid[:, 0:512]
        hsT = mid[:, 512:1024].rearrange("p (t n) -> p t n", t=2)
        small = sb("small", [P, 9 * 256])
        sS = [small[:, 384 * i:384 * i + 384] for i in range(2)]
        pS = [small[:, 768 + 384 * i:768 + 384 * i + 384] for i in range(2)]
        pT = [small[:, 1536 + 384 * i:1536 + 384 * i + 384] for i in range(2)]
        sg = small[:, 0:256]
        hb = small[:, 256:512]
        hT = small[:, 512:768]
        selT = [small[:, 768 + 128 * i:896 + 128 * i].bitcast(BF16) for i in range(2)]
        rot = wide[:, 0:2 * D].rearrange("p (a t n) -> p a t n", a=2, t=TT)
        mergedT = mid[:, 0:2 * D].rearrange("p (t n) -> p t n", t=KT)
        rope_tmp = wide[:, 5 * D:].rearrange("p (i n) -> p i n", i=4)
        merge_tmp = small[:, 0:D].rearrange("p (i n) -> p i n", i=4)
        cT = sb("cT", [P, KT])
        csT = sb("csT", [P, KT])
        csrep = sb("csrep", [P, KT, 32])
        modc = sb("modc", [P, 4, KT])
        adab = sb("adab", [P, 2, KT])
        wff = sb("wff", [P, KT, NH])
        bgate = sb("bgate", [P, 2 * KT])
        bforget = sb("bforget", [P, NH])
        wrt = sb("wrt", [P, KT, NE])
        rbias = sb("rbias", [P, NE])
        zf = sb("zf", [P, TT, NH])
        zabs = sb("zabs", [P, TT, NH])
        zexp = sb("zexp", [P, TT, NH])
        softp = sb("softp", [P, TT, NH])
        zneg = sb("zneg", [P, TT, NH])
        nlogf = sb("nlogf", [P, TT, NH])
        ncum = sb("ncum", [P, TT, NH])
        ncumT = sb("ncumT", [NH, S])
        nmax = sb("nmax", [P, 2, TT])
        lsum = sb("lsum", [P, 2, TT])
        rsum = sb("rsum", [P, 2, TT])
        bst = sb("bst", [P, TT, 2, 6])
        mv = sb("mv", [P, TT, 2])
        ve = sb("ve", [P, TT])
        sd = sb("sd", [P, TT])
        rstd = sb("rstd", [P, TT])
        score = mid[:, 1024:1152].rearrange("p (t e) -> p t e", t=TT)
        choice = mid[:, 1152:1280].rearrange("p (t e) -> p t e", t=TT)
        gmax = mid[:, 2176:2304].rearrange("p (t g i) -> p t g i", t=TT, g=NG)
        gsc = sb("gsc", [P, TT, NG])
        gcmp = mid[:, 2304:2432].rearrange("p (t g i) -> p t g i", t=TT, g=NG)
        geq = mid[:, 2432:2560].rearrange("p (t g i) -> p t g i", t=TT, g=NG)
        grank = sb("grank", [P, TT, NG])
        gmask = sb("gmask", [P, TT, NG])
        gpen = sb("gpen", [P, TT, NG])
        top8 = mid[:, 2560:2560 + TT * 8].rearrange("p (t i) -> p t i", t=TT)
        above = mid[:, 1280:1408].rearrange("p (t e) -> p t e", t=TT)
        nabove = sb("nabove", [P, TT])
        ties = mid[:, 1408:1536].rearrange("p (t e) -> p t e", t=TT)
        tiesum = mid[:, 1536:1664].rearrange("p (t e) -> p t e", t=TT)
        emask = mid[:, 1664:1792].rearrange("p (t e) -> p t e", t=TT)
        wraw = mid[:, 1792:1920].rearrange("p (t e) -> p t e", t=TT)
        wsum = sb("wsum", [P, TT])
        wrec = sb("wrec", [P, TT])
        wtok = mid[:, 1920:2048].rearrange("p (t e) -> p t e", t=TT)
        erank = mid[:, 4 * D + 704:4 * D + 832].rearrange("p (t e) -> p t e", t=TT)
        mostf = sb("mostf", [P, 1])
        overf = sb("overf", [P, N_THR])
        morep = sb("morep", [P, 1])
        passf = sb("passf", [P, 1])
        passi = sb("passi", [P, 1], I32)
        wp = mid[:, 4 * D + 512:4 * D + 704].bitcast(BF16).rearrange("p (i t e) -> p i t e", i=3, t=TT)
        wslot = sb("wslot", [P, OCT // 2])
        identb = sb("identb", [P, P], BF16)

        ps = [ctx.enter_context(nc.psum_tensor(f"ps{i}", [P, 512], F32)) for i in range(8)]
        ACC = ps[0:4]
        HB, GB, YB = ps[4], ps[5], ps[6:8]
        HB16 = HB[:, FF:FF + P].bitcast(BF16)

        ident = cst[:, C_ID:C_ID + P]
        tri = cst[:, C_TRI:C_TRI + P]
        tri_ones = cst[:, C_TRI:C_TRI + 2 * P]
        tri_strict = cst[:, C_TRIS:C_TRIS + P]
        ones = cst[:, C_ONES:C_ONES + P]
        quad = cst[:, C_QUAD:C_QUAD + P]

        def x_bank(which, tt):
            return 0 if which else 4 + 2 * tt

        def mask(kind, tt):
            a = C_MASK + 384 * kind
            return cst[:, a:a + P] if tt == 0 else cst[:, a + P:a + 384]

        def part(tt):
            return slice(0, P) if tt == 0 else slice(P, 384)

        def static_view(n, tiles):
            at = slot_of(n) * PIECE
            return ring[:, at:at + 2 * PIECE].rearrange("p (t n) -> p t n", t=tiles)

        def gu_view(slot):
            return ring[:, slot * PIECE:(slot + 2) * PIECE].rearrange("p (g t f) -> p g t f", g=2, t=KT)

        def down_view(slot):
            return ring[:, slot * PIECE:(slot + 1) * PIECE].rearrange("p (t n) -> p t n", t=2)

        def gu_slots(q):
            return [PAIR_PIECES * (q % 2) + i for i in range(4)]

        def down_slots(q):
            return [PAIR_PIECES * (q % 2) + 4 + e for e in range(2)]

        const_in, x_in, c_in = sem("const_in"), sem("x_in"), sem("c_in")
        params_in, ln_in, adab_in = sem("params_in"), sem("ln_in"), sem("adab_in")
        bias_in = [sem(f"bias_in{i}") for i in range(2)]
        ring_full = [sem(f"ring_full{i}") for i in range(SLOTS)]
        ring_free = [sem(f"ring_free{i}") for i in range(SLOTS)]
        out_done = sem("out_done")
        cs_ready, csrep_ready = sem("cs_ready"), sem("csrep_ready")
        zero_parts, ada_ready, parts_act, parts_dve = sem("zero_parts"), sem("ada_ready"), sem("parts_act"), sem("parts_dve")
        red_ready, red_used = sem("red_ready"), sem("red_used")
        xt_ready, u_dve, u_act = sem("xt_ready"), sem("u_dve"), sem("u_act")
        proj_ready, qkv_act, rot_ready = sem("proj_ready"), sem("qkv_act"), sem("rot_ready")
        rt_ready = sem("rt_ready")
        ff_ready, ffz_ready, softp_ready = sem("ff_ready"), sem("ffz_ready"), sem("softp_ready")
        nlogf_ready, cum_ready, cumc_ready = sem("nlogf_ready"), sem("cum_ready"), sem("cumc_ready")
        s_ready, nm_ready, exp_ready = sem("s_ready"), sem("nm_ready"), sem("exp_ready")
        p_ready, pt_ready, pts_ready = sem("p_ready"), sem("pt_ready"), sem("pts_ready")
        pv_ready, y_ready = sem("pv_ready"), sem("y_ready")
        gate_ready, gates_raw, gates_ready = sem("gate_ready"), sem("gates_raw"), sem("gates_ready")
        br_ready, merged_ready, wo_ready = sem("br_ready"), sem("merged_ready"), sem("wo_ready")
        ve_ready, sd_ready, x_ready = sem("ve_ready"), sem("sd_ready"), sem("x_ready")
        xp0_ready, xr_ready, xp1_ready, xp2_ready = sem("xp0_ready"), sem("xr_ready"), sem("xp1_ready"), sem("xp2_ready")
        logits_ready, score_ready, shgu_ready = sem("logits_ready"), sem("score_ready"), sem("shgu_ready")
        shs_ready, hs_ready, emask_ready = sem("shs_ready"), sem("hs_ready"), sem("emask_ready")
        rank_ready, pass_ready = sem("rank_ready"), sem("pass_ready")
        sel_ready, zeroed = sem("sel_ready"), sem("zeroed")
        gth0_ready, gth1_ready, xg_act, xg_dve = sem("gth0_ready"), sem("gth1_ready"), sem("xg_act"), sem("xg_dve")
        gu_ready, sg_ready, h_ready = sem("gu_ready"), sem("sg_ready"), sem("h_ready")
        ht_ready, hts_ready = sem("ht_ready"), sem("hts_ready")
        sts_ready, yb_ready, y0_ready = sem("sts_ready"), sem("yb_ready"), sem("y0_ready")
        yr_ready, y1_ready, y2_ready, acc_ready = sem("yr_ready"), sem("y1_ready"), sem("y2_ready"), sem("acc_ready")
        dve_step, act_step = sem("dve_step"), sem("act_step")
        gone_by = sem("gone_by")

        def apart(eng):
            eng.sem_inc(gone_by, 1)

        block = ctx.enter_context(nc.Block())

        @block.sync
        def _(sp):
            sp.dma_start(cT[:, :], c.rearrange("o (p t) -> p (o t)", t=KT)).then_inc(c_in, 16)

            ada = w_ada.rearrange("l (p t) n -> l p t n", t=KT)
            win = w_in.rearrange("l (p t) n -> l p t n", t=KT)
            wbr = [w.rearrange("l (t p) n -> l p t n", p=P) for w in (w_br_fox, w_br_dil)]
            wo = w_o.rearrange("l (t p) n -> l p t n", p=P)
            sh_g, sh_u = (w.rearrange("l (p t) f -> l p t f", t=KT) for w in (w_sh_gate, w_sh_up))
            sh_d = w_sh_down.rearrange("l (p t) n -> l p t n", t=2)
            ex_g, ex_u = (w.rearrange("l (o e) (p t) f -> l o e p t f", e=OCT, t=KT) for w in (w_exp_gate, w_exp_up))
            ex_d = w_exp_down.rearrange("l (o e) (p t) n -> l o e p t n", e=OCT, t=2)

            def load(slot, gen, src, rows):
                sp.wait_ge(ring_free[slot], gen + 1)
                apart(sp)
                dst = ring[:, slot * PIECE:(slot + 1) * PIECE].rearrange("p (t n) -> p t n", t=rows)
                sp.dma_start(dst, src).then_inc(ring_full[slot], 16)

            for h in range(4):
                slot = slot_of(h - AHEAD)
                for i in range(2):
                    load(slot + i, 0, ada[0][:, 4 * i:4 * i + 4, h * 512:h * 512 + 512], 4)

            sp.dma_start(cst[:, :], consts).then_inc(const_in, 16)
            sp.dma_start(xs[:, :, :], x[0].rearrange("(t p) d -> p t d", p=P)).then_inc(x_in, 16)

            with sp.Fori(0, DEPTH) as l:
                sp.wait_ge(pass_ready, l + 1)
                apart(sp)
                base = sp.value_load(passi[0:1, 0:1], min_val=0, max_val=4 * (DEPTH - 1))

                def columns(n, w, col, width=512, count=KT):
                    for i in range(2):
                        tiles = slice(i * count // 2, (i + 1) * count // 2)
                        slot = slot_of(n) + i
                        load(slot, static_gen(slot, n, l, base * ROUNDS), w[:, tiles, col:col + width], count // 2)

                def pair(q, rnd, o):
                    for slot, e, w in zip(gu_slots(q), (0, 0, 1, 1), (ex_g, ex_u, ex_g, ex_u)):
                        load(slot, expert_gen(slot, q, l, rnd), w[l, o, 2 * q + e], KT)
                    for e, slot in enumerate(down_slots(q)):
                        load(slot, expert_gen(slot, q, l, rnd), ex_d[l, o, 2 * q + e], 2)

                def vector_half(v, half):
                    columns(ADA_AT[v][half], ada[l], v * D + half * 512)

                for i, col in enumerate((2 * BW, FF_COL + NH + 2 * BW, FF_COL + NH, FF_COL + NH + BW, 0, BW)):
                    columns(INPUT_AT[i], win[l], col)
                for h in range(2 * NH):
                    if h % 4 == 0:
                        columns(GATES_AT[h // 4], win[l], FF_COL + NH + 3 * BW + BW * (h // 4))
                    if h < len(ADA_STEPS) and ADA_STEPS[h][1] == "sum":
                        vector_half(ADA_STEPS[h][0], ADA_STEPS[h][2])
                for i, w in enumerate(wbr):
                    columns(BRANCH_AT + i, w[l], 0, D, BT)
                for half in range(2):
                    columns(WO_AT + half, wo[l], half * 512)
                for h in range(4):
                    columns(NEXT_AT + h, ada[(l + 1) % DEPTH], h * 512)
                slot = slot_of(SHARED_AT)
                for i, w in enumerate((sh_g, sh_u)):
                    load(slot + i, static_gen(slot + i, SHARED_AT, l, base * ROUNDS), w[l], KT)
                slot = slot_of(SHARED_AT + 1)
                load(slot, static_gen(slot, SHARED_AT + 1, l, base * ROUNDS), sh_d[l], 2)
                assert SHARED_AT + 2 == STATIC_LOADS
                for q in range(OCT // 2):
                    pair(q, base * ROUNDS, 0)
                sp.wait_ge(pass_ready, l + 2)
                apart(sp)
                end = sp.value_load(passi[0:1, 0:1], min_val=1, max_val=4 * DEPTH)
                with sp.Fori(base * ROUNDS + 1, end * ROUNDS) as rnd:
                    for q in range(OCT // 2):
                        pair(q, rnd, rnd % ROUNDS)
            for tt in range(TT):
                sp.wait_ge(x_ready, 4 * DEPTH + 1 + tt)
                sp.dma_start(out[0].rearrange("(t p) d -> p t d", p=P)[:, tt, :], xs[:, tt, :]).then_inc(out_done, 16)
            sp.wait_ge(out_done, 16 * TT)

        @block.gpsimd
        def _(pool):
            def next_biases(l):
                pool.dma_start(adab[:, :, :], b_ada.rearrange("l (v p t) -> l p v t", p=P, t=KT)[l][:, 0:2, :],
                               allow_slow_non_contiguous=True).then_inc(adab_in, 16)

            next_biases(0)
            with pool.Fori(0, DEPTH) as l:
                pool.wait_ge(x_ready, l * 4 + 2)
                for dst, src in ((wff[:, :, :], w_in.rearrange("l (p t) n -> l p t n", t=KT)[l][:, :, FF_COL:FF_COL + NH]),
                                 (bgate[:, :], b_gate.rearrange("l (g p) -> l p g", p=P)[l]),
                                 (bforget[:, :], b_forget[l].partition_broadcast(P)),
                                 (wrt[:, :, :], w_router.rearrange("l (p t) n -> l p t n", t=KT)[l]),
                                 (rbias[:, :], router_bias[l].partition_broadcast(P))):
                    pool.dma_start(dst, src, allow_slow_non_contiguous=True).then_inc(params_in, 16)

                def norm_params(which):
                    for i, w in enumerate((ln_g, ln_b)):
                        pool.dma_start(lnp[:, i, :], w[l][which, :].partition_broadcast(P)).then_inc(ln_in, 16)

                norm_params(0)
                pool.wait_ge(red_used, reductions(l))
                apart(pool)
                next_biases((l + 1) % DEPTH)
                for v in range(2, 6):
                    if v < 4:
                        pool.wait_ge(red_ready, reductions(l))
                    else:
                        pool.wait_ge(red_ready, reductions(l, v - 1))
                    apart(pool)
                    pool.memset(parts[v % 2][:, :], 0.0).then_inc(zero_parts, 1)
                    pool.wait_ge(zero_parts, l * 4 + v - 1)
                    pool.dma_start(parts[v % 2][0:1, :], b_ada.unsqueeze(1)[l][:, v * D:v * D + D]).then_inc(bias_in[v % 2], 16)
                pool.wait_ge(x_ready, l * 4 + 4)
                norm_params(1)
                pool.wait_ge(xp0_ready, l + 1)
                pool.tensor_tensor(xrest, xs[:, :, :], xp[:, 0, :, :], ALU.subtract).then_inc(xr_ready, 1)
                pool.wait_ge(xp1_ready, l + 1)
                pool.tensor_tensor(xp[:, 2, :, :], xrest, xp[:, 1, :, :], ALU.subtract).then_inc(xp2_ready, 1)
                pool.wait_ge(xp2_ready, l + 1)
                apart(pool)
                pool.memset(wide[:, 3 * D:3 * D + 3 * D // 2], 0.0).then_inc(zeroed, 1)
                pool.memset(small[:, 896:1024], 0.0).then_inc(zeroed, 1)

        @block.tensor
        def _(pe):
            def mm(dst, lhsT, rhs, start=True, stop=True, **kw):
                return nc.tensor.matmul(dst, lhsT, rhs, start=start, stop=stop, **kw)

            for i in range(SLOTS):
                pe.sem_inc(ring_free[i], 1)
            pe.wait_ge(csrep_ready, 1)
            freed = []

            def free(ins):
                ins.then_inc(ring_free[freed.pop(0)], 1)

            def both_landed(slot, gens):
                pe.wait_ge(ring_full[slot], (gens[0] + 1) * 16)
                pe.wait_ge(ring_full[slot + 1], (gens[1] + 1) * 16)

            def vector_sums(n, bank):
                w = static_view(n, KT)
                for t in range(KT):
                    q = t % 4
                    m = mm(ps[bank][32 * q:32 * q + 32, :], csrep[:, t, :], w[:, t, :], t < 4, t >= 4, tile_position=(0, 32 * q))
                    if freed and t < KT - 1:
                        free(m)
                m.then_inc(ada_ready, 1)
                freed.extend((slot_of(n), slot_of(n) + 1))

            def vector_reduced(v, half, bank):
                if v in GATES:
                    m = mm(ps[bank][:, :], quad, parts[v % 2][:, half * 512:half * 512 + 512])
                else:
                    for t in range(KT):
                        m = mm(ps[bank][:, t:t + 1], parts[v % 2][:, t:D:KT], quad[:, 0:1])
                m.then_inc(red_ready, 1)

            def next_reduced(v):
                for t in range(KT):
                    m = mm(ps[7][:, v * KT + t:v * KT + t + 1], parts[v][:, t:D:KT], quad[:, 0:1])
                    if freed and t < KT - 1:
                        free(m)
                if v:
                    m.then_inc(red_ready, 1)

            for h in range(4):
                both_landed(slot_of(h - AHEAD), (0, 0))
                vector_sums(h - AHEAD, 2 + h)
            pe.wait_ge(const_in, 16)
            for v in (0, 1):
                pe.wait_ge(parts_act, 2 * v + 2)
                next_reduced(v)
            pe.wait_ge(red_used, 1)
            with pe.Fori(0, DEPTH) as l:
                pe.wait_ge(pass_ready, l + 1)
                apart(pe)
                base = pe.value_load(passi[0:1, 0:1], min_val=0, max_val=4 * (DEPTH - 1))

                def gens(n):
                    return [static_gen(slot_of(n) + i, n, l, base * ROUNDS) for i in range(2)]

                def landed(n):
                    both_landed(slot_of(n), gens(n))

                def transpose_x(which, tt):
                    pe.wait_ge(x_ready, l * 4 + 2 * which + tt + 1)
                    for t in range(KT):
                        m = nc.tensor.transpose(ps[x_bank(which, tt) + t // 4][:, t % 4 * P:t % 4 * P + P], xs[:, tt, t:D:KT], ident)
                        if t % 4 == 3:
                            m.then_inc(xt_ready, 1)
                        elif freed:
                            free(m)

                def modulated(which, tt):
                    pe.wait_ge(u_act, l * 6 + 3 * which + 2 + tt)
                    if tt:
                        pe.wait_ge(u_dve, l * 2 + which + 1)

                def forget_logits():
                    pe.wait_ge(params_in, l * 80 + 80)
                    for tt in range(TT):
                        for t in range(KT):
                            m = mm(ps[4][:, tt * NH:tt * NH + NH], uT[:, t, tt * P:tt * P + P], wff[:, t, :], t == 0, t == KT - 1)
                            if freed and t < KT - 1:
                                free(m)
                    m.then_inc(ff_ready, 1)

                def forget_sums():
                    pe.wait_ge(nlogf_ready, l + 1)
                    mm(ps[5][:, 0:NH], tri, nlogf[:, 0, :])
                    mm(ps[5][:, NH:2 * NH], ones, nlogf[:, 0, :], True, False)
                    mm(ps[5][:, NH:2 * NH], tri, nlogf[:, 1, :], False, True)
                    mm(ps[5][0:NH, P:3 * P], nlogf[:, 0, :], tri_ones, True, False)
                    mm(ps[5][0:NH, 2 * P:3 * P], nlogf[:, 1, :], tri, False, True).then_inc(cum_ready, 1)

                transpose_x(0, 0)
                transpose_x(0, 1)
                modulated(0, 0)
                for i in range(6):
                    n = INPUT_AT[i]
                    landed(n)
                    w = static_view(n, KT)
                    if i in (2, 3):
                        pe.wait_ge(qkv_act, l * 12 + 2 * (i - 1))
                    if i in (4, 5):
                        pe.wait_ge(rot_ready, l * 4 + 2 * (i - 3))
                    for half in range(2):
                        bank = ps[2 * (i % 2) + half]
                        if i == 0 and half:
                            modulated(0, 1)
                        for b in range(2 if i >= 4 else 1):
                            for t in range(KT):
                                if i >= 4:
                                    f = (2 * half + b) * P
                                    m = mm(bank[:, b * S:b * S + S], w[:, t, f:f + P], uT[:, t, :], t == 0, t == KT - 1)
                                else:
                                    m = mm(bank[:, :], uT[:, t, half * P:half * P + P], w[:, t, :], t == 0, t == KT - 1)
                                if freed and t < KT - 1:
                                    free(m)
                        m.then_inc(proj_ready, 1)
                    freed.extend((slot_of(n), slot_of(n) + 1))
                    if i == 3:
                        forget_logits()
                    if i == 4:
                        forget_sums()
                pe.wait_ge(rot_ready, l * 4 + 4)
                for b in range(4):
                    if b % 2 == 0:
                        pe.wait_ge(qkv_act, l * 12 + 6 + b)
                    for kt in (2 * b, 2 * b + 1):
                        for tt in range(TT):
                            a = kt % 2 * S + tt * P
                            m = nc.tensor.transpose(ps[b][:, a:a + P], rot[:, kt // BT, tt, kt % BT * P:kt % BT * P + P], ident)
                    m.then_inc(rt_ready, 1)
                def scores(h):
                    kind, kt = h // NH, h % NH // 2
                    if h:
                        pe.wait_ge(nm_ready, l * 16 + h)
                    for tt in range(TT):
                        keys = (tt + 1) * P
                        for i in range(2):
                            rows = slice(HD * i, HD * i + HD)
                            m = mm(ps[4 + i][:, part(tt)], qkT[rows, 2 * kind, kt, tt * P:tt * P + P], qkT[rows, 2 * kind + 1, kt, 0:keys],
                                   True, kind == 1)
                            if kind and tt:
                                m.then_inc(s_ready, 1)
                        for i in range(2 * (kind == 0)):
                            m = mm(ps[4 + i][:, part(tt)], ident[0:NH, h + i:h + i + 1].to_broadcast([NH, P]), ncumT[:, 0:keys],
                                   False, True)
                            if tt:
                                m.then_inc(s_ready, 1)

                def gate_columns(g):
                    n = GATES_AT[g // 4]
                    if g % 4 == 0:
                        landed(n)
                    if g:
                        pe.wait_ge(gates_raw, l * 16 + g)
                    w = static_view(n, KT)
                    for t in range(KT):
                        m = mm(ps[0][:, 0:S], w[:, t, g % 4 * P:g % 4 * P + P], uT[:, t, :], t == 0, t == KT - 1)
                        if freed:
                            free(m)
                    m.then_inc(gate_ready, 1)
                    if g % 4 == 3:
                        freed.extend((slot_of(n), slot_of(n) + 1))

                def vector_step(k):
                    v, what, i = ADA_STEPS[k]
                    if what == "sum":
                        if i:
                            pe.wait_ge(parts_dve, l * 8 + 2 * (v - 2) + 1)
                        else:
                            pe.wait_ge(red_used, reductions(l, v))
                        landed(ADA_AT[v][i])
                        vector_sums(ADA_AT[v][i], 1)
                    else:
                        if i:
                            pe.wait_ge(red_used, reductions(l, v, 1))
                        else:
                            pe.wait_ge(parts_dve, l * 8 + 2 * (v - 2) + 2)
                        vector_reduced(v, i, 1)

                def probs_transposed(h):
                    pe.wait_ge(p_ready, l * 16 + h + 1)
                    if h >= 2:
                        pe.wait_ge(pts_ready, l * 16 + h - 1)
                    for i in range(3):
                        m = nc.tensor.transpose(ps[6 + h % 2][:, (0, 1, 2)[i] * P:(i + 1) * P], pS[h % 2][:, i * P:i * P + P], ident)
                    m.then_inc(pt_ready, 1)

                def values(n):
                    kind, kt = divmod(n, NH // 2)
                    if n >= 2:
                        pe.wait_ge(y_ready, l * 8 + n - 1)
                    pe.wait_ge(pts_ready, l * 16 + 2 * n + 2)
                    for tt in range(TT):
                        for i in range(2):
                            a = HD * i
                            col = slice(kt * P + a, kt * P + a + HD)
                            m = mm(ps[2 + n % 2][a:a + HD, tt * P:S], vv[:, kind, tt, col], pT[i][:, tt * S:S + tt * P],
                                   tt == 0, tt == 1, tile_position=(0, a))
                    m.then_inc(pv_ready, 1)

                pe.wait_ge(cumc_ready, l * 2 + 2)
                pe.wait_ge(qkv_act, l * 12 + 12)
                for h in range(2 * NH + 2):
                    if h < 2 * NH:
                        if h % 2 == 0:
                            scores(h)
                        gate_columns(h)
                    if h < len(ADA_STEPS):
                        vector_step(h)
                    if h >= 3 and h % 2:
                        values((h - 3) // 2)
                    if 1 <= h <= 2 * NH:
                        probs_transposed(h - 1)

                pe.wait_ge(y_ready, l * 8 + 8)
                nb = BRANCH_AT
                landed(nb)
                landed(nb + 1)
                pe.wait_ge(gates_raw, l * 16 + 16)
                pe.wait_ge(red_used, reductions(l, 5, 2))
                for j in range(KT):
                    if j >= 2:
                        pe.wait_ge(merged_ready, l * 8 + j - 1)
                    for b in range(2):
                        w = static_view(nb + b, BT)
                        for kt in range(BT):
                            m = mm(ps[j % 2][:, b * S:b * S + S], w[:, kt, j * P:j * P + P], yT[:, b, kt, :], kt == 0, kt == BT - 1)
                            if freed and kt < BT - 1:
                                free(m)
                    m.then_inc(br_ready, 1)
                freed += [slot_of(nb) + i for i in range(2)] + [slot_of(nb + 1) + i for i in range(2)]
                pe.wait_ge(merged_ready, l * 8 + 8)
                for tt in range(TT):
                    for half in range(2):
                        n = WO_AT + half
                        if tt == 0:
                            landed(n)
                        w = static_view(n, KT)
                        for t in range(KT):
                            m = mm(ps[4 + 2 * tt + half][:, :], mergedT[:, t, tt * P:tt * P + P], w[:, t, :], t == 0, t == KT - 1)
                            if freed and t < KT - 1:
                                free(m)
                    m.then_inc(wo_ready, 1)
                freed += [slot_of(WO_AT) + i for i in range(2)] + [slot_of(WO_AT + 1) + i for i in range(2)]

                transpose_x(1, 0)
                for h in range(4):
                    landed(NEXT_AT + h)
                    vector_sums(NEXT_AT + h, 2 + h)
                pe.wait_ge(parts_act, l * 4 + 8)
                n = SHARED_AT
                for tt in range(TT):
                    if tt:
                        transpose_x(1, 1)
                        for v in (0, 1):
                            next_reduced(v)
                    modulated(1, tt)
                    tokens = slice(tt * P, tt * P + P)
                    for t in range(KT):
                        m = mm(ps[4][:, tt * NE:tt * NE + NE], uT[:, t, tokens], wrt[:, t, :], t == 0, t == KT - 1)
                        if freed and t < KT - 1:
                            free(m)
                    m.then_inc(logits_ready, 1)
                    if tt == 0:
                        landed(n)
                    for g, bank in enumerate((5, 2)):
                        for ft in range(2):
                            for t in range(KT):
                                m = mm(ps[bank][:, ft * S + tt * P:ft * S + tt * P + P], gu_view(slot_of(n))[:, g, t, ft:FF:2],
                                       uT[:, t, tokens], t == 0, t == KT - 1)
                m.then_inc(shgu_ready, 1)
                freed.extend((slot_of(n), slot_of(n) + 1))
                pe.wait_ge(emask_ready, l * 2 + 2)
                pe.wait_ge(red_used, reductions(l + 1))
                free(mm(ps[7][:, 0:NE], tri_strict, emask[:, 0, :]))
                free(mm(ps[7][:, NE:2 * NE], ones, emask[:, 0, :], True, False))
                assert not freed
                mm(ps[7][:, NE:2 * NE], tri_strict, emask[:, 1, :], False, True)
                mm(ps[7][:, 2 * NE:3 * NE], ones, emask[:, 0, :], True, False)
                mm(ps[7][:, 2 * NE:3 * NE], ones, emask[:, 1, :], False, True).then_inc(rank_ready, 1)
                n += 1
                pe.wait_ge(ring_full[slot_of(n)], (gens(n)[0] + 1) * 16)
                pe.wait_ge(hs_ready, l + 1)
                for tt in range(TT):
                    for half in range(2):
                        for ft in range(2):
                            m = mm(ACC[tt * 2 + half][:, :], hsT[:, ft, tt * P:tt * P + P],
                                   down_view(slot_of(n))[:, ft, half * 512:half * 512 + 512], ft == 0, False, skip_group_check=True)
                m.then_inc(ring_free[slot_of(n)], 1)
                pe.wait_ge(pass_ready, l + 2)
                apart(pe)
                end = pe.value_load(passi[0:1, 0:1], min_val=1, max_val=4 * DEPTH)

                pe.wait_ge(zeroed, l * 2 + 2)
                pe.wait_ge(xp2_ready, l + 1)

                def scatter(pairs, q, half):
                    if half == 0:
                        pe.wait_ge(sts_ready, pairs + 1)
                        pe.wait_ge(y2_ready, pairs + 1)
                    for tt in range(TT):
                        for i in range(3):
                            mm(ACC[tt * 2 + half][:, :], selT[q % 2][:, tt * P:tt * P + P],
                               yp[:, i, half * 512:half * 512 + 512], False, False, skip_group_check=True)

                def gather(gathers, q, half, bank=GB):
                    if half == 0:
                        pe.wait_ge(sel_ready, gathers + l + 1)
                    elif bank is GB:
                        pe.wait_ge(xg_act, gathers + 1)
                    for t in range(4 * half, 4 * half + 4):
                        for i in range(3):
                            for tt in range(TT):
                                m = mm(bank[:, t % 4 * P:t % 4 * P + P], xp[:, i, tt, t:D:KT], sel[:, tt, 2 * q:2 * q + 2, :],
                                       i == 0 and tt == 0, i == 2 and tt == TT - 1)
                                if freed:
                                    free(m)
                    m.then_inc((gth0_ready, gth1_ready)[half], 1)

                gather(base * ROUNDS * 4 + l, 0, 0)
                gather(base * ROUNDS * 4 + l, 0, 1, HB)
                pe.wait_ge(xg_dve, base * ROUNDS * 4 + l + 1)
                apart(pe)
                with pe.Fori(base * ROUNDS, end * ROUNDS) as rnd:
                    for q in range(OCT // 2):
                        n = rnd * 4 + q
                        gu, down = gu_slots(q), down_slots(q)
                        for slot in gu:
                            pe.wait_ge(ring_full[slot], (expert_gen(slot, q, l, rnd) + 1) * 16)
                        pe.wait_ge(sts_ready, n + 1)
                        pe.wait_ge(xg_act, n + l + 1)
                        for t in range(KT):
                            if t == 4:
                                pe.wait_ge(xg_dve, n + l + 1)
                            for e in range(2):
                                m = mm(HB[64 * e:64 * e + 64, :], xg[q % 2][:, t, e * CAP:e * CAP + CAP],
                                       gu_view(gu[2 * e])[:, :, t, :], t == 0, t == KT - 1, tile_position=(0, 64 * e))
                                if freed:
                                    free(m)
                        m.then_inc(gu_ready, 1)
                        freed.extend(gu)
                        gather(n + l + 1, (q + 1) % 4, 0)
                        scatter(n, q + 3, 0)
                        pe.wait_ge(h_ready, n + 1)
                        for ft in range(2):
                            nc.tensor.transpose(HB[:, ft * P:ft * P + P], hb[:, ft:FF:2], ident)
                        for tt in range(TT):
                            nc.tensor.transpose(HB16[:, tt * P:tt * P + P], sel[:, tt, 2 * q:2 * q + 2, :], identb[:, :])
                        own = (rnd % ROUNDS) * OCT + 2 * q
                        for i in range(3):
                            for tt in range(TT):
                                m = mm(HB[:, FF + P:FF + P + 2], sel[:, tt, 2 * q:2 * q + 2, :], wp[:, i, tt, bass.ds(own, 2)],
                                       i == 0 and tt == 0, i == 2 and tt == TT - 1)
                        m.then_inc(ht_ready, 1)
                        scatter(n, q + 3, 1)
                        gather(n + l + 1, (q + 1) % 4, 1)
                        for slot in down:
                            pe.wait_ge(ring_full[slot], (expert_gen(slot, q, l, rnd) + 1) * 16)
                        pe.wait_ge(hts_ready, n + 1)
                        for half in range(2):
                            for ft in range(2):
                                for e in range(2):
                                    m = mm(YB[half][64 * e:64 * e + 64, :], hT[:, ft * P + e * CAP:ft * P + e * CAP + CAP],
                                           down_view(down[e])[:, ft, half * 512:half * 512 + 512], ft == 0, ft == 1,
                                           tile_position=(0, 64 * e))
                                    if half and ft and e == 0:
                                        m.then_inc(ring_free[down[0]], 1)
                            m.then_inc(yb_ready, 1)
                        freed.append(down[1])
                    pe.wait_ge(sts_ready, rnd * 4 + 5)
                    free(nc.tensor.transpose(HB[:, 0:P], hb[:, 0:FF:2], ident))
                for i in range(3):
                    if i == 0:
                        pe.wait_ge(y0_ready, end * 8 * ROUNDS)
                    elif i == 1:
                        pe.wait_ge(y1_ready, end * 4 * ROUNDS)
                    else:
                        pe.wait_ge(y2_ready, end * 4 * ROUNDS + 1)
                    for tt in range(TT):
                        for half in range(2):
                            m = mm(ACC[tt * 2 + half][:, :], selT[1][:, tt * P:tt * P + P], yp[:, i, half * 512:half * 512 + 512],
                                   False, False, skip_group_check=True)
                            if i == 2:
                                m.then_inc(acc_ready, 1)

        @block.scalar
        def _(act):
            def apply(dst, src, func=ACT.Copy, **kw):
                return nc.scalar.activation(dst, src, func, **kw)

            act.wait_ge(c_in, 16)
            apply(csT[:, :], cT[:, :], ACT.Silu).then_inc(cs_ready, 1)
            apply(sd[:, :], cT[:, 0:TT]).then_inc(sts_ready, 1)
            def next_parts(v, sums):
                for half in range(2):
                    act.wait_ge(ada_ready, sums + half + 1)
                    apply(parts[v][:, half * 512:half * 512 + 512], ps[2 + 2 * v + half][:, :]).then_inc(parts_act, 1)

            for v in (0, 1):
                next_parts(v, 2 * v)
            with act.Fori(0, DEPTH) as l:
                act.wait_ge(pass_ready, l + 1)
                apart(act)
                base = act.value_load(passi[0:1, 0:1], min_val=0, max_val=4 * (DEPTH - 1))

                def modulate(which, tt):
                    act.wait_ge(red_used, reductions(l, 5 if which else 2))
                    for b in range(tt, 2):
                        act.wait_ge(xt_ready, l * 8 + which * 4 + 2 * tt + b + 1)
                        for t in range(4 * b, 4 * b + 4):
                            m = apply(uT[:, t, tt * P:tt * P + P], ps[x_bank(which, tt) + b][:, t % 4 * P:t % 4 * P + P], ACT.Identity,
                                      scale=modc[:, 2 + which, t:t + 1], bias=modc[:, which, t:t + 1])
                        m.then_inc(u_act, 1)

                modulate(0, 0)
                modulate(0, 1)
                for i in range(4):
                    act.wait_ge(proj_ready, l * 12 + i + 1)
                    apply(vv[:, i // 2, i % 2, :], ps[i][:, :]).then_inc(qkv_act, 1)
                act.wait_ge(ffz_ready, l + 1)
                apply(zabs[:, :, :], zf[:, :, :], ACT.Abs).then_inc(act_step, 1)
                act.wait_ge(act_step, l * 2 + 1)
                apply(zexp[:, :, :], zabs[:, :, :], ACT.Exp, scale=-1.0).then_inc(act_step, 1)
                act.wait_ge(act_step, l * 2 + 2)
                apply(softp[:, :, :], zexp[:, :, :], ACT.Ln, bias=1.0).then_inc(softp_ready, 1)
                for i in range(4):
                    act.wait_ge(proj_ready, l * 12 + 9 + i)
                    apply(qkT[:, i // 2, 2 * (i % 2):2 * (i % 2) + 2, :], ps[i][:, :].rearrange("p (t n) -> p t n", t=2),
                          scale=SCALE if i < 2 else 1.0).then_inc(qkv_act, 1)
                for b in range(4):
                    act.wait_ge(rt_ready, l * 4 + b + 1)
                    apply(qkT[:, 2 + b // 2, 2 * (b % 2):2 * (b % 2) + 2, :], ps[b][:, :].rearrange("p (t n) -> p t n", t=2),
                          scale=SCALE if b < 2 else 1.0).then_inc(qkv_act, 1)
                for h in range(2 * NH + 1):
                    if h < 2 * NH:
                        act.wait_ge(nm_ready, l * 16 + h + 1)
                        for tt in range(TT):
                            m = apply(pS[h % 2][:, part(tt)], sS[h % 2][:, part(tt)], ACT.Exp, bias=nmax[:, h % 2, tt:tt + 1],
                                      accum_out=lsum[:, h % 2, tt:tt + 1])
                        m.then_inc(exp_ready, 1)
                        act.wait_ge(gate_ready, l * 16 + h + 1)
                        apply(gatesT[:, h, :], ps[0][:, 0:S], ACT.Identity, bias=bgate[:, h:h + 1]).then_inc(gates_raw, 1)
                    if h:
                        act.wait_ge(pt_ready, l * 16 + h)
                        apply(pT[(h - 1) % 2], ps[6 + (h - 1) % 2][:, 0:384]).then_inc(pts_ready, 1)
                act.wait_ge(gates_raw, l * 16 + 16)
                both = gatesT.rearrange("p (b j) n -> p b j n", b=2)
                for j in range(0, KT, 2):
                    apply(both[:, :, j:j + 2, :], both[:, :, j:j + 2, :], ACT.Sigmoid).then_inc(gates_ready, 1)

                def norm_sqrt(which, tt):
                    act.wait_ge(ve_ready, l * 4 + 2 * which + tt + 1)
                    apply(sd[:, tt:tt + 1], ve[:, tt:tt + 1], ACT.Sqrt).then_inc(sd_ready, 1)

                norm_sqrt(0, 0)
                modulate(1, 0)
                next_parts(0, half_sums(l, 6))
                norm_sqrt(0, 1)
                next_parts(1, half_sums(l, 7))
                modulate(1, 1)
                act.wait_ge(x_ready, l * 4 + 4)
                apply(xp[:, 0, :, :], xs[:, :, :]).then_inc(xp0_ready, 1)
                act.wait_ge(logits_ready, l * 2 + 2)
                apply(score[:, :, :], ps[4][:, 0:2 * NE].rearrange("p (t n) -> p t n", t=TT), ACT.Sigmoid)\
                    .then_inc(score_ready, 1)
                act.wait_ge(shgu_ready, l + 1)
                apply(shs, ps[5][:, :], ACT.Silu).then_inc(shs_ready, 1)
                act.wait_ge(xr_ready, l + 1)
                apply(xp[:, 1, :, :], xrest).then_inc(xp1_ready, 1)

                act.wait_ge(pass_ready, l + 2)
                apart(act)
                end = act.value_load(passi[0:1, 0:1], min_val=1, max_val=4 * DEPTH)
                def gathered(gathers, b):
                    act.wait_ge(gth0_ready, gathers + 1)
                    for t in range(4):
                        m = apply(xg[b][:, t, :], GB[:, t * P:t * P + P], ACT.Identity, scale=modc[:, 3, t:t + 1], bias=modc[:, 1, t:t + 1])
                    m.then_inc(xg_act, 1)

                gathered(base * ROUNDS * 4 + l, 0)
                with act.Fori(base * ROUNDS, end * ROUNDS) as rnd:
                    for q in range(OCT // 2):
                        n = rnd * 4 + q
                        act.wait_ge(gu_ready, n + 1)
                        apply(sg, HB[:, 0:FF], ACT.Silu).then_inc(sg_ready, 1)
                        gathered(n + l + 1, (q + 1) % 2)
                        act.wait_ge(hts_ready, n + 1)
                        for e in range(2):
                            rows = slice(64 * e, 64 * e + 64)
                            apply(wslot[rows, q:q + 1], HB[rows, FF + P + e:FF + P + e + 1])
                        apply(selT[q % 2], HB16[:, :]).then_inc(sts_ready, 1)
                        act.wait_ge(sts_ready, n + 2)
                        for half in range(2):
                            act.wait_ge(yb_ready, rnd * 8 + 2 * q + half + 1)
                            apply(yp[:, 0, half * 512:half * 512 + 512], YB[half][:, :], scale=wslot[:, q:q + 1])\
                                .then_inc(y0_ready, 1)
                        act.wait_ge(yr_ready, rnd * 8 + 2 * q + 2)
                        apply(yp[:, 1, :], yrest).then_inc(y1_ready, 1)
                norm_sqrt(1, 0)
                norm_sqrt(1, 1)

        @block.vector
        def _(dve):
            V = nc.vector

            V.memset(passf[:, :], 0.0).then_inc(dve_step, 1)
            dve.wait_ge(dve_step, 1)
            V.tensor_copy(passi[:, :], passf[:, :]).then_inc(pass_ready, 1)
            V.memset(morep[:, :], 0.0).then_inc(y2_ready, 1)
            dve.wait_ge(cs_ready, 1)
            V.tensor_copy(csrep[:, :, :], csT[:, :].unsqueeze(2).to_broadcast([P, KT, 32])).then_inc(csrep_ready, 1)
            dve.wait_ge(const_in, 16)
            V.tensor_copy(identb[:, :], ident)
            dve.wait_ge(x_in, 16)
            V.memset(rstd[:, :], 0.0).then_inc(x_ready, 2)

            def next_used(number, biases):
                dve.wait_ge(red_ready, number)
                dve.wait_ge(adab_in, 16 * biases)
                for v in (0, 1):
                    m = V.scalar_tensor_tensor(modc[:, 2 * v, :], ps[7][:, v * KT:v * KT + KT], float(v), adab[:, v, :], ALU.add, ALU.add)
                m.then_inc(red_used, 1)

            next_used(1, 1)
            with dve.Fori(0, DEPTH) as l:
                dve.wait_ge(pass_ready, l + 1)
                apart(dve)
                base = dve.value_load(passi[0:1, 0:1], min_val=0, max_val=4 * (DEPTH - 1))
                steps = [0]

                def step(ins):
                    steps[0] += 1
                    ins.then_inc(dve_step, 1)
                    dve.wait_ge(dve_step, l * DVE_STEPS + steps[0] + 1)

                def vector_step(v, what, i):
                    half = slice(i * 512, i * 512 + 512)
                    if what == "sum":
                        dve.wait_ge(bias_in[v % 2], l * 32 + 16 * (v // 2))
                        dve.wait_ge(ada_ready, half_sums(l, v, i + 1))
                        V.tensor_tensor(parts[v % 2][:, half], ps[1][:, :], parts[v % 2][:, half], ALU.add).then_inc(parts_dve, 1)
                        return
                    dve.wait_ge(red_ready, reductions(l, v, i + 1))
                    if v in GATES:
                        m = V.tensor_scalar(gate1p[:, v // 5, half], ps[1][:, :], 1.0, None, ALU.add)
                    else:
                        m = V.tensor_scalar(modc[:, 2 * (v - 3) + 1, :], ps[1][:, 0:KT], float(v - 3), None, ALU.add)
                    m.then_inc(red_used, 1)

                def modulate(which):
                    dve.wait_ge(red_used, reductions(l, 5 if which else 2))
                    dve.wait_ge(xt_ready, l * 8 + which * 4 + 3)
                    for t in range(4):
                        m = V.tensor_scalar(uT[:, t, P:2 * P], ps[x_bank(which, 1)][:, t * P:t * P + P], modc[:, 2 + which, t:t + 1],
                                            modc[:, which, t:t + 1], ALU.mult, ALU.add)
                    m.then_inc(u_dve, 1)

                modulate(0)
                for a in range(2):
                    for tt in range(TT):
                        dve.wait_ge(proj_ready, l * 12 + (2 + a) * 2 + tt + 1)
                        w = ps[2 * a + tt][:, :].rearrange("p (h c j) -> p h c j", c=2, j=HD // 2)
                        o = rot[:, a, tt, :].rearrange("p (h c j) -> p h c j", c=2, j=HD // 2)
                        cos, sin = (cst[:, C_ROPE + tt * HD + i * 32:C_ROPE + tt * HD + i * 32 + 32].unsqueeze(1)
                                    .to_broadcast([P, NH, HD // 2]) for i in range(2))
                        tmp = [rope_tmp[:, i, :].rearrange("p (h j) -> p h j", h=NH) for i in range(4)]
                        if a or tt:
                            dve.wait_ge(rot_ready, l * 4 + 2 * a + tt)
                        V.tensor_tensor(tmp[0], w[:, :, 0, :], cos, ALU.mult)
                        V.tensor_tensor(tmp[1], w[:, :, 1, :], sin, ALU.mult)
                        V.tensor_tensor(tmp[2], w[:, :, 1, :], cos, ALU.mult)
                        step(V.tensor_tensor(tmp[3], w[:, :, 0, :], sin, ALU.mult))
                        V.tensor_tensor(o[:, :, 0, :], tmp[0], tmp[1], ALU.subtract)
                        V.tensor_tensor(o[:, :, 1, :], tmp[2], tmp[3], ALU.add).then_inc(rot_ready, 1)
                dve.wait_ge(ff_ready, l + 1)
                dve.wait_ge(params_in, l * 80 + 80)
                V.tensor_tensor(zf[:, :, :], ps[4][:, 0:TT * NH].rearrange("p (t h) -> p t h", t=TT),
                                bforget[:, :].unsqueeze(1).to_broadcast([P, TT, NH]), ALU.add).then_inc(ffz_ready, 1)
                dve.wait_ge(ffz_ready, l + 1)
                step(V.tensor_scalar(zneg[:, :, :], zf[:, :, :], -1.0, 0.0, ALU.mult, ALU.max))
                dve.wait_ge(softp_ready, l + 1)
                V.tensor_tensor(nlogf[:, :, :], zneg[:, :, :], softp[:, :, :], ALU.add).then_inc(nlogf_ready, 1)
                dve.wait_ge(cum_ready, l + 1)
                V.tensor_copy(ncum[:, :, :], ps[5][:, 0:TT * NH].rearrange("p (t h) -> p t h", t=TT)).then_inc(cumc_ready, 1)
                V.tensor_copy(ncumT[:, :], ps[5][0:NH, P:3 * P]).then_inc(cumc_ready, 1)
                dve.wait_ge(cumc_ready, l * 2 + 2)

                def biased_max(h):
                    kind, hh = divmod(h, NH)
                    dve.wait_ge(s_ready, l * 16 + h + 1)
                    for tt in range(TT):
                        dst, src = sS[h % 2][:, part(tt)], ps[4 + h % 2][:, part(tt)]
                        if kind == 0:
                            m = V.scalar_tensor_tensor(dst, src, ncum[:, tt, hh:hh + 1], mask(0, tt), ALU.subtract, ALU.add)
                        else:
                            m = V.tensor_tensor(dst, src, mask(1, tt), ALU.add)
                    step(m)
                    for tt in range(TT):
                        m = V.tensor_reduce(nmax[:, h % 2, tt:tt + 1], sS[h % 2][:, part(tt)], AX, ALU.max, negate=True)
                    m.then_inc(nm_ready, 1)

                def normalise(h):
                    dve.wait_ge(exp_ready, l * 16 + h + 1)
                    step(V.reciprocal(rsum[:, h % 2, :], lsum[:, h % 2, :]))
                    for tt in range(TT):
                        m = V.tensor_scalar(pS[h % 2][:, part(tt)], pS[h % 2][:, part(tt)], rsum[:, h % 2, tt:tt + 1], None, ALU.mult)
                    m.then_inc(p_ready, 1)

                for h in range(2 * NH + 2):
                    if h < 2 * NH:
                        biased_max(h)
                    if 1 <= h <= 2 * NH:
                        normalise(h - 1)
                    if h < len(ADA_STEPS):
                        vector_step(*ADA_STEPS[h])
                    if h >= 3 and h % 2:
                        n = (h - 3) // 2
                        dve.wait_ge(pv_ready, l * 8 + n + 1)
                        V.tensor_copy(yT[:, n // BT, n % BT, :], ps[2 + n % 2][:, 0:S]).then_inc(y_ready, 1)
                for j in range(KT):
                    if j % 2 == 0:
                        dve.wait_ge(gates_ready, l * 4 + j // 2 + 1)
                    dve.wait_ge(br_ready, l * 8 + j + 1)
                    a, b = merge_tmp[:, 2 * (j % 2), :], merge_tmp[:, 2 * (j % 2) + 1, :]
                    if j >= 2:
                        dve.wait_ge(merged_ready, l * 8 + j - 1)
                    V.tensor_tensor(a, ps[j % 2][:, 0:S], gatesT[:, j, :], ALU.mult)
                    step(V.tensor_tensor(b, ps[j % 2][:, S:2 * S], gatesT[:, KT + j, :], ALU.mult))
                    V.tensor_tensor(mergedT[:, j, :], a, b, ALU.add).then_inc(merged_ready, 1)

                def norm(which, banks, ready):
                    def statistics(tt):
                        for half in range(2):
                            ready(tt, half)
                            a = slice(half * 512, half * 512 + 512)
                            m = V.tensor_tensor(z[:, tt, a], banks(tt, half)[:, :], gate1p[:, which, a], ALU.mult)
                        step(m)
                        step(V.scalar_tensor_tensor(z[:, tt, :], xs[:, tt, :], ALPHA, z[:, tt, :], ALU.mult, ALU.add))
                        for half in range(2):
                            m = V.bn_stats(bst[:, tt, half, :], z[:, tt, half * 512:half * 512 + 512])
                        step(m)
                        apart(dve)
                        step(V.bn_aggr(mv[:, tt, :], bst[:, tt, :, :].rearrange("p a b -> p (a b)")))
                        V.tensor_scalar(ve[:, tt:tt + 1], mv[:, tt, 1:2], LN_EPS, None, ALU.add).then_inc(ve_ready, 1)

                    def normalised(tt):
                        dve.wait_ge(sd_ready, l * 4 + 2 * which + tt + 1)
                        step(V.reciprocal(rstd[:, tt:tt + 1], sd[:, tt:tt + 1]))
                        dve.wait_ge(ln_in, l * 64 + 32 * (which + 1))
                        step(V.scalar_tensor_tensor(z[:, tt, :], z[:, tt, :], mv[:, tt, 0:1], lnp[:, 0, :], ALU.subtract, ALU.mult))
                        V.scalar_tensor_tensor(xs[:, tt, :], z[:, tt, :], rstd[:, tt:tt + 1], lnp[:, 1, :], ALU.mult, ALU.add)\
                            .then_inc(x_ready, 1)

                    statistics(0)
                    if which == 0:
                        normalised(0)
                        statistics(1)
                    else:
                        statistics(1)
                        normalised(0)
                    normalised(1)

                norm(0, lambda tt, half: ps[4 + 2 * tt + half], lambda tt, half: dve.wait_ge(wo_ready, l * 2 + 1 + tt))
                modulate(1)
                next_used(reductions(l + 1), l + 2)

                dve.wait_ge(score_ready, l + 1)
                step(V.tensor_tensor(choice[:, :, :], score[:, :, :], rbias[:, :].unsqueeze(1).to_broadcast([P, TT, NE]), ALU.add))
                apart(dve)
                for tt in range(TT):
                    for g in range(NG):
                        m = V.max(gmax[:, tt, g, :], choice[:, tt, g * 8:g * 8 + 8])
                step(m)
                step(V.tensor_tensor(gsc[:, :, :], gmax[:, :, :, 0], gmax[:, :, :, 1], ALU.add))
                other = gsc[:, :, :].unsqueeze(2).to_broadcast([P, TT, NG, NG])
                own = gsc[:, :, :].unsqueeze(3).to_broadcast([P, TT, NG, NG])
                V.tensor_tensor(gcmp[:, :, :, :], other, own, ALU.is_gt)
                step(V.tensor_tensor(geq[:, :, :, :], other, own, ALU.is_equal))
                lower = cst[:, C_LT8:C_LT8 + NG * NG].rearrange("p (a b) -> p a b", a=NG).unsqueeze(1).to_broadcast([P, TT, NG, NG])
                step(V.tensor_tensor(geq[:, :, :, :], geq[:, :, :, :], lower, ALU.mult))
                step(V.tensor_tensor(gcmp[:, :, :, :], gcmp[:, :, :, :], geq[:, :, :, :], ALU.add))
                step(V.tensor_reduce(grank[:, :, :], gcmp[:, :, :, :], AX, ALU.add))
                step(V.tensor_scalar(gmask[:, :, :], grank[:, :, :], 4.0, None, ALU.is_lt))
                V.tensor_scalar(gpen[:, :, :], gmask[:, :, :], 1.0, -NEG, ALU.subtract, ALU.mult)
                grouped = choice[:, :, :].rearrange("p t (g e) -> p (t g) e", g=NG)
                flat = gmask[:, :, :].rearrange("p t g -> p (t g)").unsqueeze(2).to_broadcast([P, TT * NG, 8])
                step(V.tensor_tensor(grouped, grouped, flat, ALU.mult))
                pen = gpen[:, :, :].rearrange("p t g -> p (t g)").unsqueeze(2).to_broadcast([P, TT * NG, 8])
                step(V.tensor_tensor(grouped, grouped, pen, ALU.add))
                apart(dve)
                for tt in range(TT):
                    m = V.max(top8[:, tt, :], choice[:, tt, :])
                step(m)
                for tt in range(TT):
                    eighth = top8[:, tt, 7:8]
                    V.tensor_scalar(above[:, tt, :], choice[:, tt, :], eighth, None, ALU.is_gt)
                    m = V.tensor_scalar(ties[:, tt, :], choice[:, tt, :], eighth, None, ALU.is_equal)
                step(m)
                step(V.tensor_reduce(nabove[:, :], above[:, :, :], AX, ALU.add))
                step(V.tensor_scalar(nabove[:, :], nabove[:, :], -1.0, float(TOPK), ALU.mult, ALU.add))
                for tt in range(TT):
                    m = V.tensor_tensor_scan(tiesum[:, tt, :], ties[:, tt, :], cst[:, C_ZERO:C_ZERO + NE], 0.0, ALU.add, ALU.add)
                step(m)
                for tt in range(TT):
                    m = V.scalar_tensor_tensor(ties[:, tt, :], tiesum[:, tt, :], nabove[:, tt:tt + 1], ties[:, tt, :],
                                               ALU.is_le, ALU.mult)
                step(m)
                for tt in range(TT):
                    V.tensor_tensor(emask[:, tt, :], above[:, tt, :], ties[:, tt, :], ALU.add).then_inc(emask_ready, 1)
                dve.wait_ge(shs_ready, l + 1)
                V.tensor_tensor(hsT, shs.rearrange("p (t n) -> p t n", t=2), ps[2][:, :].rearrange("p (t n) -> p t n", t=2),
                                ALU.mult).then_inc(hs_ready, 1)
                dve.wait_ge(emask_ready, l * 2 + 2)
                for tt in range(TT):
                    m = V.scalar_tensor_tensor(wraw[:, tt, :], score[:, tt, :], 1.0, emask[:, tt, :], ALU.mult, ALU.mult,
                                               accum_out=wsum[:, tt:tt + 1])
                step(m)
                step(V.reciprocal(wrec[:, :], wsum[:, :]))
                for tt in range(TT):
                    m = V.tensor_scalar(wtok[:, tt, :], wraw[:, tt, :], wrec[:, tt:tt + 1], ROUTED_SCALE, ALU.mult, ALU.mult)
                step(m)
                step(V.tensor_copy(wp[:, 0, :, :], wtok[:, :, :]))
                step(V.tensor_tensor(wraw[:, :, :], wtok[:, :, :], wp[:, 0, :, :], ALU.subtract))
                step(V.tensor_copy(wp[:, 1, :, :], wraw[:, :, :]))
                step(V.tensor_tensor(wp[:, 2, :, :], wraw[:, :, :], wp[:, 1, :, :], ALU.subtract))
                dve.wait_ge(rank_ready, l + 1)
                step(V.scalar_tensor_tensor(erank[:, :, :], ps[7][:, 0:2 * NE].rearrange("p (t e) -> p t e", t=TT), 1.0,
                                            emask[:, :, :], ALU.add, ALU.mult))
                step(V.tensor_scalar(erank[:, :, :], erank[:, :, :], 1.0, None, ALU.subtract))
                step(V.tensor_reduce(mostf[:, :], ps[7][:, 2 * NE:3 * NE], AX, ALU.max))
                step(V.tensor_tensor(overf[:, :], mostf[:, :].to_broadcast([P, N_THR]), cst[:, C_THR:C_END], ALU.is_gt))
                step(V.tensor_reduce(morep[:, :], overf[:, :], AX, ALU.add))
                step(V.scalar_tensor_tensor(passf[:, :], morep[:, :], 1.0, passf[:, :], ALU.add, ALU.add))
                V.tensor_copy(passi[:, :], passf[:, :]).then_inc(pass_ready, 1)

                def select(n_pass, o, q):
                    V.tensor_tensor(sel[:, :, 2 * q:2 * q + 2, :],
                                    erank[:, :, bass.ds(o * OCT + 2 * q, 2)].unsqueeze(3).to_broadcast([P, TT, 2, CAP]),
                                    cst[:, bass.ds(n_pass * CAP + C_IOTA, CAP)].unsqueeze(1).unsqueeze(1).to_broadcast([P, TT, 2, CAP]),
                                    ALU.is_equal).then_inc(sel_ready, 1)

                def gathered(gathers, b, bank=GB):
                    dve.wait_ge(gth1_ready, gathers + 1)
                    for t in range(4, KT):
                        m = V.tensor_scalar(xg[b][:, t, :], bank[:, t % 4 * P:t % 4 * P + P], modc[:, 3, t:t + 1], modc[:, 1, t:t + 1],
                                            ALU.mult, ALU.add)
                    m.then_inc(xg_dve, 1)

                select(0, 0, 0)
                select(0, 0, 1)
                dve.wait_ge(pass_ready, l + 2)
                apart(dve)
                end = dve.value_load(passi[0:1, 0:1], min_val=1, max_val=4 * DEPTH)
                gathered(base * ROUNDS * 4 + l, 0, HB)
                with dve.Fori(0, end - base) as n_pass:
                    with dve.Fori(0, ROUNDS) as o:
                        rnd = (base + n_pass) * ROUNDS + o
                        for q in range(OCT // 2):
                            n = rnd * 4 + q
                            dve.wait_ge(sg_ready, n + 1)
                            V.tensor_tensor(hb, sg, HB[:, FF:2 * FF], ALU.mult).then_inc(h_ready, 1)
                            dve.wait_ge(ht_ready, n + 1)
                            V.tensor_copy(hT, HB[:, 0:FF]).then_inc(hts_ready, 1)
                            if q < 2:
                                select(n_pass, o, q + 2)
                            else:
                                select(n_pass + (o + 1) // ROUNDS, (o + 1) % ROUNDS, q - 2)
                            gathered(n + l + 1, (q + 1) % 2)
                            for half in range(2):
                                a = slice(half * 512, half * 512 + 512)
                                dve.wait_ge(y0_ready, rnd * 8 + 2 * q + half + 1)
                                V.scalar_tensor_tensor(yrest[:, a], YB[half][:, :], wslot[:, q:q + 1], yp[:, 0, a],
                                                       ALU.mult, ALU.subtract).then_inc(yr_ready, 1)
                            dve.wait_ge(y1_ready, n + 1)
                            V.tensor_tensor(yp[:, 2, :], yrest, yp[:, 1, :], ALU.subtract).then_inc(y2_ready, 1)

                norm(1, lambda tt, half: ACC[tt * 2 + half], lambda tt, half: dve.wait_ge(acc_ready, l * 4 + 2 * tt + half + 1))
                assert steps[0] == DVE_STEPS, steps


INPUTS = ("x", "c", "w_ada", "b_ada", "w_in", "b_forget", "b_gate", "w_br_fox", "w_br_dil", "w_o", "ln_g", "ln_b", "w_router",
          "router_bias", "w_exp_gate", "w_exp_up", "w_exp_down", "w_sh_gate", "w_sh_up", "w_sh_down")


def kernel(**inputs):
    import concourse.bacc as bacc
    from concourse.bass_utils import run_bass_kernel_spmd

    nc = bacc.Bacc("TRN2", target_bir_lowering=False, num_devices=1)
    arrays = {f"in_{name}": np.ascontiguousarray(inputs[name]) for name in INPUTS}
    arrays["in_constants"] = constants()
    args = [nc.dram_tensor(n, a.shape, mybir.dt.from_np(a.dtype), kind="ExternalInput").ap() for n, a in arrays.items()]
    args.append(nc.dram_tensor("out_x", (1, S, D), F32, kind="ExternalOutput").ap())
    decoder(nc, *args)
    return run_bass_kernel_spmd(nc, [arrays], core_ids=[0]).results[0]["out_x"]
```
